# Optimizing a Trainium2 kernel written in Bass

```python
import math
import jax
import jax.numpy as jnp
from jax import lax
import numpy as np
import jax, jax.numpy as jnp

D_MODEL = 1024
BATCH = 1
SEQ = 1024
DEPTH = 1

CHUNK = 64
D_MIX = D_MODEL
EPS = 1e-6

GM_WIDTH = D_MIX // 4
GM_HEADS = 4
GM_HEAD_DIM = GM_WIDTH // GM_HEADS
GM_BLOCK = 128

CV_WIDTH = D_MIX // 4
CV_KERNEL = 31

DN_WIDTH = D_MIX // 2
DN_HEAD_DIM = 128
DN_HEADS = DN_WIDTH // DN_HEAD_DIM
DN_CONV = 4

D_FF = -(-8 * D_MODEL // (3 * 256)) * 256

SPLIT_SIZES = (GM_WIDTH, GM_WIDTH, CV_WIDTH, CV_WIDTH,
               DN_WIDTH, DN_WIDTH, DN_WIDTH, DN_WIDTH, DN_HEADS, DN_HEADS)
D_PROJ = 2 * GM_WIDTH + 2 * CV_WIDTH + 4 * DN_WIDTH + 2 * DN_HEADS


def _split_offsets(sizes):
    out, s = [], 0
    for n in sizes[:-1]:
        s += n
        out.append(s)
    return out

def rms_norm(x, g):
    xf = x.astype(jnp.float32)
    y = xf * lax.rsqrt(jnp.mean(xf * xf, axis=-1, keepdims=True) + EPS)
    return (y * g.astype(jnp.float32)).astype(x.dtype)

def layer_norm(x, g, b):
    xf = x.astype(jnp.float32)
    mu = jnp.mean(xf, axis=-1, keepdims=True)
    var = jnp.mean(jnp.square(xf - mu), axis=-1, keepdims=True)
    y = (xf - mu) * lax.rsqrt(var + EPS)
    return (y * g.astype(jnp.float32) + b.astype(jnp.float32)).astype(x.dtype)

def causal_depthwise_conv(x, w):
    k = w.shape[0]
    return lax.conv_general_dilated(
        x, w[:, None, :].astype(x.dtype), window_strides=(1,), padding=[(k - 1, 0)],
        dimension_numbers=("NWC", "WIO", "NWC"), feature_group_count=x.shape[-1])

def spatial_gating(u, v, ln_g, ln_b, ws, bs):
    b, t, _ = v.shape
    v = layer_norm(v, ln_g, ln_b)
    causal = jnp.tril(jnp.ones((GM_BLOCK, GM_BLOCK), dtype=bool))
    ws = jnp.where(causal, ws, jnp.zeros_like(ws))
    vb = v.reshape(b, t // GM_BLOCK, GM_BLOCK, GM_HEADS, GM_HEAD_DIM)
    s = jnp.einsum("hij,bnjhd->bnihd", ws, vb) + bs.T[:, :, None]
    return u * s.reshape(b, t, GM_WIDTH)

def conformer_conv(a, gate, dw_w, dw_b, ln_g, ln_b):
    y = a * jax.nn.sigmoid(gate)
    y = causal_depthwise_conv(y, dw_w) + dw_b
    y = layer_norm(y, ln_g, ln_b)
    return jax.nn.silu(y)

def l2_normalize(x):
    return x * lax.rsqrt(jnp.sum(x * x, axis=-1, keepdims=True) + EPS)

def chunked_gated_delta_rule(q, k, v, beta, log_alpha):
    b, t, h, dk = q.shape
    dv = v.shape[-1]
    n = t // CHUNK

    def chunks(z):
        return z.reshape(b, n, CHUNK, h, -1).transpose(0, 3, 1, 2, 4)

    def chunks_scalar(z):
        return z.reshape(b, n, CHUNK, h).transpose(0, 3, 1, 2)

    qc, kc, vc = chunks(q), chunks(k), chunks(v)
    bc = chunks_scalar(beta)
    gam = jnp.cumsum(chunks_scalar(log_alpha), axis=-1)

    diff = gam[..., :, None] - gam[..., None, :]
    strict = jnp.tril(jnp.ones((CHUNK, CHUNK), dtype=bool), -1)
    incl = jnp.tril(jnp.ones((CHUNK, CHUNK), dtype=bool))
    decay_strict = jnp.exp(jnp.where(strict, diff, -jnp.inf))
    decay_incl = jnp.exp(jnp.where(incl, diff, -jnp.inf))

    kk = jnp.einsum("bhnid,bhnjd->bhnij", kc, kc)
    lower = jnp.eye(CHUNK, dtype=jnp.float32) + bc[..., :, None] * kk * decay_strict
    rhs = jnp.concatenate([bc[..., None] * vc, (bc * jnp.exp(gam))[..., None] * kc], axis=-1)
    sol = lax.linalg.triangular_solve(lower, rhs, left_side=True, lower=True)
    u_part, w_part = sol[..., :dv], sol[..., dv:]

    qk = jnp.einsum("bhnid,bhnjd->bhnij", qc, kc) * decay_incl
    q_dec = qc * jnp.exp(gam)[..., None]
    k_dec = kc * jnp.exp(gam[..., -1:] - gam)[..., None]
    chunk_decay = jnp.exp(gam[..., -1])

    def step(state, inp):
        u_n, w_n, qk_n, qd_n, kd_n, cd_n = inp
        u = u_n - jnp.einsum("bhck,bhkv->bhcv", w_n, state)
        o = jnp.einsum("bhck,bhkv->bhcv", qd_n, state) + jnp.einsum("bhij,bhjv->bhiv", qk_n, u)
        state = cd_n[..., None, None] * state + jnp.einsum("bhck,bhcv->bhkv", kd_n, u)
        return state, o

    xs = tuple(jnp.moveaxis(z, 2, 0) for z in (u_part, w_part, qk, q_dec, k_dec, chunk_decay))
    s0 = jnp.zeros((b, h, dk, dv), jnp.float32)
    _, o = lax.scan(step, s0, xs)
    return o.transpose(1, 0, 3, 2, 4).reshape(b, t, h, dv)

def gated_deltanet(q, k, v, gate, beta_logit, alpha_logit, conv_w, a_log, dt_bias, norm_g):
    b, t, _ = q.shape
    dtype = q.dtype
    qkv = jax.nn.silu(causal_depthwise_conv(jnp.concatenate([q, k, v], axis=-1), conv_w))
    q, k, v = jnp.split(qkv.astype(jnp.float32), 3, axis=-1)
    q = l2_normalize(q.reshape(b, t, DN_HEADS, DN_HEAD_DIM)) * (DN_HEAD_DIM ** -0.5)
    k = l2_normalize(k.reshape(b, t, DN_HEADS, DN_HEAD_DIM))
    v = v.reshape(b, t, DN_HEADS, DN_HEAD_DIM)
    beta = jax.nn.sigmoid(beta_logit.astype(jnp.float32))
    log_alpha = -jnp.exp(a_log.astype(jnp.float32)) * jax.nn.softplus(
        alpha_logit.astype(jnp.float32) + dt_bias.astype(jnp.float32))
    o = chunked_gated_delta_rule(q, k, v, beta, log_alpha)
    g = gate.astype(jnp.float32).reshape(b, t, DN_HEADS, DN_HEAD_DIM)
    o = rms_norm(o, norm_g) * jax.nn.silu(g)
    return o.reshape(b, t, DN_WIDTH).astype(dtype)

def first_inputs(seed: int = 0) -> dict:
    key = jax.random.key(seed)
    ks = jax.random.split(key, 22)
    f32 = jnp.float32
    L = DEPTH

    def normal(k, shape, scale):
        return scale * jax.random.normal(k, shape, f32)

    def gain(k, shape):
        return 1.0 + 0.05 * jax.random.normal(k, shape, f32)

    dt = jnp.exp(jax.random.uniform(ks[13], (L, DN_HEADS), f32, math.log(1e-3), math.log(1e-1)))
    return {
        "x": normal(ks[0], (BATCH, SEQ, D_MODEL), 1.0),
        "mix_norm_g": gain(ks[1], (L, D_MODEL)),
        "w_in": normal(ks[2], (L, D_MODEL, D_PROJ), D_MODEL ** -0.5),
        "gm_ln_g": gain(ks[3], (L, GM_WIDTH)),
        "gm_ln_b": normal(ks[4], (L, GM_WIDTH), 0.02),
        "gm_ws": normal(ks[5], (L, GM_HEADS, GM_BLOCK, GM_BLOCK), GM_BLOCK ** -0.5),
        "gm_bs": 1.0 + normal(ks[6], (L, GM_HEADS, GM_BLOCK), 0.02),
        "cv_dw_w": normal(ks[7], (L, CV_KERNEL, CV_WIDTH), CV_KERNEL ** -0.5),
        "cv_dw_b": normal(ks[8], (L, CV_WIDTH), 0.02),
        "cv_ln_g": gain(ks[9], (L, CV_WIDTH)),
        "cv_ln_b": normal(ks[10], (L, CV_WIDTH), 0.02),
        "dn_conv_w": normal(ks[11], (L, DN_CONV, 3 * DN_WIDTH), DN_CONV ** -0.5),
        "dn_a_log": jnp.log(jax.random.uniform(ks[12], (L, DN_HEADS), f32, 1.0, 16.0)),
        "dn_dt_bias": dt + jnp.log(-jnp.expm1(-dt)),
        "dn_norm_g": gain(ks[14], (L, DN_HEAD_DIM)),
        "w_out": normal(ks[15], (L, D_MIX, D_MODEL), D_MIX ** -0.5),
        "ffn_norm_g": gain(ks[16], (L, D_MODEL)),
        "w_gate": normal(ks[17], (L, D_MODEL, D_FF), D_MODEL ** -0.5),
        "w_up": normal(ks[18], (L, D_MODEL, D_FF), D_MODEL ** -0.5),
        "w_down": normal(ks[19], (L, D_FF, D_MODEL), D_FF ** -0.5),
        "final_norm_g": gain(ks[20], (D_MODEL,)),
    }

def first_block(x, mix_norm_g, w_in, gm_ln_g, gm_ln_b, gm_ws, gm_bs, cv_dw_w, cv_dw_b,
              cv_ln_g, cv_ln_b, dn_conv_w, dn_a_log, dn_dt_bias, dn_norm_g, w_out,
              ffn_norm_g, w_gate, w_up, w_down, final_norm_g):
    offsets = _split_offsets(SPLIT_SIZES)
    for l in range(DEPTH):
        h = rms_norm(x, mix_norm_g[l])
        p = jnp.einsum("btd,de->bte", h, w_in[l])
        (gm_u, gm_v, cv_a, cv_g, dn_q, dn_k, dn_v, dn_g,
         dn_beta, dn_alpha) = jnp.split(p, offsets, axis=-1)
        y_a = spatial_gating(jax.nn.gelu(gm_u, approximate=False), jax.nn.gelu(gm_v, approximate=False),
                             gm_ln_g[l], gm_ln_b[l], gm_ws[l], gm_bs[l])
        y_b = conformer_conv(cv_a, cv_g, cv_dw_w[l], cv_dw_b[l], cv_ln_g[l], cv_ln_b[l])
        y_c = gated_deltanet(dn_q, dn_k, dn_v, dn_g, dn_beta, dn_alpha, dn_conv_w[l],
                             dn_a_log[l], dn_dt_bias[l], dn_norm_g[l])
        mix = jnp.concatenate([y_a, y_b, y_c], axis=-1)
        x = x + jnp.einsum("bte,ed->btd", mix, w_out[l])
        h = rms_norm(x, ffn_norm_g[l])
        ff = jax.nn.silu(jnp.einsum("btd,df->btf", h, w_gate[l])) * jnp.einsum("btd,df->btf", h, w_up[l])
        x = x + jnp.einsum("btf,fd->btd", ff, w_down[l])
    return rms_norm(x, final_norm_g)


_first_inputs = first_inputs


def first_inputs(seed=0):
    import zlib

    import numpy as np

    out = dict(_first_inputs(seed))
    spreads = {}
    factors = {'gm_ln_g': 19.226,
     'gm_ln_b': 48.472,
     'gm_bs': 30.925,
     'cv_dw_b': 5.189,
     'cv_ln_g': 10.363,
     'cv_ln_b': 26.688,
     'dn_norm_g': 9.59,
     'ffn_norm_g': 4.713}
    for name, (base, spread) in spreads.items():
        noise = np.random.default_rng([zlib.crc32(name.encode()), seed]).standard_normal(out[name].shape)
        drawn = base * np.exp(spread * noise) if base else spread * noise
        out[name] = jnp.asarray(drawn.astype(out[name].dtype))
    for name, factor in factors.items():
        out[name] = (out[name] * factor).astype(out[name].dtype)
    return out


_narrow_inputs = first_inputs


def first_inputs(seed=0):

    out = dict(_narrow_inputs(seed))
    wider = {'gm_ln_g': 3.1,
     'gm_ln_b': 3.11,
     'gm_bs': 3.11,
     'cv_ln_g': 3.2,
     'cv_ln_b': 3.07,
     'dn_norm_g': 3.09}
    for name, times in wider.items():
        mean = out[name].mean()
        out[name] = (mean + times * (out[name] - mean)).astype(out[name].dtype)
    return out


N_META = 16
HEAD_DIM = 64
N_Q_HEADS = D_MODEL // HEAD_DIM
N_KV_HEADS = N_Q_HEADS // 4
Q_PER_KV = N_Q_HEADS // N_KV_HEADS
WINDOW = 128
BLOCK = 128
ATTN_WIDTH = N_Q_HEADS * HEAD_DIM
KV_WIDTH = N_KV_HEADS * HEAD_DIM
SSM_GROUP = 16
SSM_WIDTH = D_MODEL // 2
SSM_GROUPS = SSM_WIDTH // SSM_GROUP
SSM_STATE = 64
D_FF_2 = ((8 * D_MODEL // 3 + 255) // 256) * 256
NORM_EPS = 1e-6
NEG_INF = -1e30
SPLITS = [ATTN_WIDTH, ATTN_WIDTH + KV_WIDTH, ATTN_WIDTH + 2 * KV_WIDTH,
          ATTN_WIDTH + 2 * KV_WIDTH + SSM_WIDTH,
          ATTN_WIDTH + 2 * KV_WIDTH + SSM_WIDTH + D_MODEL]
IN_WIDTH = SPLITS[-1] + D_MODEL


def rmsnorm(x, g):
    xf = x.astype(jnp.float32)
    y = xf * lax.rsqrt(jnp.mean(xf * xf, axis=-1, keepdims=True) + NORM_EPS)
    return (y * g.astype(jnp.float32)).astype(x.dtype)

def swiglu(h, w1, w3, w2):
    return (jax.nn.silu(h @ w1) * (h @ w3)) @ w2

def sink_softmax(scores, mask, sink):
    scores = jnp.where(mask, scores, NEG_INF)
    sink_b = jnp.broadcast_to(sink[:, :, None, None], scores.shape[:-1] + (1,))
    p = jax.nn.softmax(jnp.concatenate([scores, sink_b], axis=-1), axis=-1)
    return p[..., :-1]

def sliding_window_attention(q, k, v, sinks):
    b, l = q.shape[0], q.shape[1]
    s = l - N_META
    nb = s // BLOCK
    q = (q * (HEAD_DIM ** -0.5)).reshape(b, l, N_KV_HEADS, Q_PER_KV, HEAD_DIM)
    k = k.reshape(b, l, N_KV_HEADS, HEAD_DIM)
    v = v.reshape(b, l, N_KV_HEADS, HEAD_DIM)
    sink = sinks.astype(jnp.float32).reshape(N_KV_HEADS, Q_PER_KV)
    q_meta, q_real = q[:, :N_META], q[:, N_META:]
    k_meta, k_real = k[:, :N_META], k[:, N_META:]
    v_meta, v_real = v[:, :N_META], v[:, N_META:]

    sc_m = jnp.einsum('bqkgd,bskd->bkgqs', q_meta, k_meta).astype(jnp.float32)
    mask_m = jnp.tril(jnp.ones((N_META, N_META), dtype=bool))
    p_m = sink_softmax(sc_m, mask_m, sink)
    out_m = jnp.einsum('bkgqs,bskd->bqkgd', p_m.astype(v.dtype), v_meta)

    qb = q_real.reshape(b, nb, BLOCK, N_KV_HEADS, Q_PER_KV, HEAD_DIM)
    kb = k_real.reshape(b, nb, BLOCK, N_KV_HEADS, HEAD_DIM)
    vb = v_real.reshape(b, nb, BLOCK, N_KV_HEADS, HEAD_DIM)
    k_band = jnp.concatenate([jnp.concatenate([jnp.zeros_like(kb[:, :1]), kb[:, :-1]], axis=1), kb], axis=2)
    v_band = jnp.concatenate([jnp.concatenate([jnp.zeros_like(vb[:, :1]), vb[:, :-1]], axis=1), vb], axis=2)
    qi = jnp.arange(BLOCK)[:, None]
    kj = jnp.arange(2 * BLOCK)[None, :]
    rel = BLOCK + qi - kj
    band_ok = (rel >= 0) & (rel < WINDOW)
    meta_ok = jnp.ones((BLOCK, N_META), dtype=bool)

    def block_fn(args):
        n, qn, kn, vn = args
        keys = jnp.concatenate([k_meta, kn], axis=1)
        vals = jnp.concatenate([v_meta, vn], axis=1)
        sc = jnp.einsum('bqkgd,bskd->bkgqs', qn, keys).astype(jnp.float32)
        valid = band_ok & ((n - 1) * BLOCK + kj >= 0)
        mask = jnp.concatenate([meta_ok, valid], axis=1)
        p = sink_softmax(sc, mask, sink)
        return jnp.einsum('bkgqs,bskd->bqkgd', p.astype(vals.dtype), vals)

    out_r = lax.map(block_fn, (jnp.arange(nb, dtype=jnp.int32), jnp.moveaxis(qb, 1, 0),
                               jnp.moveaxis(k_band, 1, 0), jnp.moveaxis(v_band, 1, 0)))
    out_r = jnp.moveaxis(out_r, 0, 1).reshape(b, s, ATTN_WIDTH)
    return jnp.concatenate([out_m.reshape(b, N_META, ATTN_WIDTH), out_r], axis=1)

def s5_ssm(u, a_re, a_im, log_step, b_re, b_im, c_re, c_im, d_skip):
    b, l, _ = u.shape
    uf = u.astype(jnp.float32).reshape(b, l, SSM_GROUPS, SSM_GROUP)
    ar, ai = a_re.astype(jnp.float32), a_im.astype(jnp.float32)
    step = jnp.exp(log_step.astype(jnp.float32))[:, None]
    mag = jnp.exp(ar * step)
    ang = ai * step
    lam_re, lam_im = mag * jnp.cos(ang), mag * jnp.sin(ang)
    den = ar * ar + ai * ai
    nr, ni = lam_re - 1.0, lam_im
    coef_re = (nr * ar + ni * ai) / den
    coef_im = (ni * ar - nr * ai) / den
    br, bi = b_re.astype(jnp.float32), b_im.astype(jnp.float32)
    bb_re = coef_re[..., None] * br - coef_im[..., None] * bi
    bb_im = coef_re[..., None] * bi + coef_im[..., None] * br
    bu_re = jnp.einsum('blgc,gnc->blgn', uf, bb_re)
    bu_im = jnp.einsum('blgc,gnc->blgn', uf, bb_im)
    la_re = jnp.broadcast_to(lam_re[None, None], (1, l, SSM_GROUPS, SSM_STATE))
    la_im = jnp.broadcast_to(lam_im[None, None], (1, l, SSM_GROUPS, SSM_STATE))

    def combine(e1, e2):
        a1r, a1i, b1r, b1i = e1
        a2r, a2i, b2r, b2i = e2
        return (a2r * a1r - a2i * a1i, a2r * a1i + a2i * a1r,
                a2r * b1r - a2i * b1i + b2r, a2r * b1i + a2i * b1r + b2i)

    _, _, x_re, x_im = lax.associative_scan(combine, (la_re, la_im, bu_re, bu_im), axis=1)
    y = (jnp.einsum('blgn,gcn->blgc', x_re, c_re.astype(jnp.float32))
         - jnp.einsum('blgn,gcn->blgc', x_im, c_im.astype(jnp.float32)))
    y = y + d_skip.astype(jnp.float32).reshape(SSM_GROUPS, SSM_GROUP) * uf
    return y.reshape(b, l, SSM_WIDTH).astype(u.dtype)

def second_inputs(seed: int = 0) -> dict:
    key = jax.random.key(seed)
    ks = jax.random.split(key, 32)
    nrm = lambda k, shape, scale: jax.random.normal(k, shape, jnp.float32) * scale
    n_idx = jnp.arange(SSM_STATE, dtype=jnp.float32)
    return {
        "x": nrm(ks[0], (BATCH, SEQ, D_MODEL), 1.0),
        "meta_tokens": nrm(ks[1], (N_META, D_MODEL), 1.0),
        "ffn1_norm": 1.0 + nrm(ks[2], (DEPTH, D_MODEL), 0.02),
        "ffn1_w1": nrm(ks[3], (DEPTH, D_MODEL, D_FF_2), D_MODEL ** -0.5),
        "ffn1_w3": nrm(ks[4], (DEPTH, D_MODEL, D_FF_2), D_MODEL ** -0.5),
        "ffn1_w2": nrm(ks[5], (DEPTH, D_FF_2, D_MODEL), D_FF_2 ** -0.5),
        "mix_norm": 1.0 + nrm(ks[6], (DEPTH, D_MODEL), 0.02),
        "w_in": nrm(ks[7], (DEPTH, D_MODEL, IN_WIDTH), D_MODEL ** -0.5),
        "attn_sinks": nrm(ks[8], (DEPTH, N_Q_HEADS), 0.5),
        "ssm_a_re": -0.5 + nrm(ks[9], (DEPTH, SSM_GROUPS, SSM_STATE), 0.01),
        "ssm_a_im": math.pi * n_idx[None, None, :] + nrm(ks[10], (DEPTH, SSM_GROUPS, SSM_STATE), 0.01),
        "ssm_log_step": jax.random.uniform(ks[11], (DEPTH, SSM_GROUPS), jnp.float32,
                                           math.log(0.001), math.log(0.1)),
        "ssm_b_re": nrm(ks[12], (DEPTH, SSM_GROUPS, SSM_STATE, SSM_GROUP), (2 * SSM_GROUP) ** -0.5),
        "ssm_b_im": nrm(ks[13], (DEPTH, SSM_GROUPS, SSM_STATE, SSM_GROUP), (2 * SSM_GROUP) ** -0.5),
        "ssm_c_re": nrm(ks[14], (DEPTH, SSM_GROUPS, SSM_GROUP, SSM_STATE), SSM_STATE ** -0.5),
        "ssm_c_im": nrm(ks[15], (DEPTH, SSM_GROUPS, SSM_GROUP, SSM_STATE), SSM_STATE ** -0.5),
        "ssm_d": nrm(ks[16], (DEPTH, SSM_WIDTH), 1.0),
        "ssm_glu_a": nrm(ks[17], (DEPTH, SSM_WIDTH, D_MODEL), SSM_WIDTH ** -0.5),
        "ssm_glu_b": nrm(ks[18], (DEPTH, SSM_WIDTH, D_MODEL), SSM_WIDTH ** -0.5),
        "w_out": nrm(ks[19], (DEPTH, D_MODEL, D_MODEL), D_MODEL ** -0.5),
        "ffn2_norm": 1.0 + nrm(ks[20], (DEPTH, D_MODEL), 0.02),
        "ffn2_w1": nrm(ks[21], (DEPTH, D_MODEL, D_FF_2), D_MODEL ** -0.5),
        "ffn2_w3": nrm(ks[22], (DEPTH, D_MODEL, D_FF_2), D_MODEL ** -0.5),
        "ffn2_w2": nrm(ks[23], (DEPTH, D_FF_2, D_MODEL), D_FF_2 ** -0.5),
        "final_norm": 1.0 + nrm(ks[24], (D_MODEL,), 0.02),
    }

def second_block(x, meta_tokens, ffn1_norm, ffn1_w1, ffn1_w3, ffn1_w2, mix_norm, w_in,
              attn_sinks, ssm_a_re, ssm_a_im, ssm_log_step, ssm_b_re, ssm_b_im,
              ssm_c_re, ssm_c_im, ssm_d, ssm_glu_a, ssm_glu_b, w_out,
              ffn2_norm, ffn2_w1, ffn2_w3, ffn2_w2, final_norm):
    b = x.shape[0]
    meta = jnp.broadcast_to(meta_tokens[None].astype(x.dtype), (b, N_META, D_MODEL))
    h = jnp.concatenate([meta, x], axis=1)
    for i in range(DEPTH):
        h = h + 0.5 * swiglu(rmsnorm(h, ffn1_norm[i]), ffn1_w1[i], ffn1_w3[i], ffn1_w2[i])
        hn = rmsnorm(h, mix_norm[i])
        q, k, v, u, g_attn, g_ssm = jnp.split(hn @ w_in[i], SPLITS, axis=-1)
        attn = sliding_window_attention(q, k, v, attn_sinks[i])
        y = s5_ssm(u, ssm_a_re[i], ssm_a_im[i], ssm_log_step[i], ssm_b_re[i], ssm_b_im[i],
                   ssm_c_re[i], ssm_c_im[i], ssm_d[i])
        y = jax.nn.gelu(y)
        ssm = (y @ ssm_glu_a[i]) * jax.nn.sigmoid(y @ ssm_glu_b[i])
        merged = jax.nn.sigmoid(g_attn) * attn + jax.nn.sigmoid(g_ssm) * ssm
        h = h + merged @ w_out[i]
        h = h + 0.5 * swiglu(rmsnorm(h, ffn2_norm[i]), ffn2_w1[i], ffn2_w3[i], ffn2_w2[i])
    return rmsnorm(h, final_norm)[:, N_META:]


def setup_inputs(seed=0):
    out = dict(first_inputs(seed))
    for name, value in second_inputs(seed + 1).items():
        if name != "x":
            out[name + "_2"] = value
    return out


def reference(
    x, mix_norm_g, w_in, gm_ln_g, gm_ln_b, gm_ws, gm_bs, cv_dw_w, cv_dw_b, cv_ln_g, cv_ln_b,
    dn_conv_w, dn_a_log, dn_dt_bias, dn_norm_g, w_out, ffn_norm_g, w_gate, w_up, w_down,
    final_norm_g, meta_tokens_2, ffn1_norm_2, ffn1_w1_2, ffn1_w3_2, ffn1_w2_2, mix_norm_2,
    w_in_2, attn_sinks_2, ssm_a_re_2, ssm_a_im_2, ssm_log_step_2, ssm_b_re_2, ssm_b_im_2,
    ssm_c_re_2, ssm_c_im_2, ssm_d_2, ssm_glu_a_2, ssm_glu_b_2, w_out_2, ffn2_norm_2, ffn2_w1_2,
    ffn2_w3_2, ffn2_w2_2, final_norm_2,
):
    x = first_block(
        x, mix_norm_g, w_in, gm_ln_g, gm_ln_b, gm_ws, gm_bs, cv_dw_w, cv_dw_b, cv_ln_g, cv_ln_b,
        dn_conv_w, dn_a_log, dn_dt_bias, dn_norm_g, w_out, ffn_norm_g, w_gate, w_up, w_down,
        final_norm_g,
    )
    return second_block(
        x, meta_tokens_2, ffn1_norm_2, ffn1_w1_2, ffn1_w3_2, ffn1_w2_2, mix_norm_2, w_in_2,
        attn_sinks_2, ssm_a_re_2, ssm_a_im_2, ssm_log_step_2, ssm_b_re_2, ssm_b_im_2,
        ssm_c_re_2, ssm_c_im_2, ssm_d_2, ssm_glu_a_2, ssm_glu_b_2, w_out_2, ffn2_norm_2,
        ffn2_w1_2, ffn2_w3_2, ffn2_w2_2, final_norm_2,
    )


_drawn_inputs = setup_inputs


def setup_inputs(seed=0):
    import zlib

    import numpy as np

    out = dict(_drawn_inputs(seed))
    spreads = {}
    factors = {'ffn1_norm_2': 6.695,
     'mix_norm_2': 8.0,
     'attn_sinks_2': 8.0,
     'ssm_a_re_2': 64.0,
     'ssm_a_im_2': 16.471,
     'ssm_log_step_2': 20.914,
     'ssm_b_re_2': 32.818,
     'ssm_b_im_2': 34.208,
     'ssm_c_re_2': 31.152,
     'ssm_c_im_2': 31.376,
     'ffn2_norm_2': 7.339,
     'final_norm_2': 8.016}
    for name, (base, spread) in spreads.items():
        noise = np.random.default_rng([zlib.crc32(name.encode()), seed]).standard_normal(out[name].shape)
        drawn = base * np.exp(spread * noise) if base else spread * noise
        out[name] = jnp.asarray(drawn.astype(out[name].dtype))
    for name, factor in factors.items():
        out[name] = (out[name] * factor).astype(out[name].dtype)
    return out
```

```python
import math
from contextlib import ExitStack, contextmanager

import numpy as np

import concourse.bass as bass
from concourse import mybir

F32 = mybir.dt.float32
F32R = mybir.dt.float32r
I32 = mybir.dt.int32
ALU = mybir.AluOpType
ACT = mybir.ActivationFunctionType
AX_X = mybir.AxisListType.X

P = 128
D = 1024
KD = D // P
SEQ = 1024
NBLK = SEQ // P
META = 16
L = META + SEQ
EPS = 1e-6
NEG = -1e30

HEADS = 4
TAPS = 31
DTAPS = 4
D_FF = 2816
FT = D_FF // P
FQ = [6, 6, 5, 5]
FMAX = max(FQ)
assert sum(FQ) == FT

PAIRS = 16
SC = 8
NCH = L // SC
GATES_A = 3

CH1 = [(META, 512), (META + 512, 512)]
CH2 = [(0, 348), (348, 346), (694, 346)]

CONST = {}


def _constants():
    j = np.arange(P)[:, None]
    i = np.arange(P)[None, :]
    parts = [("ident", np.eye(P)), ("ones", np.ones((P, P))), ("upper", j <= i), ("lower", j > i),
             ("negmask", np.where(i >= j, 0.0, NEG)), ("strict", i > j)]
    b = 1
    while b < P:
        same = (i // (2 * b)) == (j // (2 * b))
        parts.append((f"off{b}", same & (i % (2 * b) >= b) & (j % (2 * b) < b)))
        b *= 2
    prev = np.where(i > j, 0.0, NEG)
    cur = np.where(i <= j, 0.0, NEG)
    meta = np.zeros((P, META))
    parts.append(("band", np.concatenate([meta, prev, cur], 1)))
    parts.append(("band0", np.concatenate([meta, cur], 1)))
    parts.append(("eps", np.full((P, 1), EPS)))
    parts.append(("mean", np.full((P, P), 1.0 / D)))
    parts.append(("mean256", np.full((P, P), 1.0 / 256)))
    parts.append(("mean128", np.full((P, P), 1.0 / 128)))
    at = 0
    for name, a in parts:
        CONST[name] = (at, a.shape[1])
        at += a.shape[1]
    return np.concatenate([np.asarray(a, np.float32) for _, a in parts], 1).astype(np.float32)


CONSTANTS = _constants()


class Chain:

    def __init__(self, eng, sem):
        self.eng, self.sem, self.base, self.k, self.i, self.per = eng, sem, 0, 0, None, 0

    def mark(self, ins):
        self.k += 1
        ins.then_inc(self.sem, 1)

    def count(self):
        n = self.base + self.k
        return n if self.i is None else self.i * self.per + n

    def wait(self, back=0):
        self.eng.wait_ge(self.sem, self.count() - back)

    def link(self, ins):
        self.mark(ins)
        self.wait()

    @contextmanager
    def loop(self, count, per):
        self.base, self.k = self.base + self.k, 0
        with self.eng.Fori(0, count) as i:
            self.i, self.per = i, per
            yield i
        assert self.k == per, (self.k, per)
        self.base, self.k, self.i = self.base + count * per, 0, None


def slabs_of(w, parts=None):
    k, n = w.shape
    return w.reshape(k // P, P, n // P, P).transpose(2, 1, 0, 3).reshape(n // P, P, k)


PARTS = ("mix1", "ffn0", "ffn1", "mix2", "ffn2")


class Segment:

    def __init__(self, n0, q0, pairs, kt, chunks, src):
        self.n0, self.q0, self.pairs, self.kt, self.chunks, self.src = n0, q0, pairs, kt, chunks, src


def slab_plan(t, parts):
    segs, n, q = {}, 0, 0

    def add(name, pairs, kt, chunks, src):
        nonlocal n, q
        segs[name] = Segment(n, q, pairs, kt, chunks, src)
        n += 2 * pairs
        q += pairs * len(chunks)

    def run(w, first):
        return lambda i, j: w[bass.ds(i * 2 + (first + j), 1)]

    def pair(wa, wb, first=0):
        w = (wa, wb)
        return lambda i, j: w[j][bass.ds(i + first, 1)]

    def ffn(name, wg, wu, wd, chunks):
        f = 0
        for part, nf in enumerate(FQ):
            add(f"{name}_up{part}", nf, KD, chunks, pair(wg, wu, f))
            add(f"{name}_down{part}", KD // 2, nf, chunks, run(wd[part], 0))
            f += nf

    if "mix1" in parts:
        add("gm", 2, KD, CH1, run(t["w_in"], 0))
        add("cv", 2, KD, CH1, run(t["w_in"], 4))
        add("dn_kv", 4, KD, CH1, run(t["w_in"], 12))
        add("dn_q", 2, KD, CH1, run(t["w_in"], 8))
        add("dn_g", 2, KD, CH1, run(t["w_in"], 20))
        add("out1", 4, KD, CH1, run(t["w_out"], 0))
    if "ffn0" in parts:
        ffn("ffn0", t["w_gate"], t["w_up"], t["w_down"], CH1)
    if "ffn1" in parts:
        ffn("ffn1", t["ffn1_w1_2"], t["ffn1_w3_2"], t["ffn1_w2_2"], CH2)
    if "mix2" in parts:
        add("at_u", 2, KD, CH2, run(t["w_in_2"], 12))
        add("at_q", 4, KD, CH2, run(t["w_in_2"], 0))
        add("at_g", GATES_A, KD, CH2, run(t["w_in_2"], 16))
        add("at_kv", 2, KD, CH2, run(t["w_in_2"], 8))
        add("at_h", 8 - GATES_A, KD, CH2, run(t["w_in_2"], 16 + 2 * GATES_A))
        add("glu", 8, KD // 2, CH2, pair(t["ssm_glu_a_2"], t["ssm_glu_b_2"]))
        add("out2", 4, KD, CH2, run(t["w_out_2"], 0))
    if "ffn2" in parts:
        ffn("ffn2", t["ffn2_w1_2"], t["ffn2_w3_2"], t["ffn2_w2_2"], CH2)
    return segs


PARAM = {}


def pack_params(a):
    def cols(v):
        return np.ascontiguousarray(v.reshape(-1, P).T)

    def rep(v):
        return np.broadcast_to(v.reshape(1, -1), (P, v.size))

    def states(v):
        return v.reshape(PAIRS, P).T

    def blocks(v):
        out = np.zeros((2, 64, PAIRS, 2, 16), v.dtype)
        w = v.reshape(PAIRS, 2, 64, 16)
        for g in range(2):
            out[g, :, :, g, :] = w[:, g].transpose(1, 0, 2)
        return out.reshape(P, -1)

    parts = [
        ("mix_g", cols(a["mix_norm_g"][0])), ("ffn_g", cols(a["ffn_norm_g"][0])), ("final_g", cols(a["final_norm_g"])),
        ("ffn1_g", cols(a["ffn1_norm_2"][0])), ("mix2_g", cols(a["mix_norm_2"][0])),
        ("ffn2_g", cols(a["ffn2_norm_2"][0])), ("final2_g", cols(a["final_norm_2"])),
        ("cv_b", cols(a["cv_dw_b"][0])), ("cvln_g", cols(a["cv_ln_g"][0])), ("cvln_b", cols(a["cv_ln_b"][0])),
        ("cv_w", a["cv_dw_w"][0].T.reshape(2, P, TAPS).transpose(1, 0, 2).reshape(P, -1)),
        ("dn_w", a["dn_conv_w"][0].T.reshape(12, P, DTAPS).transpose(1, 0, 2).reshape(P, -1)),
        ("dn_norm", cols(a["dn_norm_g"][0])),
        ("a_log", rep(a["dn_a_log"][0])), ("dt_bias", rep(a["dn_dt_bias"][0])),
        ("sinks", rep(a["attn_sinks_2"][0])),
        ("a_re", states(a["ssm_a_re_2"][0])), ("a_im", states(a["ssm_a_im_2"][0])),
        ("log_step", states(np.repeat(a["ssm_log_step_2"][0], 64))), ("ssm_d", cols(a["ssm_d_2"][0])),
        ("meta", a["meta_tokens_2"].T.reshape(KD, P, META).transpose(1, 0, 2).reshape(P, -1)),
        ("w_ba", a["w_in"][0][:, 3072:].reshape(KD, P, 8).transpose(1, 0, 2).reshape(P, -1)),
    ]
    at = 0
    for name, v in parts:
        PARAM[name] = (at, v.shape[1])
        at += v.shape[1]
    ssm = [blocks(a["ssm_b_re_2"][0]), blocks(a["ssm_b_im_2"][0]),
           blocks(a["ssm_c_re_2"][0].transpose(0, 2, 1)), blocks(a["ssm_c_im_2"][0].transpose(0, 2, 1))]
    gm = [rep(a["gm_ln_g"][0]), rep(a["gm_ln_b"][0]), rep(a["gm_bs"][0]),
          a["gm_ws"][0].transpose(2, 0, 1).reshape(P, -1)]
    return np.concatenate([v for _, v in parts], 1), np.concatenate(ssm, 1), np.concatenate(gm, 1)


def build_program(nc, t, parts=PARTS, dumps=None):
    with ExitStack() as ctx:
        base = 16512

        def place(name, offset, shape, dtype=F32):
            return nc.alloc_sbuf_tensor_at(name, shape, dtype, offset=base + offset)

        sems = {}

        def sem(name):
            if name not in sems:
                sems[name] = ctx.enter_context(nc.semaphore(name))
            return sems[name]

        def two(name):
            return [sem(name + "0"), sem(name + "1")]

        col = L * 4
        h_hi = place("h_hi", 0, [P, KD, L], F32R)
        h_lo = place("h_lo", 8 * col, [P, KD, L], F32R)
        w_raw = place("w_raw", 66560, [P, 2, KD * P])
        w_hi = place("w_hi", 74752, [P, 2, KD * P], F32R)
        w_lo = place("w_lo", 82944, [P, 2, KD * P], F32R)
        n_const, n_param = CONSTANTS.shape[1], t["params"].shape[1]
        consts = place("consts", 91136, [P, n_const])
        at = 91136 + 4 * n_const
        at += -at % 32
        params = place("params", at, [P, n_param])
        at += 4 * n_param
        at += -at % 32
        ba_hi = place("ba_hi", at, [P, KD, 8], F32R)
        ba_lo = place("ba_lo", at + 256, [P, KD, 8], F32R)
        small = place("small", at + 512, [P, 32, 16])
        W = 91136 + 14336
        assert at + 512 + 32 * 64 <= W

        def const(name):
            a, n = CONST[name]
            return consts[:, a:a + n]

        def param(name):
            a, n = PARAM[name]
            return params[:, a:a + n]

        x = place("x", W, [P, KD, L])
        ff_hi = place("ff_hi", W + 8 * col, [P, FMAX, L], F32R)
        ff_lo = place("ff_lo", W + 14 * col, [P, FMAX, L], F32R)
        tmp = place("tmp", W + 20 * col, [P, 4, 512])
        ssq = place("ssq", W + 20 * col + 8192, [P, L])
        rs = place("rs", W + 21 * col + 8192, [P, L])
        sq = place("sq", W + 22 * col + 8192, [P, 512])
        sqx = place("sqx", W + 8 * col, [P, 2, L])
        fin = place("fin", W + 8 * col, [P, KD, L])

        kT = place("kT", W, [P, HEADS, SEQ])
        qT = place("qT", W + 16384, [P, HEADS, SEQ])
        vtok = place("vtok", W + 32768, [P, NBLK, HEADS, P])
        gate = place("gate", W + 49152, [P, HEADS, SEQ])
        cv_a = place("cv_a", W + 16128, [P, 2, SEQ])
        cv_g = place("cv_g", W + 55296, [P, 2, SEQ])
        cv_y = place("cv_y", W + 32768 - 8448, [P, 2, TAPS - 1 + SEQ])
        gm_u = place("gm_u", W + 65536, [P, 2, SEQ])
        gm_v = place("gm_v", W + 73728, [P, 2, SEQ])
        gm_t = place("gm_t", W + 81920, [P, NBLK, 256])
        gm_par = place("gm_par", W + 49152, [P, 768 + 256 + 512])
        cv_acc = place("cv_acc", W + 81920, [P, 2, SEQ])
        pre = place("pre", W + 90112, [P, 2, DTAPS - 1 + SEQ + 1])
        cvo = place("cvo", W + 98336, [P, 2, SEQ])
        dsq = place("dsq", W + 73728, [P, SEQ])
        drs = place("drs", W + 77824, [P, SEQ])
        vf = place("vf", W + 57344, [P, SEQ])
        cv_sq = place("cv_sq", W + 90112, [P, 2, SEQ])

        y_all = place("y_all", 4 * col, [P, NBLK, HEADS, P])
        a_all = place("a_all", 12 * col, [P, NBLK, HEADS, P])
        lane = [[place(f"lane{v}_{k}", W + 65536 + (6 * v + k) * 2048, [P, HEADS, P]) for k in range(6)]
                for v in range(2)]
        la_b, dec, e_row, b_t, off_t, x_inv = zip(*lane)
        g1 = la_b
        kd, r_u, u_sc = [place(n, W + 90112 + k * 2048, [P, HEADS, P]) for k, n in enumerate(("kd", "r_u", "u_sc"))]
        state = place("state", W + 96256, [P, 2, HEADS, P])
        osq = place("osq", W + 65536, [P, 2, SEQ])
        ors = place("ors", W + 73728, [P, SEQ])
        oy = place("oy", W + 77824, [P, 2, SEQ])

        u2 = place("u2", W, [P, 4, L])
        q2 = place("q2", W + 4 * col, [P, 8, L])
        k2 = place("k2", W + 12 * col, [P, 2, L])
        ks2 = place("ks2", W + 14 * col, [P, 2, L])
        vt2 = place("vt2", W + 66560, [P, NBLK, 256])
        vm2 = place("vm2", W + 66560 + 8192, [P, 256])
        v2 = place("v2", W + 83328, [P, 2, L])
        sc = place("sc", W + 91648, [P, 2, 2, META + 256])
        pt = place("pt", W + 96000, [P, 2, 2, 384])
        st = place("st", W + 102144, [P, 2, 5, 2])
        et = place("et", W + 4 * col, [P, 4, SC, 2, P])
        hbd = place("hbd", W + 12 * col, [P, 4, SC, P])
        xs = place("xs", W + 16 * col, [P, NCH + 1, 2, PAIRS])
        bl = [[place(f"bl{v}{r}", W + 83328 + (2 * v + r) * 2048, [P, PAIRS, 32]) for r in range(2)] for v in range(2)]
        ssm_in = place("ssm_in", W + 91520, [P, 4, PAIRS, 32])
        prod = [place(f"prod{r}", W + 99712 + r * 2048, [P, PAIRS, 32]) for r in range(2)]
        quad = place("quad", W + 103808, [P, 2, 2, PAIRS])
        gstage = place("gstage", W + 104192, [P, 2, 352])
        y_hi = place("y_hi", W + 12 * col, [P, 4, L], F32R)
        y_lo = place("y_lo", W + 16 * col, [P, 4, L], F32R)
        gld = place("gld", W + 83328, [P, 2, 2, L])
        gtmp = place("gtmp", W + 83328 + 4 * col, [P, 3, 512])

        acc = ctx.enter_context(nc.psum_tensor("acc", [P, 8, 512], F32))

        SEG = slab_plan(t, parts)
        split_done = sem("split_done")
        raw_full = two("raw_full")
        acc_full, acc_free = two("acc_full"), two("acc_free")
        aux_full, aux_free = two("aux_full"), two("aux_free")

        EVENT = {}

        def event(name):
            EVENT[name] = (len(EVENT) % 2, len(EVENT) // 2)

        if "mix1" in parts:
            for name in ["logits", "decays"] + [f"gm_t{e}" for e in range(4)] + [f"gm_s{e}" for e in range(4)]:
                event(name)
            for tile in range(12):
                for c in range(2):
                    event(f"dn{tile}_{c}")
            for name in ("cv_mean0", "cv_mean1", "cv_var0", "cv_var1"):
                event(name)
            for h in range(HEADS):
                for c in range(2):
                    event(f"on{h}_{c}")
        for name in ("v2_0", "v2_1", "v2_2", "v2_3", "v2_m"):
            event(name)

        def aux(name):
            return acc[:, 6 + EVENT[name][0], :]

        def aux_wait(eng, name):
            b, turn = EVENT[name]
            eng.wait_ge(aux_full[b], turn + 1)

        def aux_take(eng, name):
            b, turn = EVENT[name]
            if turn:
                eng.wait_ge(aux_free[b], turn)

        def aux_done(ins, name):
            ins.then_inc(aux_full[EVENT[name][0]], 1)

        def aux_release(ins, name):
            ins.then_inc(aux_free[EVENT[name][0]], 1)

        def chunk_no(seg, i, c):
            return i * len(seg.chunks) + (seg.q0 + c)

        def acc_wait(eng, seg, i, j, c):
            eng.wait_ge(acc_full[j], chunk_no(seg, i, c) + 1)

        ones, ident = const("ones"), const("ident")
        block = ctx.enter_context(nc.Block())

        @block.sync
        def _(sp):
            sp.dma_start(consts[:, :], t["consts"]).then_inc(sem("params_full"), 16)
            sp.dma_start(params[:, :], t["params"]).then_inc(sem("params_full"), 16)
            for seg in SEG.values():
                width = seg.kt * P

                def load(i, j, seg=seg, width=width):
                    sp.dma_start(w_raw[:, j:j + 1, 0:width], seg.src(i, j).rearrange("a p n -> p a n")).then_inc(raw_full[j], 16)

                if seg.n0 == 0:
                    for j in range(2):
                        load(0, j)
                with sp.Fori(1 if seg.n0 == 0 else 0, seg.pairs) as i:
                    for j in range(2):
                        sp.wait_ge(split_done, i * 2 + (seg.n0 + j - 1))
                        load(i, j)
            for (buf, dst, name, value) in dumps or []:
                sp.wait_ge(sem(name), value)
                sp.dma_start(dst, buf).then_inc(sem("dumped"), 16)
            if dumps:
                sp.wait_ge(sem("dumped"), 16 * len(dumps))

        @block.gpsimd
        def _(pool):
            own = Chain(pool, sem("pool_own"))
            pool.wait_ge(sem("params_full"), 32)
            for seg in SEG.values():
                width, n = seg.kt * P, len(seg.chunks)

                def split(i, j, seg=seg, width=width, n=n):
                    pool.wait_ge(raw_full[j], (i + seg.n0 // 2 + 1) * 16)
                    raw, hi, lo = w_raw[:, j, 0:width], w_hi[:, j, 0:width], w_lo[:, j, 0:width]
                    if not (seg.n0 == 0 and isinstance(i, int) and i == 0):
                        pool.wait_ge(acc_full[j], i * n + seg.q0)
                    blocks = "p (k n) -> p k n"
                    own.link(pool.tensor_tensor(hi.rearrange(blocks, n=P), raw.rearrange(blocks, n=P),
                                                ones.unsqueeze(1).broadcast_to([P, seg.kt, P]), ALU.mult))
                    pool.tensor_tensor(lo, raw, hi.bitcast(F32), ALU.subtract).then_inc(split_done, 1)

                if seg.n0 == 0:
                    for j in range(2):
                        split(0, j)
                    own.base, own.k = own.k - 2, 0
                    with pool.Fori(1, seg.pairs) as i:
                        own.i, own.per = i, 2
                        for j in range(2):
                            split(i, j)
                    own.base, own.k, own.i = 2 * seg.pairs, 0, None
                else:
                    with own.loop(seg.pairs, 2) as i:
                        for j in range(2):
                            split(i, j)

        def pe_norm(pe, name, chunks, ready=1):
            pe.wait_ge(sem("ssq_" + name), ready)
            for c, (c0, w) in enumerate(chunks):
                pe.matmul(acc[:, c, 0:w], const("mean"), ssq[:, c0:c0 + w], start=True, stop=True)\
                  .then_inc(sem("ms_" + name), 1)

        def act_norm(act, name, chunks, split=True):
            for c, (c0, w) in enumerate(chunks):
                act.wait_ge(sem("ms_" + name), c + 1)
                act.activation(rs[:, c0:c0 + w], acc[:, c, 0:w], ACT.Sqrt, bias=const("eps")).then_inc(sem("sd_" + name), 1)
            if split:
                for c, (c0, w) in enumerate(chunks):
                    for k in range(KD):
                        act.wait_ge(sem("scaled_" + name), c * KD + k + 1)
                        act.copy(h_hi[:, k, c0:c0 + w], tmp[:, k % 4, 0:w]).then_inc(sem("hi_" + name), 1)

        def dve_norm(dve, own, name, chunks, gain, dst=None):
            for c, (c0, w) in enumerate(chunks):
                dve.wait_ge(sem("sd_" + name), c + 1)
                own.link(dve.reciprocal(rs[:, c0:c0 + w], rs[:, c0:c0 + w]))
                if dst is not None:
                    for k in range(KD):
                        own.mark(dve.scalar_tensor_tensor(dst[:, k, c0:c0 + w], x[:, k, c0:c0 + w], gain[:, k:k + 1],
                                                          rs[:, c0:c0 + w], ALU.mult, ALU.mult))
                    continue
                for k in range(KD + 2):
                    if k < KD:
                        if k >= 4:
                            own.wait(1)
                        dve.scalar_tensor_tensor(tmp[:, k % 4, 0:w], x[:, k, c0:c0 + w], gain[:, k:k + 1],
                                                 rs[:, c0:c0 + w], ALU.mult, ALU.mult).then_inc(sem("scaled_" + name), 1)
                    if k >= 2:
                        dve.wait_ge(sem("hi_" + name), c * KD + k - 1)
                        own.mark(dve.tensor_tensor(h_lo[:, k - 2, c0:c0 + w], tmp[:, (k - 2) % 4, 0:w],
                                                   h_hi[:, k - 2, c0:c0 + w].bitcast(F32), ALU.subtract))
                own.wait()
                dve.sem_inc(sem("h_" + name), 1)

        def pe_slab(pe, seg, i, j, rhs, before=None, order=None):
            n = len(seg.chunks)
            pe.wait_ge(split_done, i * 2 + (seg.n0 + j + 1))
            for c, (c0, w) in enumerate(seg.chunks):
                if before:
                    before(c)
                if not (seg.q0 == 0 and isinstance(i, int) and i == 0):
                    pe.wait_ge(acc_free[j], i * n + (seg.q0 + c + 1 - n))
                bank = acc[:, 3 * j + c, 0:w]
                for k in range(seg.kt):
                    wh, wl = w_hi[:, j, k * P:(k + 1) * P], w_lo[:, j, k * P:(k + 1) * P]
                    rh, rl = rhs[0][:, k, c0:c0 + w], rhs[1][:, k, c0:c0 + w]
                    pe.matmul(bank, wh, rh, start=(k == 0), stop=False)
                    pe.matmul(bank, wh, rl, start=False, stop=False)
                    ins = pe.matmul(bank, wl, rh, start=False, stop=(k == seg.kt - 1))
                ins.then_inc(acc_full[j], 1)

        def pe_ffn(pe, name, chunks):
            done = 0
            for part, nf in enumerate(FQ):
                if part == 0:
                    for c in range(len(chunks)):
                        pe.wait_ge(sem("h_" + name), c + 1)
                up, down = SEG[f"{name}_up{part}"], SEG[f"{name}_down{part}"]
                with pe.Fori(0, up.pairs) as i:
                    for j in range(2):
                        pe_slab(pe, up, i, j, (h_hi, h_lo))
                done += nf * len(chunks)
                pe.wait_ge(sem("ff_" + name), done)
                with pe.Fori(0, down.pairs) as i:
                    for j in range(2):
                        pe_slab(pe, down, i, j, (ff_hi, ff_lo))

        def act_ffn(act, name, chunks):
            n = len(chunks)
            for part in range(len(FQ)):
                seg = SEG[f"{name}_up{part}"]
                with act.Fori(0, seg.pairs) as i:
                    for c, (c0, w) in enumerate(chunks):
                        acc_wait(act, seg, i, 0, c)
                        act.wait_ge(acc_free[1], i * n + (seg.q0 + c + 1 - n))
                        act.activation(tmp[:, c, 0:w], acc[:, c, 0:w], ACT.Silu).then_inc(acc_free[0], 1)

        def dve_ffn(dve, own, name, chunks, scale, then):
            n = len(chunks)
            for part in range(len(FQ)):
                seg = SEG[f"{name}_up{part}"]
                with own.loop(seg.pairs, 2 * n) as i:
                    for c, (c0, w) in enumerate(chunks):
                        acc_wait(dve, seg, i, 1, c)
                        dve.wait_ge(acc_free[0], chunk_no(seg, i, c) + 1)
                        hi = ff_hi[:, bass.ds(i, 1), c0:c0 + w]
                        g, up = tmp[:, c:c + 1, 0:w], acc[:, 3 + c:4 + c, 0:w]
                        own.mark(dve.tensor_tensor(hi, g, up, ALU.mult))
                        own.wait(1)
                        dve.tensor_tensor(tmp[:, 3:4, 0:w], g, up, ALU.mult).then_inc(acc_free[1], 1)
                        dve.wait_ge(acc_free[1], chunk_no(seg, i, c) + 1)
                        own.wait()
                        own.mark(dve.tensor_tensor(ff_lo[:, bass.ds(i, 1), c0:c0 + w], tmp[:, 3:4, 0:w],
                                                   hi.bitcast(F32), ALU.subtract))
                own.wait()
                dve.sem_inc(sem("ff_" + name), seg.pairs * n)
                last = part == len(FQ) - 1
                if last:
                    own.link(dve.memset(ssq[:, :], 0.0))
                dve_residual(dve, own, SEG[f"{name}_down{part}"], scale, last)
            own.wait()
            dve.sem_inc(sem("ssq_" + then), 1)

        def dve_residual(dve, own, seg, scale, squares):
            with own.loop(seg.pairs, 4 * len(seg.chunks) if squares else 0) as i:
                for j in range(2):
                    for c, (c0, w) in enumerate(seg.chunks):
                        acc_wait(dve, seg, i, j, c)
                        xt = x[:, bass.ds(i * 2 + j, 1), c0:c0 + w]
                        dve.scalar_tensor_tensor(xt, acc[:, 3 * j + c:3 * j + c + 1, 0:w], scale, xt,
                                                 ALU.mult, ALU.add).then_inc(acc_free[j], 1)
                        if squares:
                            dve.wait_ge(acc_free[j], chunk_no(seg, i, c) + 1)
                            own.link(dve.tensor_tensor(sq[:, 0:w].unsqueeze(1), xt, xt, ALU.mult))
                            own.link(dve.tensor_tensor(ssq[:, c0:c0 + w], ssq[:, c0:c0 + w], sq[:, 0:w], ALU.add))

        def act_squares(act, name, cols):
            for k in range(KD):
                if k >= 2:
                    act.wait_ge(sem("sqsum_" + name), k - 1)
                act.activation(sqx[:, k % 2, cols], x[:, k, cols], ACT.Square).then_inc(sem("sqt_" + name), 1)

        def dve_squares(dve, own, name, cols):
            for k in range(KD):
                dve.wait_ge(sem("sqt_" + name), k + 1)
                if k == 0:
                    ins = dve.tensor_copy(ssq[:, cols], sqx[:, 0, cols])
                else:
                    dve.wait_ge(sem("sqsum_" + name), k)
                    ins = dve.tensor_tensor(ssq[:, cols], ssq[:, cols], sqx[:, k % 2, cols], ALU.add)
                ins.then_inc(sem("sqsum_" + name), 1)
            dve.wait_ge(sem("sqsum_" + name), KD)
            dve.sem_inc(sem("ssq_" + name), 1)

        def flat(a, b):
            return small[:, a:b, :].rearrange("p a b -> p (a b)")

        logits, beta, z_a, z_abs, z_ln, decay = (flat(0, 4), flat(4, 6), flat(6, 8), flat(8, 10), flat(10, 12), flat(12, 14))
        g_col, k_dec, c_dec, e_col, rate = flat(14, 16), flat(16, 18), flat(18, 20), flat(20, 22), flat(22, 23)
        gm_st, gm_mv, gm_sd = flat(24, 27), flat(27, 28), flat(28, 29)
        by_head = "p (n h) -> p n h"

        SLABS1 = [(seg, i, j) for seg in ("dn_kv", "dn_q", "dn_g") if "mix1" in parts
                  for i in range(SEG[seg].pairs) for j in range(2)]
        DN = [("k", h, 4 + h) for h in range(4)] + [("v", h, 8 + h) for h in range(4)] + [("q", h, h) for h in range(4)]
        KQ = [n for n, d in enumerate(DN) if d[0] != "v"]
        TAP_STEPS = 9

        def dn_dst(tile):
            kind, h, _ = DN[tile]
            return {"k": kT[:, h, :], "q": qT[:, h, :], "v": vf[:, :]}[kind]

        def blk(n):
            return slice(n * P, (n + 1) * P)

        def cc(c):
            return slice(c * 512, (c + 1) * 512)

        def pe_mix1(pe):
            for c in range(2):
                pe.wait_ge(sem("h_mix1"), c + 1)
            pe.wait_ge(sem("ba_full"), 1)
            aux_take(pe, "logits")
            for n in range(NBLK):
                cols = slice(META + n * P, META + (n + 1) * P)
                for k in range(KD):
                    out = aux("logits")[:, n * 8:n * 8 + 8]
                    pe.matmul(out, h_hi[:, k, cols], ba_hi[:, k, :], start=(k == 0), stop=False)
                    pe.matmul(out, h_hi[:, k, cols], ba_lo[:, k, :], start=False, stop=False)
                    ins = pe.matmul(out, h_lo[:, k, cols], ba_hi[:, k, :], start=False, stop=(k == KD - 1))
            aux_done(ins, "logits")
            h = (h_hi, h_lo)
            for i in range(2):
                for j in range(2):
                    pe_slab(pe, SEG["gm"], i, j, h)
            pe_slab(pe, SEG["cv"], 0, 0, h)
            pe.wait_ge(sem("decay_full"), 1)
            aux_take(pe, "decays")
            for m, name in enumerate(("upper", "lower", "ones")):
                ins = pe.matmul(aux("decays")[:, 32 * m:32 * m + 32], const(name), decay, start=True, stop=True)
            aux_done(ins, "decays")
            pe.wait_ge(sem("gm_full"), 8)
            for e in range(4):
                aux_take(pe, f"gm_t{e}")
                for n in (2 * e, 2 * e + 1):
                    for ct in range(2):
                        ins = pe.transpose(aux(f"gm_t{e}")[:, (n % 2) * 256 + ct * P:(n % 2) * 256 + ct * P + P],
                                           gm_v[:, ct, blk(n)], ident)
                aux_done(ins, f"gm_t{e}")
            for i, j in ((0, 1), (1, 0), (1, 1)):
                pe_slab(pe, SEG["cv"], i, j, h)

            def gating():
                pe.wait_ge(sem("gm_normed"), 1)
                for e in range(4):
                    ct, half = e // 2, e % 2
                    aux_take(pe, f"gm_s{e}")
                    for n in range(4 * half, 4 * half + 4):
                        for hh in range(2):
                            hd = 2 * ct + hh
                            out = aux(f"gm_s{e}")[hh * 64:hh * 64 + 64, (n % 4) * P:(n % 4) * P + P]
                            pe.matmul(out, gm_t[:, n, hd * 64:hd * 64 + 64], gm_par[:, 1024 + hd * P:1024 + hd * P + P],
                                      start=True, stop=False, skip_group_check=True)
                            ins = pe.matmul(out, ones[0:1, 0:64], gm_par[0:1, 512 + hd * P:512 + hd * P + P],
                                            start=False, stop=True, skip_group_check=True)
                    aux_done(ins, f"gm_s{e}")

            def dn_event(u):
                kind, hd, _ = DN[u]
                for c in range(2):
                    name = f"dn{u}_{c}"
                    if kind == "v":
                        pe.wait_ge(sem("silu_done"), u + 1)
                        aux_take(pe, name)
                        for n in range(4):
                            ins = pe.transpose(aux(name)[:, n * P:n * P + P], vf[:, blk(4 * c + n)], ident)
                    else:
                        pe.wait_ge(sem("dsq_full"), KQ.index(u) + 1)
                        aux_take(pe, name)
                        ins = pe.matmul(aux(name), ones, dsq[:, cc(c)], start=True, stop=True)
                    aux_done(ins, name)

            for s, (seg, i, j) in enumerate(SLABS1):
                pe_slab(pe, SEG[seg], i, j, h)
                if s == 0:
                    gating()
                if 0 <= s - 2 < 12:
                    dn_event(s - 2)
            for stat, src in (("mean", cv_acc), ("var", cv_sq)):
                for c in range(2):
                    pe.wait_ge(sem("cv_" + stat + "_in"), 1 if stat == "mean" else c + 1)
                    aux_take(pe, f"cv_{stat}{c}")
                    for ct in range(2):
                        ins = pe.matmul(aux(f"cv_{stat}{c}"), const("mean256"), src[:, ct, cc(c)],
                                        start=(ct == 0), stop=(ct == 1))
                    aux_done(ins, f"cv_{stat}{c}")
            for j in range(2):
                pe.wait_ge(acc_free[j], SEG["dn_g"].q0 + 4)
            for b in range(2):
                pe.wait_ge(aux_free[b], EVENT["cv_var" + str(b)][1] + 1)
            pe.wait_ge(sem("dscaled"), 8)
            for it in range(NBLK // 2):
                for v in range(2):
                    n = 2 * it + v
                    pe.wait_ge(sem("la_full"), n + 1)
                    if it:
                        pe.wait_ge(sem(f"xy_done{v}"), 7 * it)
                    for hd in range(HEADS):
                        o = slice(hd * P, hd * P + P)
                        pe.matmul(acc[:, 4 * v, o], la_b[v][:, hd, :], const("upper"), start=True, stop=True)
                        pe.matmul(acc[:, 4 * v + 1, o], kT[:, hd, blk(n)], kT[:, hd, blk(n)], start=True, stop=True)
                        ins = pe.matmul(acc[:, 4 * v + 2, o], kT[:, hd, blk(n)], qT[:, hd, blk(n)], start=True, stop=True)
                    ins.then_inc(sem(f"g_full{v}"), 1)
                for lv in range(7):
                    for v in range(2):
                        n = 2 * it + v
                        pe.wait_ge(sem(f"off_full{v}"), 7 * it + lv + 1)
                        if lv:
                            pe.wait_ge(sem(f"xy_done{v}"), 7 * it + lv)
                        for hd in range(HEADS):
                            o = slice(hd * P, hd * P + P)
                            if lv == 0:
                                ins = pe.transpose(acc[:, 4 * v, o], off_t[v][:, hd, :], ident)
                            else:
                                ins = pe.matmul(acc[:, 4 * v + 1, o], off_t[v][:, hd, :], x_inv[v][:, hd, :], start=True, stop=True)
                        ins.then_inc(sem(f"g1_full{v}"), 1)
                    for v in range(2):
                        n = 2 * it + v
                        if lv == 0:
                            continue
                        pe.wait_ge(sem(f"g1_copied{v}"), 6 * it + lv)
                        for hd in range(HEADS):
                            o = slice(hd * P, hd * P + P)
                            if lv < 6:
                                pe.matmul(acc[:, 4 * v + 2, o], y_all[:, n, hd, :], g1[v][:, hd, :], start=True, stop=True)
                            ins = pe.matmul(acc[:, 4 * v + 3, o], g1[v][:, hd, :], y_all[:, n, hd, :], start=True, stop=True)
                        ins.then_inc(sem(f"xy_full{v}"), 1)
            for v in range(2):
                pe.wait_ge(sem(f"xy_done{v}"), 7 * NBLK // 2)
            for n in range(NBLK):
                cur = n % 2
                pe.wait_ge(sem("state_full"), n + 1)
                if n:
                    pe.wait_ge(sem("kd_full"), n)
                for hd in range(HEADS):
                    o = slice(hd * P, hd * P + P)
                    pe.transpose(acc[:, 1, o], kT[:, hd, blk(n)], ident)
                    ins = pe.matmul(acc[:, 0, o], kT[:, hd, blk(n)], state[:, cur, hd, :], start=True, stop=True)
                ins.then_inc(sem("ks_full"), 1)
                pe.wait_ge(sem("r_full"), n + 1)
                for hd in range(HEADS):
                    ins = pe.matmul(acc[:, 2, hd * P:hd * P + P], y_all[:, n, hd, :], r_u[:, hd, :], start=True, stop=True)
                ins.then_inc(sem("xr_full"), 1)
                pe.wait_ge(sem("u_full"), n + 1)
                pe.wait_ge(sem("kd_full"), n + 1)
                for hd in range(HEADS):
                    ins = pe.matmul(acc[:, 4, hd * P:hd * P + P], kd[:, hd, :], u_sc[:, hd, :], start=True, stop=True)
                ins.then_inc(sem("ds_full"), 1)
                if n:
                    pe.wait_ge(sem("o_copied"), n)
                for hd in range(HEADS):
                    o = slice(hd * P, hd * P + P)
                    pe.matmul(acc[:, 3, o], state[:, cur, hd, :], qT[:, hd, blk(n)], start=True, stop=False)
                    ins = pe.matmul(acc[:, 3, o], u_sc[:, hd, :], a_all[:, n, hd, :], start=False, stop=True)
                ins.then_inc(sem("o_full"), 1)
            for hd in range(HEADS):
                pe.wait_ge(sem("osq_full"), hd + 1)
                for c in range(2):
                    aux_take(pe, f"on{hd}_{c}")
                    aux_done(pe.matmul(aux(f"on{hd}_{c}"), const("mean128"), osq[:, hd % 2, cc(c)], start=True, stop=True),
                             f"on{hd}_{c}")
            pe.wait_ge(sem("mixed1"), 1)
            with pe.Fori(0, SEG["out1"].pairs) as i:
                for j in range(2):
                    pe_slab(pe, SEG["out1"], i, j, h)

        def act_mix1(act):
            own = Chain(act, sem("act_own"))
            act.wait_ge(sem("h_mix1"), 2)
            act.dma_start(gm_par[:, :], t["gm"]).then_inc(sem("gm_par_full"), 16)
            aux_wait(act, "logits")
            aux_release(act.copy(logits, aux("logits")[:, 0:64]), "logits")
            act.wait_ge(aux_free[EVENT["logits"][0]], 1)
            act.sem_inc(sem("logits_full"), 1)
            own.mark(act.activation(beta.rearrange(by_head, h=4), logits.rearrange("p (n e) -> p n e", e=8)[:, :, 0:4], ACT.Sigmoid))
            act.wait_ge(sem("z_full"), 1)
            own.link(act.activation(z_ln, z_abs, ACT.Exp, scale=-1.0))
            own.link(act.activation(z_ln, z_ln, ACT.Ln, bias=ones[:, 0:1]))
            own.link(act.activation(rate[:, 0:4], param("a_log"), ACT.Exp))
            act.sem_inc(sem("z_ln_full"), 1)
            for s in range(4):
                i, j = s // 2, s % 2
                for c in range(2):
                    acc_wait(act, SEG["gm"], i, j, c)
                    dst = (gm_u if i == 0 else gm_v)[:, j, cc(c)]
                    act.activation(dst, acc[:, 3 * j + c, :], ACT.Gelu).then_inc(acc_free[j], 1)
            for j in range(2):
                act.wait_ge(acc_free[j], chunk_no(SEG["gm"], 1, 1) + 1)
            act.sem_inc(sem("gm_full"), 8)
            for s in range(4):
                i, j = s // 2, s % 2
                if s == 1:
                    aux_wait(act, "decays")
                    sums = aux("decays")
                    own.mark(act.copy(g_col, sums[:, 0:32]))
                    own.mark(act.activation(e_col, sums[:, 0:32], ACT.Exp))
                    own.mark(act.activation(k_dec, sums[:, 32:64], ACT.Exp))
                    aux_release(act.activation(c_dec, sums[:, 64:96], ACT.Exp), "decays")
                    for e in range(4):
                        aux_wait(act, f"gm_t{e}")
                        aux_release(act.copy(gm_t[:, 2 * e:2 * e + 2, :], aux(f"gm_t{e}").rearrange("p (n c) -> p n c", n=2)), f"gm_t{e}")
                    act.wait_ge(sem("gm_var"), 1)
                    own.mark(act.activation(gm_sd[:, 0:8], gm_mv.rearrange("p (n e) -> p n e", e=2)[:, :, 1], ACT.Sqrt, bias=const("eps")))
                    own.wait()
                    act.sem_inc(sem("gm_sd_full"), 1)
                for c in range(2):
                    acc_wait(act, SEG["cv"], i, j, c)
                    if i == 0:
                        act.copy(cv_a[:, j, cc(c)], acc[:, 3 * j + c, :]).then_inc(acc_free[j], 1)
                    else:
                        act.activation(cv_g[:, j, cc(c)], acc[:, 3 * j + c, :], ACT.Sigmoid).then_inc(acc_free[j], 1)
            for s in range(16):
                seg, i, j = SLABS1[s]
                for c in range(2):
                    acc_wait(act, SEG[seg], i, j, c)
                    if s < 12:
                        if s >= 2:
                            act.wait_ge(sem("conv_done"), s - 1)
                        a = DTAPS - 1 + c * 512
                        ins = act.copy(pre[:, s % 2, a:a + 512], acc[:, 3 * j + c, :])
                    else:
                        ins = act.activation(gate[:, s - 12, cc(c)], acc[:, 3 * j + c, :], ACT.Silu)
                    ins.then_inc(acc_free[j], 1)
                if 0 <= s - 2 < 12:
                    kind, hd, _ = DN[s - 2]
                    for c in range(2):
                        name = f"dn{s - 2}_{c}"
                        aux_wait(act, name)
                        if kind == "v":
                            ins = act.copy(vtok[:, 4 * c:4 * c + 4, hd, :], aux(name).rearrange("p (n d) -> p n d", n=4))
                        else:
                            done = KQ.index(s - 2)
                            if done:
                                act.wait_ge(sem("dscaled"), done)
                            ins = act.activation(drs[:, cc(c)], aux(name), ACT.Sqrt, bias=const("eps"))
                        aux_release(ins, name)
                if 0 <= s - 1 < 12:
                    act.wait_ge(sem("conv_done"), s)
                    if s - 1 == 0:
                        act.wait_ge(sem("gm_gated"), 1)
                    act.activation(dn_dst(s - 1), cvo[:, (s - 1) % 2, :], ACT.Silu).then_inc(sem("silu_done"), 1)
                    if s - 1 in KQ:
                        act.wait_ge(sem("silu_done"), s)
                        act.activation(dsq[:, :], dn_dst(s - 1), ACT.Square).then_inc(sem("dsq_full"), 1)
            for c in range(2):
                act.wait_ge(sem("cv_centred"), 2 * c + 2)
                act.activation(cv_sq[:, :, cc(c)], cv_acc[:, :, cc(c)], ACT.Square).then_inc(sem("cv_var_in"), 1)
            for c in range(2):
                aux_wait(act, f"cv_var{c}")
                if c == 0:
                    act.wait_ge(sem("dscaled"), 8)
                aux_release(act.activation(drs[:, cc(c)], aux(f"cv_var{c}"), ACT.Sqrt, bias=const("eps")), f"cv_var{c}")
            act.wait_ge(sem("cv_normed"), 1)
            for ct in range(2):
                own.mark(act.activation(cv_acc[:, ct, :], cv_acc[:, ct, :], ACT.Silu,
                                        bias=param("cvln_b")[:, ct:ct + 1], scale=param("cvln_g")[:, ct:ct + 1]))
            own.wait()
            for j in range(2):
                act.wait_ge(acc_full[j], SEG["dn_g"].q0 + 4)
            for k in range(4):
                src = gm_u[:, k, :] if k < 2 else cv_acc[:, k - 2, :]
                act.copy(h_hi[:, k, META:L], src).then_inc(sem("mix_hi"), 1)
            for it in range(NBLK // 2):
                for v in range(2):
                    act.wait_ge(sem(f"dd_full{v}"), it + 1)
                    own.mark(act.activation(e_row[v][:, :, :], acc[:, 4 * v, :].rearrange("p (h i) -> p h i", h=4), ACT.Exp))
                    act.activation(dec[v][:, :, :], dec[v][:, :, :], ACT.Exp).then_inc(sem(f"dt_full{v}"), 1)
                for lv in range(1, 7):
                    for v in range(2):
                        act.wait_ge(sem(f"g1_full{v}"), 7 * it + lv + 1)
                        act.copy(g1[v][:, :, :], acc[:, 4 * v + 1, :].rearrange("p (h i) -> p h i", h=4))\
                           .then_inc(sem(f"g1_copied{v}"), 1)
            for n in range(NBLK):
                act.wait_ge(sem("ks_full"), n + 1)
                if n:
                    act.wait_ge(sem("ds_full"), n)
                for hd in range(HEADS):
                    ins = act.activation(kd[:, hd, :], acc[:, 1, hd * P:hd * P + P], ACT.Copy,
                                         scale=k_dec[:, n * 4 + hd:n * 4 + hd + 1])
                ins.then_inc(sem("kd_full"), 1)
                act.wait_ge(sem("o_full"), n + 1)
                act.copy(qT[:, :, blk(n)], acc[:, 3, :].rearrange("p (h i) -> p h i", h=4)).then_inc(sem("o_copied"), 1)
            act.wait_ge(sem("o_copied"), NBLK)
            for hd in range(HEADS + 1):
                if hd < HEADS:
                    act.activation(osq[:, hd % 2, :], qT[:, hd, :], ACT.Square).then_inc(sem("osq_full"), 1)
                    for c in range(2):
                        aux_wait(act, f"on{hd}_{c}")
                        if hd:
                            act.wait_ge(sem("oy_full"), hd)
                        aux_release(act.activation(ors[:, cc(c)], aux(f"on{hd}_{c}"), ACT.Sqrt, bias=const("eps")), f"on{hd}_{c}")
                if hd:
                    act.wait_ge(sem("oy_full"), hd)
                    act.copy(h_hi[:, 3 + hd, META:L], oy[:, (hd - 1) % 2, :]).then_inc(sem("mix_hi"), 1)
            act.wait_ge(sem("oy_full"), HEADS)
            for k in range(0, KD, 4):
                act.dma_start(x[:, k:k + 4, META:L], t["x"][:, k:k + 4, :]).then_inc(sem("x_full"), 16)

        def dve_mix1(dve, own):
            own.link(dve.tensor_copy(ba_hi[:, :, :], param("w_ba").rearrange("p (k e) -> p k e", k=KD)))
            own.link(dve.tensor_tensor(ba_lo[:, :, :], param("w_ba").rearrange("p (k e) -> p k e", k=KD),
                                       ba_hi[:, :, :].bitcast(F32), ALU.subtract))
            dve.sem_inc(sem("ba_full"), 1)
            dve.wait_ge(sem("logits_full"), 1)
            z3 = z_a.rearrange(by_head, h=4)
            own.link(dve.tensor_tensor(z3, logits.rearrange("p (n e) -> p n e", e=8)[:, :, 4:8],
                                       param("dt_bias").unsqueeze(1).broadcast_to([P, NBLK, 4]), ALU.add))
            dve.scalar_tensor_tensor(z_abs, z_a, -1.0, z_a, ALU.mult, ALU.max).then_inc(sem("z_full"), 1)
            dve.wait_ge(sem("z_full"), 1)
            own.link(dve.tensor_single_scalar(z_a, z_a, 0.0, ALU.max))
            dve.wait_ge(sem("z_ln_full"), 1)
            own.link(dve.tensor_tensor(z_a, z_a, z_ln, ALU.add))
            dve.scalar_tensor_tensor(decay.rearrange(by_head, h=4), z3, -1.0, rate[:, 0:4].unsqueeze(1).broadcast_to([P, NBLK, 4]),
                                     ALU.mult, ALU.mult).then_inc(sem("decay_full"), 1)
            dve.wait_ge(sem("gm_par_full"), 16)
            ws = gm_par[:, 1024:1536].rearrange("p (h i) -> p h i", h=4)
            own.mark(dve.tensor_tensor(ws, ws, const("upper").unsqueeze(1).broadcast_to([P, 4, P]), ALU.mult))
            for n in range(NBLK):
                b, turn = EVENT[f"gm_t{n // 2}"]
                dve.wait_ge(aux_free[b], turn + 1)
                own.link(dve.bn_stats(gm_st[:, 6 * n:6 * n + 6], gm_t[:, n, :]))
                own.mark(dve.bn_aggr(gm_mv[:, 2 * n:2 * n + 2], gm_st[:, 6 * n:6 * n + 6]))
            own.wait()
            dve.sem_inc(sem("gm_var"), 1)
            dve.wait_ge(sem("gm_sd_full"), 1)
            own.link(dve.reciprocal(gm_sd[:, 0:8], gm_sd[:, 0:8]))
            for n in range(NBLK):
                own.mark(dve.tensor_scalar(gm_t[:, n, :], gm_t[:, n, :], gm_mv[:, 2 * n:2 * n + 1], gm_sd[:, n:n + 1],
                                           ALU.subtract, ALU.mult))
            own.wait()
            for k, op in ((0, ALU.mult), (1, ALU.add)):
                own.link(dve.tensor_tensor(gm_t[:, :, :], gm_t[:, :, :],
                                           gm_par[:, 256 * k:256 * k + 256].unsqueeze(1).broadcast_to([P, NBLK, 256]), op))
            dve.sem_inc(sem("gm_normed"), 1)
            own.mark(dve.memset(cv_y[:, :, 0:TAPS - 1], 0.0))
            own.mark(dve.memset(pre[:, :, 0:DTAPS - 1], 0.0))
            for j in range(2):
                dve.wait_ge(acc_free[j], chunk_no(SEG["cv"], 1, 1) + 1)
            own.link(dve.tensor_tensor(cv_y[:, :, TAPS - 1:], cv_a[:, :, :], cv_g[:, :, :], ALU.mult))
            for e in range(4):
                aux_wait(dve, f"gm_s{e}")
                ct, half = e // 2, e % 2
                dst = gm_u[:, ct, cc(half)]
                aux_release(dve.tensor_tensor(dst, dst, aux(f"gm_s{e}"), ALU.mult), f"gm_s{e}")
            for e in (2, 3):
                b, turn = EVENT[f"gm_s{e}"]
                dve.wait_ge(aux_free[b], turn + 1)
            dve.sem_inc(sem("gm_gated"), 1)
            taps = [(ct, i) for i in range(TAPS) for ct in range(2)]
            per = -(-len(taps) // TAP_STEPS)
            for s in range(14):
                if s < 12:
                    seg, i, j = SLABS1[s]
                    for c in range(2):
                        dve.wait_ge(acc_free[j], chunk_no(SEG[seg], i, c) + 1)
                    if s >= 2:
                        dve.wait_ge(sem("silu_done"), s - 1)
                    w = param("dn_w").rearrange("p (t i) -> p t i", i=DTAPS)[:, DN[s][2], :]
                    b, dst = s % 2, cvo[:, s % 2, :]
                    own.link(dve.tensor_scalar(dst, pre[:, b, 0:SEQ], w[:, 0:1], None, ALU.mult))
                    for k in range(1, DTAPS):
                        ins = dve.scalar_tensor_tensor(dst, pre[:, b, k:k + SEQ], w[:, k:k + 1], dst, ALU.mult, ALU.add)
                        if k < DTAPS - 1:
                            own.link(ins)
                    ins.then_inc(sem("conv_done"), 1)
                if s - 2 in KQ:
                    kind = DN[s - 2][0]
                    for c in range(2):
                        b, turn = EVENT[f"dn{s - 2}_{c}"]
                        dve.wait_ge(aux_free[b], turn + 1)
                    own.link(dve.reciprocal(drs[:, :], drs[:, :]))
                    dst = dn_dst(s - 2)
                    dve.scalar_tensor_tensor(dst, dst, P ** -0.5 if kind == "q" else 1.0, drs[:, :],
                                             ALU.mult, ALU.mult).then_inc(sem("dscaled"), 1)
                for ct, k in taps[per * s:per * (s + 1)]:
                    src, w = cv_y[:, ct, k:k + SEQ], param("cv_w")[:, ct * TAPS + k:ct * TAPS + k + 1]
                    if k:
                        own.wait(1)
                        own.mark(dve.scalar_tensor_tensor(cv_acc[:, ct, :], src, w, cv_acc[:, ct, :], ALU.mult, ALU.add))
                    else:
                        own.mark(dve.tensor_scalar(cv_acc[:, ct, :], src, w, param("cv_b")[:, ct:ct + 1], ALU.mult, ALU.add))
                own.wait()
            dve.sem_inc(sem("cv_mean_in"), 1)
            for c in range(2):
                aux_wait(dve, f"cv_mean{c}")
                for ct in range(2):
                    dst = cv_acc[:, ct, cc(c)]
                    ins = dve.tensor_tensor(dst, dst, aux(f"cv_mean{c}"), ALU.subtract)
                    if ct == 0:
                        own.mark(ins)
                aux_release(ins, f"cv_mean{c}")
                own.wait()
                dve.wait_ge(aux_free[EVENT[f"cv_mean{c}"][0]], EVENT[f"cv_mean{c}"][1] + 1)
                dve.sem_inc(sem("cv_centred"), 2)
            for c in range(2):
                dve.wait_ge(aux_free[EVENT[f"cv_var{c}"][0]], EVENT[f"cv_var{c}"][1] + 1)
            own.link(dve.reciprocal(drs[:, :], drs[:, :]))
            dve.wait_ge(sem("cv_var_in"), 2)
            own.link(dve.tensor_tensor(cv_acc[:, :, :], cv_acc[:, :, :], drs[:, :].unsqueeze(1).broadcast_to([P, 2, SEQ]), ALU.mult))
            dve.sem_inc(sem("cv_normed"), 1)
            for k in range(4):
                src = gm_u[:, k, :] if k < 2 else cv_acc[:, k - 2, :]
                dve.wait_ge(sem("mix_hi"), k + 1)
                own.mark(dve.tensor_tensor(h_lo[:, k, META:L], src, h_hi[:, k, META:L].bitcast(F32), ALU.subtract))
            own.wait()
            own.link(dve.tensor_single_scalar(e_col, e_col, -1.0, ALU.mult))
            own.mark(dve.memset(state[:, 0, :, :], 0.0))
            own.wait()
            dve.sem_inc(sem("state_full"), 1)
            heads = [P, HEADS, P]

            def bank(b):
                return acc[:, b, :].rearrange("p (h i) -> p h i", h=HEADS)

            def mask(name):
                return const(name).unsqueeze(1).broadcast_to(heads)

            for it in range(NBLK // 2):
                for v in range(2):
                    n = 2 * it + v
                    if it:
                        dve.wait_ge(sem(f"xy_full{v}"), 6 * it)
                    dve.tensor_copy(la_b[v][:, :, :], decay[:, 4 * n:4 * n + 4].unsqueeze(2).broadcast_to(heads))\
                       .then_inc(sem("la_full"), 1)
                for v in range(2):
                    n = 2 * it + v
                    dve.wait_ge(sem(f"g_full{v}"), it + 1)
                    for hd in range(HEADS):
                        ins = dve.scalar_tensor_tensor(dec[v][:, hd, :], const("negmask"), g_col[:, 4 * n + hd:4 * n + hd + 1],
                                                       acc[:, 4 * v, hd * P:hd * P + P], ALU.subtract, ALU.add)
                    ins.then_inc(sem(f"dd_full{v}"), 1)
                for v in range(2):
                    n = 2 * it + v
                    dve.wait_ge(sem(f"dt_full{v}"), it + 1)
                    own.mark(dve.tensor_tensor(a_all[:, n, :, :], bank(4 * v + 2), dec[v][:, :, :], ALU.mult))
                    own.link(dve.tensor_tensor(b_t[v][:, :, :], bank(4 * v + 1), dec[v][:, :, :], ALU.mult))
                    for hd in range(HEADS):
                        own.mark(dve.scalar_tensor_tensor(b_t[v][:, hd, :], b_t[v][:, hd, :], beta[:, 4 * n + hd:4 * n + hd + 1],
                                                          const("strict"), ALU.mult, ALU.mult))
                    own.mark(dve.tensor_tensor(qT[:, :, blk(n)], qT[:, :, blk(n)], e_row[v][:, :, :], ALU.mult))
                    own.wait()
                    own.link(dve.tensor_tensor(off_t[v][:, :, :], b_t[v][:, :, :], mask("off1"), ALU.mult))
                    dve.sem_inc(sem(f"off_full{v}"), 1)
                    own.mark(dve.tensor_tensor(y_all[:, n, :, :], mask("ident"), off_t[v][:, :, :], ALU.subtract))
                for lv in range(7):
                    for v in range(2):
                        n = 2 * it + v
                        dve.wait_ge(sem(f"g1_full{v}"), 7 * it + lv + 1)
                        if lv < 6:
                            own.wait()
                            dve.tensor_tensor(off_t[v][:, :, :], b_t[v][:, :, :], mask(f"off{2 << lv}"), ALU.mult)\
                               .then_inc(sem(f"off_full{v}"), 1)
                        if lv == 0:
                            own.link(dve.tensor_tensor(x_inv[v][:, :, :], mask("ident"), bank(4 * v), ALU.subtract))
                        else:
                            dve.wait_ge(sem(f"xy_full{v}"), 6 * it + lv)
                            if lv < 6:
                                own.mark(dve.tensor_tensor(x_inv[v][:, :, :], x_inv[v][:, :, :], bank(4 * v + 2), ALU.subtract))
                            own.link(dve.tensor_tensor(y_all[:, n, :, :], y_all[:, n, :, :], bank(4 * v + 3), ALU.subtract))
                        dve.sem_inc(sem(f"xy_done{v}"), 1)
            for n in range(NBLK):
                cur = n % 2
                dve.wait_ge(sem("ks_full"), n + 1)
                for hd in range(HEADS):
                    ins = dve.scalar_tensor_tensor(r_u[:, hd, :], acc[:, 0, hd * P:hd * P + P], e_col[:, 4 * n + hd:4 * n + hd + 1],
                                                   vtok[:, n, hd, :], ALU.mult, ALU.add)
                ins.then_inc(sem("r_full"), 1)
                dve.wait_ge(sem("xr_full"), n + 1)
                if n:
                    dve.wait_ge(sem("o_full"), n)
                dve.tensor_tensor(u_sc[:, :, :], bank(2), beta[:, 4 * n:4 * n + 4].unsqueeze(2).broadcast_to(heads), ALU.mult)\
                   .then_inc(sem("u_full"), 1)
                dve.wait_ge(sem("ds_full"), n + 1)
                for hd in range(HEADS):
                    own.mark(dve.scalar_tensor_tensor(state[:, 1 - cur, hd, :], state[:, cur, hd, :],
                                                      c_dec[:, 4 * n + hd:4 * n + hd + 1],
                                                      acc[:, 4, hd * P:hd * P + P], ALU.mult, ALU.add))
                own.wait()
                dve.sem_inc(sem("state_full"), 1)
            for hd in range(HEADS):
                for c in range(2):
                    b, turn = EVENT[f"on{hd}_{c}"]
                    dve.wait_ge(aux_free[b], turn + 1)
                own.link(dve.reciprocal(ors[:, :], ors[:, :]))
                dst = oy[:, hd % 2, :]
                own.link(dve.scalar_tensor_tensor(dst, qT[:, hd, :], param("dn_norm")[:, 0:1], ors[:, :], ALU.mult, ALU.mult))
                dve.tensor_tensor(dst, dst, gate[:, hd, :], ALU.mult).then_inc(sem("oy_full"), 1)
                dve.wait_ge(sem("mix_hi"), 5 + hd)
                own.mark(dve.tensor_tensor(h_lo[:, 4 + hd, META:L], dst, h_hi[:, 4 + hd, META:L].bitcast(F32), ALU.subtract))
            own.wait()
            dve.sem_inc(sem("mixed1"), 1)
            own.link(dve.memset(ssq[:, :], 0.0))
            dve.wait_ge(sem("x_full"), 64)
            dve_residual(dve, own, SEG["out1"], 1.0, True)
            own.wait()
            dve.sem_inc(sem("ssq_ffn0"), 1)

        INV_2PI, ROUND = 1.0 / (2.0 * math.pi), 12582912.0
        PI_A, PI_B = 6.28125, 0.0019350051879882812
        PI_C = 2.0 * math.pi - PI_A - PI_B
        PI_MAX = 3.1415925
        ROWS = dict(step=16, real=17, mag=18, angle=19, turns=20, rest=21, rest_c=22, sin=23, cos=24,
                    l_re=26, l_im=27, c_re=28, c_im=29, den=30, part=31)
        u2s = u2[:, :, :].rearrange("p t (m s) -> p t s m", s=SC)

        def row(name):
            return small[:, ROWS[name], :]

        def power(t, r):
            return small[:, 2 * (t - 1) + r, :]

        step8 = small[:, 16:20, :].rearrange("p (a b) s -> p a b s", a=2)

        UNITS = [(bi, hp) for bi in range(NBLK + 1) for hp in range(8)]

        def unit(u):
            bi, hp = UNITS[u]
            if bi == 0:
                return hp, slice(0, META), META, META, const("band0")[0:META, META:2 * META]
            n = bi - 1
            cols = slice(META + n * P, META + (n + 1) * P)
            return (hp, cols, P, META + P, const("band0")) if n == 0 else (hp, cols, P, META + 2 * P, const("band"))

        def at_bank(u):
            return 2 * ((u + 1) % 2)

        def at_chunk(f):
            return SEG["at_h"], f // 6, f // 3 % 2, f % 3

        GATE_CHUNKS = 6 * (8 - GATES_A)

        def gates_of(u):
            total, n = GATE_CHUNKS * KD, len(UNITS)
            return [divmod(g, KD) for g in range(total * u // n, total * (u + 1) // n)] if u < n else []

        def pe_mix2(pe):
            h = (h_hi, h_lo)
            for c in range(3):
                pe.wait_ge(sem("h_mix2"), c + 1)
            for i in range(2):
                for j in range(2):
                    pe_slab(pe, SEG["at_u"], i, j, h)
            for j in range(2):
                pe.wait_ge(acc_free[j], SEG["at_u"].q0 + 6)
            pe.wait_ge(sem("ssm_c_full"), 1)
            for d in range(SC):
                pe.wait_ge(sem("bl_full"), d + 1)
                if d >= 2:
                    pe.wait_ge(sem("et_copied"), d - 1)
                b0 = 3 * (d % 2)
                for ct in range(4):
                    for r in range(2):
                        pe.transpose(acc[:, b0 + r, ct * P:ct * P + P],
                                     bl[d % 2][r][:, 4 * ct:4 * ct + 4, :].rearrange("p a b -> p (a b)"), ident)
                for p in range(PAIRS):
                    r0, out = 32 * (p % 4), acc[32 * (p % 4):32 * (p % 4) + 32, b0 + 2, 32 * (p // 4):32 * (p // 4) + 32]
                    pe.matmul(out, bl[d % 2][0][:, p, :], ssm_in[:, 2, p, :], start=True, stop=False, skip_group_check=True)
                    ins = pe.matmul(out, bl[d % 2][1][:, p, :], ssm_in[:, 3, p, :], start=False, stop=True, skip_group_check=True)
                ins.then_inc(sem("et_full"), 1)
            pe.wait_ge(sem("et_copied"), SC)
            for p in range(PAIRS):
                if p >= 2:
                    pe.wait_ge(sem("end_copied"), p - 1)
                r0, ct = 32 * (p % 4), p // 4
                for r in range(2):
                    for s in range(SC):
                        ins = pe.matmul(acc[:, 6 + p % 2, r * NCH:(r + 1) * NCH], et[r0:r0 + 32, ct, SC - 1 - s, r, :],
                                        u2s[r0:r0 + 32, ct, s, :], start=(s == 0), stop=(s == SC - 1))
                ins.then_inc(sem("end_full"), 1)
            pe.wait_ge(sem("end_copied"), PAIRS)
            with pe.Fori(0, 4) as i:
                for j in range(2):
                    pe_slab(pe, SEG["at_q"], i, j, h)
            with pe.Fori(0, GATES_A) as i:
                for j in range(2):
                    pe_slab(pe, SEG["at_g"], i, j, h)
            for j in range(2):
                pe.wait_ge(acc_free[j], SEG["at_g"].q0 + 3 * GATES_A)
            pe.wait_ge(sem("states_full"), 1)
            for n, s in enumerate(reversed(range(SC))):
                pe.wait_ge(sem("gl_full"), n + 1)
                for ct in range(4):
                    bank = 2 * (n % 4) + ct // 2
                    if n >= 4:
                        pe.wait_ge(sem("y_out"), 4 * (n - 4) + 4)
                    cols = slice((ct % 2) * NCH, (ct % 2 + 1) * NCH)
                    for d in range(s + 1):
                        pe.matmul(acc[:, bank, cols], hbd[:, ct, d, :], u2s[:, ct, s - d, :],
                                  start=(d == 0), stop=False, skip_group_check=True)
                    for pp in range(4):
                        p = 4 * ct + pp
                        out = acc[32 * pp:32 * pp + 32, bank, cols]
                        for r in range(2):
                            ins = pe.matmul(out, bl[n % 2][r][:, p, :], xs[:, 0:NCH, r, p],
                                            start=False, stop=(r == 1), skip_group_check=True)
                ins.then_inc(sem("y_full"), 1)
            pe.wait_ge(sem("y_out"), 4 * SC)
            for i in range(2):
                for j in range(2):
                    pe_slab(pe, SEG["at_kv"], i, j, h)
            for j in range(2):
                pe.wait_ge(acc_free[j], SEG["at_kv"].q0 + 6)
            for e in range(4):
                aux_take(pe, f"v2_{e}")
                for nn in range(2):
                    for ct in range(2):
                        c0 = META + (2 * e + nn) * P
                        ins = pe.transpose(aux(f"v2_{e}")[:, nn * 256 + ct * P:nn * 256 + ct * P + P], v2[:, ct, c0:c0 + P], ident)
                aux_done(ins, f"v2_{e}")
            aux_take(pe, "v2_m")
            for ct in range(2):
                ins = pe.transpose(aux("v2_m")[0:META, ct * P:ct * P + P], v2[:, ct, 0:META], ident)
            aux_done(ins, "v2_m")
            for b in range(2):
                name = "v2_m" if EVENT["v2_m"][0] == b else "v2_3"
                pe.wait_ge(aux_free[b], EVENT[name][1] + 1)
            pe.wait_ge(sem("ks_swapped"), 32)

            def gate_piece(piece):
                f, k = piece
                seg, i, j, c = at_chunk(f)
                c0, w = CH2[c]
                if k == 0:
                    pe.wait_ge(split_done, i * 2 + (seg.n0 + j + 1))
                    if f >= 2:
                        _, i_, j_, c_ = at_chunk(f - 2)
                        pe.wait_ge(acc_free[j_], chunk_no(seg, i_, c_) + 1)
                bank = acc[:, 6 + f % 2, 0:w]
                wh, wl = w_hi[:, j, k * P:(k + 1) * P], w_lo[:, j, k * P:(k + 1) * P]
                rh, rl = h_hi[:, k, c0:c0 + w], h_lo[:, k, c0:c0 + w]
                pe.matmul(bank, wh, rh, start=(k == 0), stop=False, skip_group_check=True)
                pe.matmul(bank, wh, rl, start=False, stop=False, skip_group_check=True)
                ins = pe.matmul(bank, wl, rh, start=False, stop=(k == KD - 1), skip_group_check=True)
                if k == KD - 1:
                    ins.then_inc(acc_full[j], 1)

            def scores(u):
                hp, cols, nq, kw, _ = unit(u)
                kv = hp // 2
                if u >= 2:
                    pe.wait_ge(sem("at_masked"), u - 1)
                if u >= 3:
                    pe.wait_ge(sem("at_oc"), u - 2)
                for hd in range(2):
                    r = slice(64 * hd, 64 * hd + 64)
                    keys = (k2 if (kv % 2) == hd else ks2)[r, kv // 2, :]
                    b = 2 * (u % 2) + hd
                    if kw <= META + P:
                        ins = pe.matmul(acc[0:nq, b, 0:kw], q2[r, hp, cols], keys[:, 0:kw], start=True, stop=True)
                    else:
                        pe.matmul(acc[0:nq, b, 0:META], q2[r, hp, cols], keys[:, 0:META], start=True, stop=True)
                        ins = pe.matmul(acc[0:nq, b, META:kw], q2[r, hp, cols], keys[:, cols.start - P:cols.stop], start=True, stop=True)
                ins.then_inc(sem("at_s"), 1)

            def turn(u):
                hp, cols, nq, kw, _ = unit(u)
                pe.wait_ge(sem("at_p"), u + 1)
                if u:
                    pe.wait_ge(sem("at_ptc"), u)
                for hd in range(2):
                    pr = sc[0:nq, u % 2, hd, :]
                    ins = pe.transpose(acc[0:META, 4 + hd, 0:nq], pr[:, 0:META], ident[0:nq, 0:nq])
                    for k in range((kw - META) // P):
                        a = 384 - (kw - META) + k * P
                        ins = pe.transpose(acc[:, 4 + hd, a:a + nq], pr[:, META + k * P:META + (k + 1) * P], ident[0:nq, 0:nq])
                ins.then_inc(sem("at_pt"), 1)

            def values(u):
                hp, cols, nq, kw, _ = unit(u)
                vc = slice(64 * (hp // 2), 64 * (hp // 2) + 64)
                pe.wait_ge(sem("at_ptc"), u + 1)
                if u + 1 < len(UNITS):
                    pe.wait_ge(sem("at_masked"), u + 2)
                else:
                    pe.wait_ge(sem("at_oc"), u - 1)
                nk = (kw - META) // P
                for hd in range(2):
                    out = acc[64 * hd:64 * hd + 64, at_bank(u), 384:384 + nq]
                    ins = pe.matmul(out, vm2[0:META, vc], pt[0:META, u % 2, hd, 0:nq], start=True, stop=(nk == 0), skip_group_check=True)
                    for k in range(nk):
                        n = UNITS[u][0] - nk + k
                        a = 384 - nk * P + k * P
                        ins = pe.matmul(out, vt2[:, n, vc], pt[:, u % 2, hd, a:a + P], start=False, stop=(k == nk - 1), skip_group_check=True)
                ins.then_inc(sem("at_o"), 1)

            for u in range(len(UNITS) + 2):
                for piece in gates_of(u):
                    gate_piece(piece)
                if u >= 2:
                    values(u - 2)
                if u < len(UNITS):
                    scores(u)
                if 1 <= u <= len(UNITS):
                    turn(u - 1)
            pe.wait_ge(sem("at_oc"), len(UNITS))
            pe.wait_ge(sem("at_masked"), len(UNITS))
            pe.wait_ge(sem("y_split"), 4)
            with pe.Fori(0, 8) as i:
                for j in range(2):
                    pe_slab(pe, SEG["glu"], i, j, (y_hi, y_lo))
            pe.wait_ge(sem("glu_done"), 9)
            with pe.Fori(0, SEG["out2"].pairs) as i:
                for j in range(2):
                    pe_slab(pe, SEG["out2"], i, j, h)

        def act_mix2(act):
            own = Chain(act, sem("act_own2"))
            act.dma_start(t["x_kept"], x[:, :, :]).then_inc(sem("x_stored"), 16)
            act.wait_ge(sem("h_mix2"), 3)
            act.dma_start(ssm_in[:, :, :, :], t["ssm"].rearrange("p (a b c) -> p a b c", a=4, b=PAIRS)).then_inc(sem("ssm_full"), 16)
            act.activation(row("step"), param("log_step"), ACT.Exp).then_inc(sem("ssm_step"), 1)
            act.wait_ge(sem("ssm_angle"), 1)
            own.mark(act.activation(row("mag"), row("real"), ACT.Exp))
            act.wait_ge(sem("ssm_rest"), 1)
            own.mark(act.activation(row("sin"), row("rest"), ACT.Sin))
            own.link(act.activation(row("cos"), row("rest_c"), ACT.Sin))
            act.sem_inc(sem("ssm_trig"), 1)
            act.wait_ge(sem("x_stored"), 16)
            def evacuate(seg, i, j, dst, func=ACT.Copy):
                for c, (c0, w) in enumerate(CH2):
                    acc_wait(act, SEG[seg], i, j, c)
                    act.activation(dst[:, c0:c0 + w], acc[:, 3 * j + c, 0:w], func).then_inc(acc_free[j], 1)

            for s in range(4):
                evacuate("at_u", s // 2, s % 2, u2[:, s, :])
            act.wait_ge(sem("hbd_zero"), 1)
            for d in range(SC):
                act.wait_ge(sem("et_full"), d + 1)
                b0 = 3 * (d % 2)
                for r in range(2):
                    own.mark(act.copy(et[:, :, d, r, :], acc[:, b0 + r, :].rearrange("p (t s) -> p t s", t=4)))
                for pp in range(4):
                    rows = slice(32 * pp, 32 * pp + 32)
                    ins = act.copy(hbd[rows, :, d, rows], acc[rows, b0 + 2, 0:P].rearrange("p (t c) -> p t c", t=4))
                ins.then_inc(sem("et_copied"), 1)
            for p in range(PAIRS):
                act.wait_ge(sem("end_full"), p + 1)
                if p == 0:
                    act.wait_ge(sem("xs_zero"), 1)
                act.copy(xs[:, 1:NCH, :, p], acc[:, 6 + p % 2, 0:2 * NCH].rearrange("p (r m) -> p m r", r=2)[:, 0:NCH - 1, :])\
                   .then_inc(sem("end_copied"), 1)
            for s in range(8):
                evacuate("at_q", s // 2, s % 2, q2[:, s, :])
            for s in range(2):
                act.sem_inc(sem(f"gate_stored{s}"), 16)

            def gate_chunk(seg, i, j, c, first, s, bank):
                c0, w = CH2[c]
                act.wait_ge(sem(f"gate_stored{s}"), i * 48 + (first * 16 + 16))
                acc_wait(act, seg, i, j, c)
                act.activation(gstage[:, s, 0:w], acc[:, bank, 0:w], ACT.Sigmoid).then_inc(acc_free[j], 1)
                act.wait_ge(acc_free[j], chunk_no(seg, i, c) + 1)
                slab = i * 2 + (j if seg is SEG["at_g"] else j + 2 * GATES_A)
                act.dma_start(t["gates_kept"][bass.ds(slab, 1), :, c0:c0 + w].rearrange("a p n -> p a n"),
                              gstage[:, s:s + 1, 0:w]).then_inc(sem(f"gate_stored{s}"), 16)

            with act.Fori(0, GATES_A) as i:
                for j in range(2):
                    for c in range(3):
                        gate_chunk(SEG["at_g"], i, j, c, (3 * j + c) // 2, (3 * j + c) % 2, 3 * j + c)
            for ct in range(4):
                act.wait_ge(sem("y_out"), 4 * SC)
                act.activation(u2[:, ct, :], u2[:, ct, :], ACT.Gelu_apprx_tanh).then_inc(sem("y_gelu"), 1)
            for s in range(4):
                evacuate("at_kv", s // 2, s % 2, k2[:, s, :] if s < 2 else v2[:, s - 2, :])
                if s == 1:
                    for j in range(2):
                        act.wait_ge(acc_free[j], chunk_no(SEG["at_kv"], 0, 2) + 1)
                    for lo, hi in ((0, 64), (64, 0)):
                        act.dma_start(ks2[lo:lo + 64, :, :], k2[hi:hi + 64, :, :]).then_inc(sem("ks_swapped"), 16)
            for e in range(4):
                aux_wait(act, f"v2_{e}")
                aux_release(act.copy(vt2[:, 2 * e:2 * e + 2, :], aux(f"v2_{e}").rearrange("p (n c) -> p n c", n=2)), f"v2_{e}")
            aux_wait(act, "v2_m")
            aux_release(act.copy(vm2[0:META, :], aux("v2_m")[0:META, 0:256]), "v2_m")

            def exps(u):
                hp, cols, nq, kw, _ = unit(u)
                b = u % 2
                act.wait_ge(sem("at_max"), u + 1)
                for hd in range(2):
                    own.mark(act.activation(sc[0:nq, b, hd, 0:kw], sc[0:nq, b, hd, 0:kw], ACT.Exp,
                                            bias=st[0:nq, b, 0, hd:hd + 1], accum_out=st[0:nq, b, 1, hd:hd + 1]))
                    ins = act.activation(st[0:nq, b, 2, hd:hd + 1], param("sinks")[0:nq, 2 * hp + hd:2 * hp + hd + 1], ACT.Exp,
                                         bias=st[0:nq, b, 0, hd:hd + 1])
                ins.then_inc(sem("at_exp"), 1)

            def copies(u):
                hp, cols, nq, kw, _ = unit(u)
                b = u % 2
                act.wait_ge(sem("at_pt"), u + 1)
                if u >= 2:
                    act.wait_ge(sem("at_o"), u - 1)
                ins = act.copy(pt[0:META, b, :, 0:nq], acc[0:META, 4:6, 0:nq])
                if kw > META:
                    own.mark(ins)
                    a = 384 - (kw - META)
                    ins = act.copy(pt[:, b, :, a:384], acc[:, 4:6, a:384])
                ins.then_inc(sem("at_ptc"), 1)

            for u in range(len(UNITS) + 1):
                for f, k in gates_of(u):
                    if k == KD - 1:
                        seg, i, j, c = at_chunk(f)
                        gate_chunk(seg, i, j, c, 3 * GATES_A + (3 * j + c) // 2, f % 2, 6 + f % 2)
                if u < len(UNITS):
                    exps(u)
                if u:
                    copies(u - 1)
            act.wait_ge(sem("at_oc"), len(UNITS))
            for ct in range(4):
                act.copy(y_hi[:, ct, :], u2[:, ct, :]).then_inc(sem("y_hi_full"), 1)
            for s in range(2):
                act.wait_ge(sem(f"gate_stored{s}"), 16 * (24 + 1))

            def load_gates(m, b):
                for r in range(2):
                    act.dma_start(gld[:, b, r:r + 1, :], t["gates_kept"][bass.ds(m + 8 * r, 1)].rearrange("a p n -> p a n"))\
                       .then_inc(sem(f"gates_full{b}"), 16)

            def glu(m, again, b):
                for c, (c0, w) in enumerate(CH2):
                    acc_wait(act, SEG["glu"], m, 1, c)
                    act.wait_ge(sem("glu_done"), m + 1)
                    act.activation(gtmp[:, c, 0:w], acc[:, 3 + c, 0:w], ACT.Sigmoid).then_inc(acc_free[1], 1)
                if again:
                    act.wait_ge(sem("glu_done"), m + 2)
                    load_gates(m + 2, b)

            for b in range(2):
                load_gates(b, b)
            with act.Fori(0, 3) as ii:
                for b in range(2):
                    glu(ii * 2 + b, True, b)
            for b in range(2):
                glu(6 + b, False, b)
            act.wait_ge(sem("glu_done"), 9)
            act.dma_start(x[:, :, :], t["x_kept"]).then_inc(sem("x_again"), 16)

        def dve_mix2(dve, own):
            def tt(dst, a, b, op):
                own.link(dve.tensor_tensor(dst, a, b, op))

            def ts(dst, a, s1, s2, op0, op1):
                own.link(dve.tensor_scalar(dst, a, s1, s2, op0, op1))

            def stt(dst, a, s, b, op0, op1):
                own.link(dve.scalar_tensor_tensor(dst, a, s, b, op0, op1))

            R, a_re, a_im = row, param("a_re"), param("a_im")
            dve.wait_ge(sem("ssm_step"), 1)
            tt(R("real"), a_re, R("step"), ALU.mult)
            tt(R("angle"), a_im, R("step"), ALU.mult)
            dve.sem_inc(sem("ssm_angle"), 1)
            ts(R("turns"), R("angle"), INV_2PI, ROUND, ALU.mult, ALU.add)
            ts(R("turns"), R("turns"), ROUND, None, ALU.subtract, ALU.bypass)
            stt(R("rest"), R("turns"), -PI_A, R("angle"), ALU.mult, ALU.add)
            stt(R("rest"), R("turns"), -PI_B, R("rest"), ALU.mult, ALU.add)
            stt(R("rest"), R("turns"), -PI_C, R("rest"), ALU.mult, ALU.add)
            ts(R("rest"), R("rest"), PI_MAX, -PI_MAX, ALU.min, ALU.max)
            stt(R("rest_c"), R("rest"), -1.0, R("rest"), ALU.mult, ALU.max)
            ts(R("rest_c"), R("rest_c"), -1.0, math.pi / 2, ALU.mult, ALU.add)
            dve.sem_inc(sem("ssm_rest"), 1)
            tt(R("den"), a_re, a_re, ALU.mult)
            tt(R("part"), a_im, a_im, ALU.mult)
            tt(R("den"), R("den"), R("part"), ALU.add)
            own.link(dve.reciprocal(R("den"), R("den")))
            dve.wait_ge(sem("ssm_trig"), 1)
            tt(R("l_re"), R("mag"), R("cos"), ALU.mult)
            tt(R("l_im"), R("mag"), R("sin"), ALU.mult)
            ts(R("rest"), R("l_re"), 1.0, None, ALU.subtract, ALU.bypass)
            for dst, first, second_, op in (("c_re", a_re, a_im, ALU.add), ("c_im", None, None, ALU.subtract)):
                if first is not None:
                    tt(R(dst), R("rest"), a_re, ALU.mult)
                    tt(R("part"), R("l_im"), a_im, ALU.mult)
                else:
                    tt(R(dst), R("l_im"), a_re, ALU.mult)
                    tt(R("part"), R("rest"), a_im, ALU.mult)
                tt(R(dst), R(dst), R("part"), op)
                tt(R(dst), R(dst), R("den"), ALU.mult)

            def cmul(dst, a, b, p):
                tt(p[0], a[0], b[0], ALU.mult)
                tt(p[1], a[1], b[1], ALU.mult)
                tt(dst[0], p[0], p[1], ALU.subtract)
                tt(p[0], a[0], b[1], ALU.mult)
                tt(p[1], a[1], b[0], ALU.mult)
                tt(dst[1], p[0], p[1], ALU.add)

            lam, parts2 = (R("l_re"), R("l_im")), (R("den"), R("part"))
            for r in range(2):
                own.link(dve.tensor_copy(power(1, r), lam[r]))
            for k in range(2, SC + 1):
                cmul([power(k, r) for r in range(2)], [power(k - 1, r) for r in range(2)], lam, parts2)
            for a in range(2):
                own.link(dve.tensor_copy(step8[:, 0, a, :], power(SC, 0)))
            own.link(dve.tensor_copy(step8[:, 1, 0, :], power(SC, 1)))
            ts(step8[:, 1, 1, :], power(SC, 1), -1.0, None, ALU.mult, ALU.bypass)

            def wide(r):
                return r.unsqueeze(2).broadcast_to([P, PAIRS, 32])

            dve.wait_ge(sem("x_stored"), 16)
            own.mark(dve.memset(hbd[:, :, :, :], 0.0))
            own.wait()
            dve.sem_inc(sem("hbd_zero"), 1)
            dve.wait_ge(sem("ssm_full"), 16)
            ts(ssm_in[:, 3, :, :], ssm_in[:, 3, :, :], -1.0, None, ALU.mult, ALU.bypass)
            dve.sem_inc(sem("ssm_c_full"), 1)
            pw = [p[:, :, :] for p in prod]
            b_in = [ssm_in[:, r, :, :] for r in range(2)]
            cmul([bl[0][r][:, :, :] for r in range(2)], b_in, [wide(R("c_re")), wide(R("c_im"))], pw)
            dve.sem_inc(sem("bl_full"), 1)
            for d in range(1, SC):
                if d >= 2:
                    dve.wait_ge(sem("et_full"), d - 1)
                cmul([bl[d % 2][r][:, :, :] for r in range(2)], [bl[(d - 1) % 2][r][:, :, :] for r in range(2)],
                     [wide(R("l_re")), wide(R("l_im"))], pw)
                dve.sem_inc(sem("bl_full"), 1)
            own.link(dve.memset(xs[:, 0:1, :, :], 0.0))
            dve.sem_inc(sem("xs_zero"), 1)
            dve.wait_ge(sem("end_copied"), PAIRS)
            per = 4
            with own.loop((NCH - 2) // per, 4 * per) as i:
                for k in range(per):
                    last = xs[:, bass.ds(i * per + (k + 1), 1), :, :]
                    now = xs[:, bass.ds(i * per + (k + 2), 1), :, :]
                    own.link(dve.tensor_tensor(quad[:, :, :, :], last.broadcast_to([P, 2, 2, PAIRS]), step8, ALU.mult))
                    own.link(dve.tensor_tensor(now, now, quad[:, 0:1, :, :], ALU.add))
                    for r in range(2):
                        ins = dve.tensor_tensor(now[:, :, r, :], now[:, :, r, :], quad[:, 1:2, 1 - r, :], ALU.add)
                        own.mark(ins)
                    own.wait()
            dve.sem_inc(sem("states_full"), 1)

            def c_power(n):
                if n >= 2:
                    dve.wait_ge(sem("y_full"), n - 1)
                g, m, k = bl[n % 2], [wide(power(SC - n, r)) for r in range(2)], [ssm_in[:, 2 + r, :, :] for r in range(2)]
                tt(pw[0], k[0], m[0], ALU.mult)
                tt(pw[1], k[1], m[1], ALU.mult)
                tt(g[0][:, :, :], pw[0], pw[1], ALU.add)
                tt(pw[0], k[1], m[0], ALU.mult)
                tt(pw[1], k[0], m[1], ALU.mult)
                tt(g[1][:, :, :], pw[0], pw[1], ALU.subtract)
                dve.sem_inc(sem("gl_full"), 1)

            c_power(0)
            for n in range(SC):
                if n + 1 < SC:
                    c_power(n + 1)
                dve.wait_ge(sem("y_full"), n + 1)
                s = SC - 1 - n
                for ct in range(4):
                    dst = u2s[:, ct, s, :]
                    dve.scalar_tensor_tensor(dst, dst, param("ssm_d")[:, ct:ct + 1],
                                             acc[:, 2 * (n % 4) + ct // 2, (ct % 2) * NCH:(ct % 2 + 1) * NCH],
                                             ALU.mult, ALU.add).then_inc(sem("y_out"), 1)
            neg_sinks = small[:, 20, :]
            ts(neg_sinks, param("sinks"), -1.0, None, ALU.mult, ALU.bypass)

            def mask_max(u):
                hp, cols, nq, kw, mask_ = unit(u)
                b = u % 2
                dve.wait_ge(sem("at_s"), u + 1)
                if u >= 2:
                    dve.wait_ge(sem("at_pt"), u - 1)
                s_ = sc[0:nq, b, :, 0:kw]
                dve.scalar_tensor_tensor(s_, acc[0:nq, 2 * b:2 * b + 2, 0:kw], 0.125, mask_.unsqueeze(1).broadcast_to([nq, 2, kw]),
                                         ALU.mult, ALU.add).then_inc(sem("at_masked"), 1)
                dve.wait_ge(sem("at_masked"), u + 1)
                own.link(dve.tensor_reduce(st[0:nq, b, 0, :], s_, AX_X, ALU.max))
                dve.scalar_tensor_tensor(st[0:nq, b, 0, :], st[0:nq, b, 0, :], -1.0, neg_sinks[0:nq, 2 * hp:2 * hp + 2],
                                         ALU.mult, ALU.min).then_inc(sem("at_max"), 1)

            def probabilities(u):
                hp, cols, nq, kw, _ = unit(u)
                b = u % 2
                dve.wait_ge(sem("at_exp"), u + 1)
                tt(st[0:nq, b, 1, :], st[0:nq, b, 1, :], st[0:nq, b, 2, :], ALU.add)
                own.link(dve.reciprocal(st[0:nq, b, 3, :], st[0:nq, b, 1, :]))
                for hd in range(2):
                    ins = dve.tensor_scalar(sc[0:nq, b, hd, 0:kw], sc[0:nq, b, hd, 0:kw], st[0:nq, b, 3, hd:hd + 1], None, ALU.mult)
                    if hd == 0:
                        own.mark(ins)
                ins.then_inc(sem("at_p"), 1)

            def outputs(u):
                hp, cols, nq, kw, _ = unit(u)
                dve.wait_ge(sem("at_o"), u + 1)
                dve.tensor_copy(q2[:, hp, cols], acc[:, at_bank(u), 384:384 + nq]).then_inc(sem("at_oc"), 1)

            for u in range(len(UNITS) + 2):
                if u < len(UNITS):
                    mask_max(u)
                if u >= 2:
                    outputs(u - 2)
                if u < len(UNITS):
                    probabilities(u)
            for ct in range(4):
                dve.wait_ge(sem("y_hi_full"), ct + 1)
                dve.tensor_tensor(y_lo[:, ct, :], u2[:, ct, :], y_hi[:, ct, :].bitcast(F32), ALU.subtract).then_inc(sem("y_split"), 1)
            dve.wait_ge(sem("at_oc"), len(UNITS))
            dve.sem_inc(sem("glu_done"), 1)
            with own.loop(4, 2 * 3 * 5) as ii:
                for b in range(2):
                    m = ii * 2 + b
                    dve.wait_ge(sem(f"gates_full{b}"), (ii + 1) * 32)
                    for c, (c0, w) in enumerate(CH2):
                        acc_wait(dve, SEG["glu"], m, 0, c)
                        dve.wait_ge(acc_free[1], chunk_no(SEG["glu"], m, c) + 1)
                        g = gtmp[:, c:c + 1, 0:w]
                        at_, out = q2[:, bass.ds(m, 1), c0:c0 + w], h_hi[:, bass.ds(m, 1), c0:c0 + w]
                        own.mark(dve.tensor_tensor(at_, at_, gld[:, b, 0:1, c0:c0 + w], ALU.mult))
                        dve.tensor_tensor(g, g, acc[:, c:c + 1, 0:w], ALU.mult).then_inc(acc_free[0], 1)
                        dve.wait_ge(acc_free[0], chunk_no(SEG["glu"], m, c) + 1)
                        own.link(dve.tensor_tensor(g, g, gld[:, b, 1:2, c0:c0 + w], ALU.mult))
                        own.mark(dve.tensor_tensor(out, g, at_, ALU.add))
                        own.link(dve.tensor_tensor(at_, g, at_, ALU.add))
                        own.mark(dve.tensor_tensor(h_lo[:, bass.ds(m, 1), c0:c0 + w], at_, out.bitcast(F32), ALU.subtract))
                    own.wait()
                    dve.sem_inc(sem("glu_done"), 1)
            own.link(dve.memset(ssq[:, :], 0.0))
            dve.wait_ge(sem("x_again"), 16)
            dve_residual(dve, own, SEG["out2"], 1.0, True)
            own.wait()
            dve.sem_inc(sem("ssq_ffn2"), 1)

        REAL, ALL = slice(META, L), slice(0, L)
        second = next(p for p in ("ffn1", "mix2", "ffn2") if p in parts)

        @block.scalar
        def _(act):
            for k in range(0, KD, 4):
                act.dma_start(x[:, k:k + 4, REAL], t["x"][:, k:k + 4, :]).then_inc(sem("x_full"), 16)
            act.wait_ge(sem("params_full"), 32)
            act.wait_ge(sem("x_full"), 32)
            if "mix1" in parts:
                act_squares(act, "mix1", REAL)
                act_norm(act, "mix1", CH1)
                act_mix1(act)
            if "ffn0" in parts:
                if "mix1" not in parts:
                    act_squares(act, "ffn0", REAL)
                act_norm(act, "ffn0", CH1)
                act_ffn(act, "ffn0", CH1)
                act_norm(act, "fin1", CH1, split=False)
            act.wait_ge(sem("x_ready"), 1)
            act_squares(act, second, ALL)
            if "ffn1" in parts:
                act_norm(act, "ffn1", CH2)
                act_ffn(act, "ffn1", CH2)
            if "mix2" in parts:
                act_norm(act, "mix2", CH2)
                act_mix2(act)
            if "ffn2" in parts:
                act_norm(act, "ffn2", CH2)
                act_ffn(act, "ffn2", CH2)
                act_norm(act, "fin2", CH2, split=False)
                for c in range(len(CH2)):
                    act.wait_ge(sem("out_ready"), c + 1)
                    c0, w = CH2[c]
                    lo = max(c0, META)
                    act.dma_start(t["out"][:, :, lo - META:c0 + w - META], fin[:, :, lo:c0 + w]).then_inc(sem("out_stored"), 16)
                act.wait_ge(sem("out_stored"), 16 * len(CH2))

        @block.vector
        def _(dve):
            own = Chain(dve, sem("dve_own"))
            dve.wait_ge(sem("params_full"), 32)
            if "mix1" in parts:
                dve_squares(dve, own, "mix1", REAL)
                dve_norm(dve, own, "mix1", CH1, param("mix_g"))
                dve_mix1(dve, own)
            if "ffn0" in parts:
                if "mix1" not in parts:
                    dve_squares(dve, own, "ffn0", REAL)
                dve_norm(dve, own, "ffn0", CH1, param("ffn_g"))
                dve_ffn(dve, own, "ffn0", CH1, 1.0, "fin1")
                dve_norm(dve, own, "fin1", CH1, param("final_g"), dst=x)
            else:
                dve.wait_ge(sem("x_full"), 32)
            own.link(dve.tensor_copy(x[:, :, 0:META], param("meta").rearrange("p (k m) -> p k m", k=KD)))
            dve.sem_inc(sem("x_ready"), 1)
            dve_squares(dve, own, second, ALL)
            if "ffn1" in parts:
                dve_norm(dve, own, "ffn1", CH2, param("ffn1_g"))
                dve_ffn(dve, own, "ffn1", CH2, 0.5, "mix2" if "mix2" in parts else "ffn2")
            if "mix2" in parts:
                dve_norm(dve, own, "mix2", CH2, param("mix2_g"))
                dve_mix2(dve, own)
            if "ffn2" in parts:
                dve_norm(dve, own, "ffn2", CH2, param("ffn2_g"))
                dve_ffn(dve, own, "ffn2", CH2, 0.5, "fin2")
                dve_norm(dve, own, "fin2", CH2, param("final2_g"), dst=fin)
                own.wait()
                dve.sem_inc(sem("out_ready"), len(CH2))

        @block.tensor
        def _(pe):
            pe.wait_ge(sem("params_full"), 32)
            if "mix1" in parts:
                pe_norm(pe, "mix1", CH1)
                pe_mix1(pe)
            if "ffn0" in parts:
                pe_norm(pe, "ffn0", CH1)
                pe_ffn(pe, "ffn0", CH1)
                pe_norm(pe, "fin1", CH1)
            if "ffn1" in parts:
                pe_norm(pe, "ffn1", CH2)
                pe_ffn(pe, "ffn1", CH2)
            if "mix2" in parts:
                pe_norm(pe, "mix2", CH2)
                pe_mix2(pe)
            if "ffn2" in parts:
                pe_norm(pe, "ffn2", CH2)
                pe_ffn(pe, "ffn2", CH2)
                pe_norm(pe, "fin2", CH2)


def laid_out(a):
    arrays = {"x": a["x"][0].T.reshape(KD, P, SEQ).transpose(1, 0, 2), "consts": CONSTANTS}
    arrays["params"], arrays["ssm"], arrays["gm"] = pack_params(a)
    arrays["w_in"] = slabs_of(a["w_in"][0][:, :3072])
    for name in ("w_out", "w_gate", "w_up", "ffn1_w1_2", "ffn1_w3_2", "w_in_2", "ssm_glu_a_2", "ssm_glu_b_2",
                 "w_out_2", "ffn2_w1_2", "ffn2_w3_2"):
        arrays[name] = slabs_of(a[name][0])
    for name in ("w_down", "ffn1_w2_2", "ffn2_w2_2"):
        f = 0
        for part, nf in enumerate(FQ):
            arrays[f"{name}/{part}"] = slabs_of(a[name][0][f * P:(f + nf) * P])
            f += nf
    return {k: np.ascontiguousarray(v) for k, v in arrays.items()}


def declare(nc, arrays):
    t = {}
    for name, a in arrays.items():
        ap = nc.dram_tensor("in_" + name.replace("/", "_") + "_dram", a.shape, F32, kind="ExternalInput").ap()
        if "/" in name:
            key = name.split("/")[0]
            t.setdefault(key, []).append(ap)
        else:
            t[name] = ap
    t["x_kept"] = nc.dram_tensor("x_kept", (P, KD, L), F32, kind="Internal").ap()
    t["gates_kept"] = nc.dram_tensor("gates_kept", (16, P, L), F32, kind="Internal").ap()
    t["out"] = nc.dram_tensor("out_dram", (P, KD, SEQ), F32, kind="ExternalOutput").ap()
    return t


def kernel(**inputs):
    import concourse.bacc as bacc
    from concourse.bass_utils import run_bass_kernel_spmd

    arrays = laid_out({k: np.asarray(v) for k, v in inputs.items()})
    nc = bacc.Bacc("TRN2", target_bir_lowering=False, num_devices=1)
    t = declare(nc, arrays)
    build_program(nc, t)
    feed = {"in_" + k.replace("/", "_") + "_dram": v for k, v in arrays.items()}
    got = run_bass_kernel_spmd(nc, [feed], core_ids=[0]).results[0]["out_dram"]
    return np.ascontiguousarray(got.transpose(1, 0, 2).reshape(D, SEQ).T)[None]
```

```python
import math
from contextlib import ExitStack, contextmanager

import numpy as np

import concourse.bass as bass
from concourse import mybir

F32 = mybir.dt.float32
F32R = mybir.dt.float32r
I32 = mybir.dt.int32
ALU = mybir.AluOpType
ACT = mybir.ActivationFunctionType
AX_X = mybir.AxisListType.X

P = 128
D = 1024
KD = D // P
SEQ = 1024
NBLK = SEQ // P
META = 16
L = META + SEQ
EPS = 1e-6
NEG = -1e30

HEADS = 4
TAPS = 31
DTAPS = 4
D_FF = 2816
FT = D_FF // P
FQ = [6, 6, 5, 5]
FMAX = max(FQ)
assert sum(FQ) == FT

PAIRS = 16
SC = 8
NCH = L // SC
GATES_A = 3

CH1 = [(META, 512), (META + 512, 512)]
CH2 = [(0, 348), (348, 346), (694, 346)]

CONST = {}


def _constants():
    j = np.arange(P)[:, None]
    i = np.arange(P)[None, :]
    parts = [("ident", np.eye(P)), ("ones", np.ones((P, P))), ("upper", j <= i), ("lower", j > i),
             ("negmask", np.where(i >= j, 0.0, NEG)), ("strict", i > j)]
    b = 1
    while b < P:
        same = (i // (2 * b)) == (j // (2 * b))
        parts.append((f"off{b}", same & (i % (2 * b) >= b) & (j % (2 * b) < b)))
        b *= 2
    prev = np.where(i > j, 0.0, NEG)
    cur = np.where(i <= j, 0.0, NEG)
    meta = np.zeros((P, META))
    parts.append(("band", np.concatenate([meta, prev, cur], 1)))
    parts.append(("band0", np.concatenate([meta, cur], 1)))
    parts.append(("eps", np.full((P, 1), EPS)))
    parts.append(("mean", np.full((P, P), 1.0 / D)))
    parts.append(("mean256", np.full((P, P), 1.0 / 256)))
    parts.append(("mean128", np.full((P, P), 1.0 / 128)))
    at = 0
    for name, a in parts:
        CONST[name] = (at, a.shape[1])
        at += a.shape[1]
    return np.concatenate([np.asarray(a, np.float32) for _, a in parts], 1).astype(np.float32)


CONSTANTS = _constants()


class Chain:

    def __init__(self, eng, sem):
        self.eng, self.sem, self.base, self.k, self.i, self.per = eng, sem, 0, 0, None, 0

    def mark(self, ins):
        self.k += 1
        ins.then_inc(self.sem, 1)

    def count(self):
        n = self.base + self.k
        return n if self.i is None else self.i * self.per + n

    def wait(self, back=0):
        self.eng.wait_ge(self.sem, self.count() - back)

    def link(self, ins):
        self.mark(ins)
        self.wait()

    @contextmanager
    def loop(self, count, per):
        self.base, self.k = self.base + self.k, 0
        with self.eng.Fori(0, count) as i:
            self.i, self.per = i, per
            yield i
        assert self.k == per, (self.k, per)
        self.base, self.k, self.i = self.base + count * per, 0, None


def slabs_of(w, parts=None):
    k, n = w.shape
    return w.reshape(k // P, P, n // P, P).transpose(2, 1, 0, 3).reshape(n // P, P, k)


PARTS = ("mix1", "ffn0", "ffn1", "mix2", "ffn2")


class Segment:

    def __init__(self, n0, q0, pairs, kt, chunks, src):
        self.n0, self.q0, self.pairs, self.kt, self.chunks, self.src = n0, q0, pairs, kt, chunks, src


def slab_plan(t, parts):
    segs, n, q = {}, 0, 0

    def add(name, pairs, kt, chunks, src):
        nonlocal n, q
        segs[name] = Segment(n, q, pairs, kt, chunks, src)
        n += 2 * pairs
        q += pairs * len(chunks)

    def run(w, first):
        return lambda i, j: w[bass.ds(i * 2 + (first + j), 1)]

    def pair(wa, wb, first=0):
        w = (wa, wb)
        return lambda i, j: w[j][bass.ds(i + first, 1)]

    def ffn(name, wg, wu, wd, chunks):
        f = 0
        for part, nf in enumerate(FQ):
            add(f"{name}_up{part}", nf, KD, chunks, pair(wg, wu, f))
            add(f"{name}_down{part}", KD // 2, nf, chunks, run(wd[part], 0))
            f += nf

    if "mix1" in parts:
        add("gm", 2, KD, CH1, run(t["w_in"], 0))
        add("cv", 2, KD, CH1, run(t["w_in"], 4))
        add("dn_kv", 4, KD, CH1, run(t["w_in"], 12))
        add("dn_q", 2, KD, CH1, run(t["w_in"], 8))
        add("dn_g", 2, KD, CH1, run(t["w_in"], 20))
        add("out1", 4, KD, CH1, run(t["w_out"], 0))
    if "ffn0" in parts:
        ffn("ffn0", t["w_gate"], t["w_up"], t["w_down"], CH1)
    if "ffn1" in parts:
        ffn("ffn1", t["ffn1_w1_2"], t["ffn1_w3_2"], t["ffn1_w2_2"], CH2)
    if "mix2" in parts:
        add("at_u", 2, KD, CH2, run(t["w_in_2"], 12))
        add("at_q", 4, KD, CH2, run(t["w_in_2"], 0))
        add("at_g", GATES_A, KD, CH2, run(t["w_in_2"], 16))
        add("at_kv", 2, KD, CH2, run(t["w_in_2"], 8))
        add("at_h", 8 - GATES_A, KD, CH2, run(t["w_in_2"], 16 + 2 * GATES_A))
        add("glu", 8, KD // 2, CH2, pair(t["ssm_glu_b_2"], t["ssm_glu_a_2"]))
        add("out2", 4, KD, CH2, run(t["w_out_2"], 0))
    if "ffn2" in parts:
        ffn("ffn2", t["ffn2_w1_2"], t["ffn2_w3_2"], t["ffn2_w2_2"], CH2)
    return segs


PARAM = {}


def pack_params(a):
    def cols(v):
        return np.ascontiguousarray(v.reshape(-1, P).T)

    def rep(v):
        return np.broadcast_to(v.reshape(1, -1), (P, v.size))

    def states(v):
        return v.reshape(PAIRS, P).T

    def blocks(v):
        out = np.zeros((2, 64, PAIRS, 2, 16), v.dtype)
        w = v.reshape(PAIRS, 2, 64, 16)
        for g in range(2):
            out[g, :, :, g, :] = w[:, g].transpose(1, 0, 2)
        return out.reshape(P, -1)

    parts = [
        ("mix_g", cols(a["mix_norm_g"][0])), ("ffn_g", cols(a["ffn_norm_g"][0])), ("final_g", cols(a["final_norm_g"])),
        ("ffn1_g", cols(a["ffn1_norm_2"][0])), ("mix2_g", cols(a["mix_norm_2"][0])),
        ("ffn2_g", cols(a["ffn2_norm_2"][0])), ("final2_g", cols(a["final_norm_2"])),
        ("cv_b", cols(a["cv_dw_b"][0])), ("cvln_g", cols(a["cv_ln_g"][0])), ("cvln_b", cols(a["cv_ln_b"][0])),
        ("cv_w", a["cv_dw_w"][0].T.reshape(2, P, TAPS).transpose(1, 0, 2).reshape(P, -1)),
        ("dn_w", a["dn_conv_w"][0].T.reshape(12, P, DTAPS).transpose(1, 0, 2).reshape(P, -1)),
        ("dn_norm", cols(a["dn_norm_g"][0])),
        ("a_log", rep(a["dn_a_log"][0])), ("dt_bias", rep(a["dn_dt_bias"][0])),
        ("sinks", rep(a["attn_sinks_2"][0])),
        ("a_re", states(a["ssm_a_re_2"][0])), ("a_im", states(a["ssm_a_im_2"][0])),
        ("log_step", states(np.repeat(a["ssm_log_step_2"][0], 64))), ("ssm_d", cols(a["ssm_d_2"][0])),
        ("meta", a["meta_tokens_2"].T.reshape(KD, P, META).transpose(1, 0, 2).reshape(P, -1)),
        ("w_ba", a["w_in"][0][:, 3072:].reshape(KD, P, 8).transpose(1, 0, 2).reshape(P, -1)),
    ]
    at = 0
    for name, v in parts:
        PARAM[name] = (at, v.shape[1])
        at += v.shape[1]
    ssm = [blocks(a["ssm_b_re_2"][0]), blocks(a["ssm_b_im_2"][0]),
           blocks(a["ssm_c_re_2"][0].transpose(0, 2, 1)), blocks(a["ssm_c_im_2"][0].transpose(0, 2, 1))]
    gm = [rep(a["gm_ln_g"][0]), rep(a["gm_ln_b"][0]), rep(a["gm_bs"][0]),
          a["gm_ws"][0].transpose(2, 0, 1).reshape(P, -1)]
    return np.concatenate([v for _, v in parts], 1), np.concatenate(ssm, 1), np.concatenate(gm, 1)


def build_program(nc, t, parts=PARTS):
    with ExitStack() as ctx:
        base = 16512

        def place(name, offset, shape, dtype=F32):
            return nc.alloc_sbuf_tensor_at(name, shape, dtype, offset=base + offset)

        sems = {}

        def sem(name):
            if name not in sems:
                sems[name] = ctx.enter_context(nc.semaphore(name))
            return sems[name]

        def two(name):
            return [sem(name + "0"), sem(name + "1")]

        col = L * 4
        h_hi = place("h_hi", 0, [P, KD, L], F32R)
        h_lo = place("h_lo", 8 * col, [P, KD, L], F32R)
        w_raw = place("w_raw", 66560, [P, 2, KD * P])
        w_hi = place("w_hi", 74752, [P, 2, KD * P], F32R)
        w_lo = place("w_lo", 82944, [P, 2, KD * P], F32R)
        n_const, n_param = CONSTANTS.shape[1], t["params"].shape[1]
        consts = place("consts", 91136, [P, n_const])
        at = 91136 + 4 * n_const
        at += -at % 32
        params = place("params", at, [P, n_param])
        at += 4 * n_param
        at += -at % 32
        ba_hi = place("ba_hi", at, [P, KD, 8], F32R)
        ba_lo = place("ba_lo", at + 256, [P, KD, 8], F32R)
        small = place("small", at + 512, [P, 32, 16])
        W = 91136 + 14336
        assert at + 512 + 32 * 64 <= W

        def const(name):
            a, n = CONST[name]
            return consts[:, a:a + n]

        def param(name):
            a, n = PARAM[name]
            return params[:, a:a + n]

        x = place("x", W, [P, KD, L])
        ff_hi = place("ff_hi", W + 8 * col, [P, FMAX, L], F32R)
        ff_lo = place("ff_lo", W + 14 * col, [P, FMAX, L], F32R)
        tmp = place("tmp", W + 20 * col, [P, 4, 512])
        ssq = place("ssq", W + 20 * col + 8192, [P, L])
        rs = place("rs", W + 21 * col + 8192, [P, L])
        sq = place("sq", W + 22 * col + 8192, [P, 512])
        sqx = place("sqx", W + 8 * col, [P, 2, L])
        fin = place("fin", W + 8 * col, [P, KD, L])

        kT = place("kT", W, [P, HEADS, SEQ])
        qT = place("qT", W + 16384, [P, HEADS, SEQ])
        vtok = place("vtok", W + 32768, [P, NBLK, HEADS, P])
        gate = place("gate", W + 49152, [P, HEADS, SEQ])
        cv_a = place("cv_a", W + 16128, [P, 2, SEQ])
        cv_g = place("cv_g", W + 55296, [P, 2, SEQ])
        cv_y = place("cv_y", W + 32768 - 8448, [P, 2, TAPS - 1 + SEQ])
        gm_u = place("gm_u", W + 65536, [P, 2, SEQ])
        gm_v = place("gm_v", W + 73728, [P, 2, SEQ])
        gm_t = place("gm_t", W + 81920, [P, NBLK, 256])
        gm_par = place("gm_par", W + 49152, [P, 768 + 256 + 512])
        cv_acc = place("cv_acc", W + 81920, [P, 2, SEQ])
        pre = place("pre", W + 90112, [P, 2, DTAPS - 1 + SEQ + 1])
        cvo = place("cvo", W + 98336, [P, 2, SEQ])
        dsq = place("dsq", W + 73728, [P, SEQ])
        drs = place("drs", W + 77824, [P, SEQ])
        vf = place("vf", W + 57344, [P, SEQ])
        lgt = place("lgt", W + 98336, [P, SEQ])
        cv_sq = place("cv_sq", W + 90112, [P, 2, SEQ])

        y_all = place("y_all", 4 * col, [P, NBLK, HEADS, P])
        a_all = place("a_all", 12 * col, [P, NBLK, HEADS, P])
        lane = [[place(f"lane{v}_{k}", W + 65536 + (6 * v + k) * 2048, [P, HEADS, P]) for k in range(6)]
                for v in range(2)]
        la_b, dec, e_row, b_t, off_t, x_inv = zip(*lane)
        g1 = la_b
        kd, r_u, u_sc = [place(n, W + 90112 + k * 2048, [P, HEADS, P]) for k, n in enumerate(("kd", "r_u", "u_sc"))]
        state = place("state", W + 96256, [P, 2, HEADS, P])
        osq = place("osq", W + 65536, [P, 2, SEQ])
        odiag = [place(f"odiag{v}", W + a, [P, NBLK, P]) for v, a in enumerate((73728, 86016))]
        oy = place("oy", W + 77824, [P, 2, SEQ])

        u2 = place("u2", W, [P, 4, L])
        q2 = place("q2", W + 4 * col, [P, 8, L])
        k2 = place("k2", W + 12 * col, [P, 2, L])
        ks2 = place("ks2", W + 14 * col, [P, 2, L])
        vt2 = place("vt2", W + 66560, [P, NBLK, 256])
        vm2 = place("vm2", W + 66560 + 8192, [P, 256])
        v2 = place("v2", W + 83328, [P, 2, L])
        sc = place("sc", W + 91648, [P, 2, 2, META + 256])
        pt = place("pt", W + 96000, [P, 2, 2, 384])
        st = place("st", W + 102144, [P, 2, 5, 2])
        et = place("et", W + 4 * col, [P, 4, SC, 2, P])
        hbd = place("hbd", W + 12 * col, [P, 4, SC, P])
        xs = place("xs", W + 16 * col, [P, NCH + 1, 2, PAIRS])
        bl = [[place(f"bl{v}{r}", W + 83328 + (2 * v + r) * 2048, [P, PAIRS, 32]) for r in range(2)] for v in range(2)]
        ssm_in = place("ssm_in", W + 91520, [P, 4, PAIRS, 32])
        prod = [place(f"prod{r}", W + 99712 + r * 2048, [P, PAIRS, 32]) for r in range(2)]
        quad = place("quad", W + 103808, [P, 2, 2, PAIRS])
        gstage = place("gstage", W + 104192, [P, 2, 352])
        y_hi = place("y_hi", W + 12 * col, [P, 4, L], F32R)
        y_lo = place("y_lo", W + 16 * col, [P, 4, L], F32R)
        gld = place("gld", W + 83328, [P, 2, 2, L])
        gtmp = place("gtmp", W + 83328 + 4 * col, [P, 3, 512])

        acc = ctx.enter_context(nc.psum_tensor("acc", [P, 8, 512], F32))

        SEG = slab_plan(t, parts)
        split_done = sem("split_done")
        raw_full = two("raw_full")
        acc_full, acc_free = two("acc_full"), two("acc_free")
        aux_full, aux_free = two("aux_full"), two("aux_free")

        EVENT = {}

        def event(name):
            EVENT[name] = (len(EVENT) % 2, len(EVENT) // 2)

        if "mix1" in parts:
            for name in ["logits_0", "logits_1", "logits", "decays"] + [f"gm_t{e}" for e in range(4)] + [f"gm_s{e}" for e in range(4)]:
                event(name)
            for tile in range(12):
                for c in range(2):
                    event(f"dn{tile}_{c}")
            for name in ("cv_mean0", "cv_mean1", "cv_var0", "cv_var1"):
                event(name)
            for h in range(HEADS):
                event(f"on{h}")
        for name in ("v2_0", "v2_1", "v2_2", "v2_3", "v2_m"):
            event(name)

        def aux(name):
            return acc[:, 6 + EVENT[name][0], :]

        def aux_wait(eng, name):
            b, turn = EVENT[name]
            eng.wait_ge(aux_full[b], turn + 1)

        def aux_take(eng, name):
            b, turn = EVENT[name]
            if turn:
                eng.wait_ge(aux_free[b], turn)

        def aux_done(ins, name):
            ins.then_inc(aux_full[EVENT[name][0]], 1)

        def aux_release(ins, name):
            ins.then_inc(aux_free[EVENT[name][0]], 1)

        def chunk_no(seg, i, c):
            return i * len(seg.chunks) + (seg.q0 + c)

        def acc_wait(eng, seg, i, j, c):
            eng.wait_ge(acc_full[j], chunk_no(seg, i, c) + 1)

        ones, ident = const("ones"), const("ident")
        block = ctx.enter_context(nc.Block())

        @block.sync
        def _(sp):
            sp.dma_start(consts[:, :], t["consts"]).then_inc(sem("params_full"), 16)
            sp.dma_start(params[:, :], t["params"]).then_inc(sem("params_full"), 16)
            for seg in SEG.values():
                width = seg.kt * P

                def load(i, j, seg=seg, width=width):
                    sp.dma_start(w_raw[:, j:j + 1, 0:width], seg.src(i, j).rearrange("a p n -> p a n")).then_inc(raw_full[j], 16)

                if seg.n0 == 0:
                    for j in range(2):
                        load(0, j)
                with sp.Fori(1 if seg.n0 == 0 else 0, seg.pairs) as i:
                    for j in range(2):
                        sp.wait_ge(split_done, i * 2 + (seg.n0 + j - 1))
                        load(i, j)

        NORM_OF = {"gm": "mix1", "ffn0_up0": "ffn0", "ffn1_up0": "ffn1", "at_u": "mix2", "ffn2_up0": "ffn2"}
        POOL_LO = (0, 1, 3, 4, 6, 7)
        CHUNKS_BEFORE, n_chunks = {}, 0
        for seg_name, norm_name in NORM_OF.items():
            if seg_name in SEG:
                CHUNKS_BEFORE[norm_name] = n_chunks
                n_chunks += len(SEG[seg_name].chunks)

        def h_ready(eng, name, c):
            eng.wait_ge(sem("h_written"), CHUNKS_BEFORE[name] + c + 1)
            eng.wait_ge(sem("lo_written"), (CHUNKS_BEFORE[name] + c + 1) * len(POOL_LO))

        @block.gpsimd
        def _(pool):
            own = Chain(pool, sem("pool_own"))
            pool.wait_ge(sem("params_full"), 32)
            for name, seg in SEG.items():
                width, n = seg.kt * P, len(seg.chunks)

                def split(i, j, seg=seg, width=width, n=n):
                    pool.wait_ge(raw_full[j], (i + seg.n0 // 2 + 1) * 16)
                    raw, hi, lo = w_raw[:, j, 0:width], w_hi[:, j, 0:width], w_lo[:, j, 0:width]
                    if not (seg.n0 == 0 and isinstance(i, int) and i == 0):
                        pool.wait_ge(acc_full[j], i * n + seg.q0)
                    blocks = "p (k n) -> p k n"
                    own.link(pool.tensor_tensor(hi.rearrange(blocks, n=P), raw.rearrange(blocks, n=P),
                                                ones.unsqueeze(1).broadcast_to([P, seg.kt, P]), ALU.mult))
                    pool.tensor_tensor(lo, raw, hi.bitcast(F32), ALU.subtract).then_inc(split_done, 1)

                if name not in NORM_OF and name != "out1":
                    with own.loop(seg.pairs, 2) as i:
                        for j in range(2):
                            split(i, j)
                    continue
                for j in range(2):
                    split(0, j)
                if name == "out1":
                    for k in range(2):
                        pool.wait_ge(sem("mix_hi"), k + 1)
                        pool.tensor_tensor(h_lo[:, k, META:L], gm_u[:, k, :], h_hi[:, k, META:L].bitcast(F32),
                                           ALU.subtract).then_inc(sem("o_lo"), 1)
                    for hd in range(HEADS):
                        dst = oy[:, hd % 2, :]
                        pool.wait_ge(sem("o_scaled"), hd + 1)
                        pool.tensor_tensor(dst, dst, gate[:, hd, :], ALU.mult).then_inc(sem("oy_full"), 1)
                        pool.wait_ge(sem("mix_hi"), 5 + hd)
                        pool.tensor_tensor(h_lo[:, 4 + hd, META:L], dst, h_hi[:, 4 + hd, META:L].bitcast(F32),
                                           ALU.subtract).then_inc(sem("o_lo"), 1)
                for c, (c0, w) in enumerate(seg.chunks):
                    for k in POOL_LO if name in NORM_OF else ():
                        norm = NORM_OF[name]
                        pool.wait_ge(sem("hi_" + norm), c * KD + k + 1)
                        pool.tensor_tensor(h_lo[:, k, c0:c0 + w], tmp[:, k % 4, 0:w], h_hi[:, k, c0:c0 + w].bitcast(F32),
                                           ALU.subtract).then_inc(sem("lo_written"), 1)
                with own.loop(seg.pairs - 1, 2) as i:
                    for j in range(2):
                        split(i + 1, j)

        def pe_norm(pe, name, chunks):
            pe.wait_ge(sem("ssq_" + name), 1)
            for c, (c0, w) in enumerate(chunks):
                pe.matmul(acc[:, c, 0:w], const("mean"), ssq[:, c0:c0 + w], start=True, stop=True)\
                  .then_inc(sem("ms_" + name), 1)

        def pe_norm_of_squares(pe, name, chunks):
            for k in range(KD):
                pe.wait_ge(sem("sqt_" + name), k + 1)
                for c, (c0, w) in enumerate(chunks):
                    ins = pe.matmul(acc[:, c, 0:w], const("mean"), sqx[:, k % 2, c0:c0 + w],
                                    start=(k == 0), stop=(k == KD - 1), skip_group_check=True)
                    if k == KD - 1:
                        ins.then_inc(sem("ms_" + name), 1)
                if k < KD - 1:
                    ins.then_inc(sem("sqsum_" + name), 1)

        def act_norm(act, name, chunks, split=True):
            for c, (c0, w) in enumerate(chunks):
                act.wait_ge(sem("ms_" + name), c + 1)
                act.activation(rs[:, c0:c0 + w], acc[:, c, 0:w], ACT.Sqrt, bias=const("eps")).then_inc(sem("sd_" + name), 1)
            if split:
                for c, (c0, w) in enumerate(chunks):
                    for k in range(KD):
                        act.wait_ge(sem("scaled_" + name), c * KD + k + 1)
                        act.copy(h_hi[:, k, c0:c0 + w], tmp[:, k % 4, 0:w]).then_inc(sem("hi_" + name), 1)

        def dve_norm(dve, own, name, chunks, gain):
            for c, (c0, w) in enumerate(chunks):
                dve.wait_ge(sem("sd_" + name), c + 1)
                own.link(dve.reciprocal(rs[:, c0:c0 + w], rs[:, c0:c0 + w]))
                for k in range(KD + 2):
                    if k < KD:
                        g = c * KD + k
                        if g >= 4:
                            before = (k - 4) % KD
                            if before in POOL_LO:
                                dve.wait_ge(sem("lo_written"), (CHUNKS_BEFORE[name] + (g - 4) // KD) * len(POOL_LO) + POOL_LO.index(before) + 1)
                            else:
                                own.wait()
                        dve.scalar_tensor_tensor(tmp[:, k % 4, 0:w], x[:, k, c0:c0 + w], gain[:, k:k + 1],
                                                 rs[:, c0:c0 + w], ALU.mult, ALU.mult).then_inc(sem("scaled_" + name), 1)
                    if k >= 2 and k - 2 not in POOL_LO:
                        dve.wait_ge(sem("hi_" + name), c * KD + k - 1)
                        own.mark(dve.tensor_tensor(h_lo[:, k - 2, c0:c0 + w], tmp[:, (k - 2) % 4, 0:w],
                                                   h_hi[:, k - 2, c0:c0 + w].bitcast(F32), ALU.subtract))
                own.wait()
                dve.sem_inc(sem("h_written"), 1)

        def dve_norm_whole(dve, own, name, chunks, gain, dst):
            for c, (c0, w) in enumerate(chunks):
                dve.wait_ge(sem("sd_" + name), c + 1)
                own.mark(dve.reciprocal(rs[:, c0:c0 + w], rs[:, c0:c0 + w]))
            own.wait()
            for k in range(KD):
                dve.scalar_tensor_tensor(dst[:, k, META:L], x[:, k, META:L], gain[:, k:k + 1], rs[:, META:L],
                                         ALU.mult, ALU.mult).then_inc(sem("tile_" + name), 1)

        def pe_slab(pe, seg, i, j, rhs, only=None):
            n = len(seg.chunks)
            pe.wait_ge(split_done, i * 2 + (seg.n0 + j + 1))
            for c, (c0, w) in enumerate(seg.chunks):
                if only is not None and c != only:
                    continue
                if not (seg.q0 == 0 and isinstance(i, int) and i == 0):
                    pe.wait_ge(acc_free[j], i * n + (seg.q0 + c + 1 - n))
                bank = acc[:, 3 * j + c, 0:w]
                for k in range(seg.kt):
                    wh, wl = w_hi[:, j, k * P:(k + 1) * P], w_lo[:, j, k * P:(k + 1) * P]
                    rh, rl = rhs[0][:, k, c0:c0 + w], rhs[1][:, k, c0:c0 + w]
                    pe.matmul(bank, wh, rh, start=(k == 0), stop=False)
                    pe.matmul(bank, wh, rl, start=False, stop=False)
                    ins = pe.matmul(bank, wl, rh, start=False, stop=(k == seg.kt - 1))
                ins.then_inc(acc_full[j], 1)

        def pe_first_pair(pe, name, seg, beside=None):
            for c in range(len(seg.chunks)):
                h_ready(pe, name, c)
                if beside:
                    beside(c)
                for j in range(2):
                    pe_slab(pe, seg, 0, j, (h_hi, h_lo), only=c)

        def pe_ffn(pe, name, chunks):
            for part in range(len(FQ)):
                up, down = SEG[f"{name}_up{part}"], SEG[f"{name}_down{part}"]
                if part == 0:
                    pe_first_pair(pe, name, up)
                with pe.Fori(1 if part == 0 else 0, up.pairs) as i:
                    for j in range(2):
                        pe_slab(pe, up, i, j, (h_hi, h_lo))
                for c in range(len(chunks)):
                    pe.wait_ge(sem("ff_" + name), part * len(chunks) + c + 1)
                    pe_slab(pe, down, 0, 0, (ff_hi, ff_lo), only=c)
                pe_slab(pe, down, 0, 1, (ff_hi, ff_lo))
                with pe.Fori(1, down.pairs) as i:
                    for j in range(2):
                        pe_slab(pe, down, i, j, (ff_hi, ff_lo))

        def act_ffn(act, name, chunks):
            n = len(chunks)
            h_ready(act, name, n - 1)
            for part in range(len(FQ)):
                seg = SEG[f"{name}_up{part}"]
                with act.Fori(0, seg.pairs) as i:
                    for c, (c0, w) in enumerate(chunks):
                        acc_wait(act, seg, i, 0, c)
                        act.wait_ge(acc_free[1], i * n + (seg.q0 + c + 1 - n))
                        act.activation(tmp[:, c, 0:w], acc[:, c, 0:w], ACT.Silu).then_inc(acc_free[0], 1)

        def dve_ffn(dve, own, name, chunks, scale, then):
            n = len(chunks)
            for part in range(len(FQ)):
                seg = SEG[f"{name}_up{part}"]

                def hidden(i, c, seg=seg):
                    c0, w = chunks[c]
                    acc_wait(dve, seg, i, 1, c)
                    dve.wait_ge(acc_free[0], chunk_no(seg, i, c) + 1)
                    hi = ff_hi[:, bass.ds(i, 1), c0:c0 + w]
                    g, up = tmp[:, c:c + 1, 0:w], acc[:, 3 + c:4 + c, 0:w]
                    own.mark(dve.tensor_tensor(hi, g, up, ALU.mult))
                    own.wait(1)
                    dve.tensor_tensor(tmp[:, 3:4, 0:w], g, up, ALU.mult).then_inc(acc_free[1], 1)
                    dve.wait_ge(acc_free[1], chunk_no(seg, i, c) + 1)
                    own.wait()
                    own.mark(dve.tensor_tensor(ff_lo[:, bass.ds(i, 1), c0:c0 + w], tmp[:, 3:4, 0:w],
                                               hi.bitcast(F32), ALU.subtract))

                with own.loop(seg.pairs - 1, 2 * n) as i:
                    for c in range(n):
                        hidden(i, c)
                for c in range(n):
                    hidden(seg.pairs - 1, c)
                    own.wait()
                    dve.sem_inc(sem("ff_" + name), 1)
                last = part == len(FQ) - 1
                if last:
                    own.link(dve.memset(ssq[:, :], 0.0))
                dve_residual(dve, own, SEG[f"{name}_down{part}"], scale, last)
            own.wait()
            dve.sem_inc(sem("ssq_" + then), 1)

        def dve_residual(dve, own, seg, scale, squares):
            with own.loop(seg.pairs, 4 * len(seg.chunks) if squares else 0) as i:
                for j in range(2):
                    for c, (c0, w) in enumerate(seg.chunks):
                        acc_wait(dve, seg, i, j, c)
                        xt = x[:, bass.ds(i * 2 + j, 1), c0:c0 + w]
                        dve.scalar_tensor_tensor(xt, acc[:, 3 * j + c:3 * j + c + 1, 0:w], scale, xt,
                                                 ALU.mult, ALU.add).then_inc(acc_free[j], 1)
                        if squares:
                            dve.wait_ge(acc_free[j], chunk_no(seg, i, c) + 1)
                            own.link(dve.tensor_tensor(sq[:, 0:w].unsqueeze(1), xt, xt, ALU.mult))
                            own.link(dve.tensor_tensor(ssq[:, c0:c0 + w], ssq[:, c0:c0 + w], sq[:, 0:w], ALU.add))

        def act_squares(act, name, cols, ready):
            for k in range(KD):
                ready(k)
                if k >= 2:
                    act.wait_ge(sem("sqsum_" + name), k - 1)
                act.activation(sqx[:, k % 2, cols], x[:, k, cols], ACT.Square).then_inc(sem("sqt_" + name), 1)

        def flat(a, b):
            return small[:, a:b, :].rearrange("p a b -> p (a b)")

        logits, beta, z_a, z_abs, z_ln, decay = (flat(0, 4), flat(4, 6), flat(6, 8), flat(8, 10), flat(10, 12), flat(12, 14))
        g_col, k_dec, c_dec, e_col, rate = flat(14, 16), flat(16, 18), flat(18, 20), flat(20, 22), flat(22, 23)
        gm_st, gm_mv, gm_sd = flat(24, 27), flat(27, 28), flat(28, 29)
        o_sd = flat(24, 26)
        by_head = "p (n h) -> p n h"

        SLABS1 = [(seg, i, j) for seg in ("dn_kv", "dn_q", "dn_g") if "mix1" in parts
                  for i in range(SEG[seg].pairs) for j in range(2)]
        DN = [("k", h, 4 + h) for h in range(4)] + [("v", h, 8 + h) for h in range(4)] + [("q", h, h) for h in range(4)]
        KQ = [n for n, d in enumerate(DN) if d[0] != "v"]
        TAP_STEPS = 9

        def dn_dst(tile):
            kind, h, _ = DN[tile]
            return {"k": kT[:, h, :], "q": qT[:, h, :], "v": vf[:, :]}[kind]

        def blk(n):
            return slice(n * P, (n + 1) * P)

        def cc(c):
            return slice(c * 512, (c + 1) * 512)

        S_A, S_B = 6, 7

        def state_steps(it, lv):
            return [(2 * (it - 1) + lv // 3, lv % 3)] if it and lv < 6 else []

        LAST_STEPS = [(n, q) for n in (NBLK - 2, NBLK - 1) for q in range(3)]

        def pe_mix1(pe):
            h = (h_hi, h_lo)

            def logits_chunk(c):
                if c == 0:
                    pe.wait_ge(sem("ba_full"), 1)
                name = f"logits_{c}"
                aux_take(pe, name)
                out, cols = aux(name)[0:8, :], slice(META + 512 * c, META + 512 * (c + 1))
                for k in range(KD):
                    pe.matmul(out, ba_hi[:, k, :], h_hi[:, k, cols], start=(k == 0), stop=False)
                    pe.matmul(out, ba_hi[:, k, :], h_lo[:, k, cols], start=False, stop=False)
                    ins = pe.matmul(out, ba_lo[:, k, :], h_hi[:, k, cols], start=False, stop=(k == KD - 1))
                aux_done(ins, name)

            pe_first_pair(pe, "mix1", SEG["gm"], beside=logits_chunk)
            pe.wait_ge(aux_free[EVENT["logits_1"][0]], EVENT["logits_1"][1] + 1)
            aux_take(pe, "logits")
            for n in range(NBLK):
                ins = pe.transpose(aux("logits")[:, n * 8:n * 8 + 8], lgt[0:8, blk(n)], ident[0:8, 0:8])
            aux_done(ins, "logits")
            for j in range(2):
                pe_slab(pe, SEG["gm"], 1, j, h)
            pe_slab(pe, SEG["cv"], 0, 0, h)
            pe.wait_ge(sem("decay_full"), 1)
            aux_take(pe, "decays")
            for m, name in enumerate(("upper", "lower", "ones")):
                ins = pe.matmul(aux("decays")[:, 32 * m:32 * m + 32], const(name), decay, start=True, stop=True)
            aux_done(ins, "decays")
            pe.wait_ge(sem("gm_full"), 8)
            for e in range(4):
                aux_take(pe, f"gm_t{e}")
                for n in (2 * e, 2 * e + 1):
                    for ct in range(2):
                        ins = pe.transpose(aux(f"gm_t{e}")[:, (n % 2) * 256 + ct * P:(n % 2) * 256 + ct * P + P],
                                           gm_v[:, ct, blk(n)], ident)
                aux_done(ins, f"gm_t{e}")
            for i, j in ((0, 1), (1, 0), (1, 1)):
                pe_slab(pe, SEG["cv"], i, j, h)

            def gating():
                pe.wait_ge(sem("gm_normed"), 1)
                for e in range(4):
                    ct, half = e // 2, e % 2
                    aux_take(pe, f"gm_s{e}")
                    for n in range(4 * half, 4 * half + 4):
                        for hh in range(2):
                            hd = 2 * ct + hh
                            out = aux(f"gm_s{e}")[hh * 64:hh * 64 + 64, (n % 4) * P:(n % 4) * P + P]
                            pe.matmul(out, gm_t[:, n, hd * 64:hd * 64 + 64], gm_par[:, 1024 + hd * P:1024 + hd * P + P],
                                      start=True, stop=False, skip_group_check=True)
                            ins = pe.matmul(out, ones[0:1, 0:64], gm_par[0:1, 512 + hd * P:512 + hd * P + P],
                                            start=False, stop=True, skip_group_check=True)
                    aux_done(ins, f"gm_s{e}")

            def dn_event(u):
                kind, hd, _ = DN[u]
                for c in range(2):
                    name = f"dn{u}_{c}"
                    if kind == "v":
                        pe.wait_ge(sem("silu_done"), u + 1)
                        aux_take(pe, name)
                        for n in range(4):
                            ins = pe.transpose(aux(name)[:, n * P:n * P + P], vf[:, blk(4 * c + n)], ident)
                    else:
                        pe.wait_ge(sem("dsq_full"), KQ.index(u) + 1)
                        aux_take(pe, name)
                        ins = pe.matmul(aux(name), ones, dsq[:, cc(c)], start=True, stop=True)
                    aux_done(ins, name)

            for s, (seg, i, j) in enumerate(SLABS1):
                pe_slab(pe, SEG[seg], i, j, h)
                if s == 0:
                    gating()
                if 0 <= s - 2 < 12:
                    dn_event(s - 2)
            for stat, src in (("mean", cv_acc), ("var", cv_sq)):
                for c in range(2):
                    pe.wait_ge(sem("cv_" + stat + "_in"), 1 if stat == "mean" else c + 1)
                    aux_take(pe, f"cv_{stat}{c}")
                    for ct in range(2):
                        ins = pe.matmul(aux(f"cv_{stat}{c}"), const("mean256"), src[:, ct, cc(c)],
                                        start=(ct == 0), stop=(ct == 1))
                    aux_done(ins, f"cv_{stat}{c}")
            for j in range(2):
                pe.wait_ge(acc_free[j], SEG["dn_g"].q0 + 4)
            for b in range(2):
                pe.wait_ge(aux_free[b], EVENT["cv_var" + str(b)][1] + 1)
            def state_step(n, q):
                cur = n % 2
                if q == 0:
                    pe.wait_ge(sem("state_full"), n + 1)
                    if n:
                        pe.wait_ge(sem("o_copied"), n)
                    for hd in range(HEADS):
                        o = slice(hd * P, hd * P + P)
                        pe.transpose(acc[:, S_B, o], kT[:, hd, blk(n)], ident)
                        ins = pe.matmul(acc[:, S_A, o], kT[:, hd, blk(n)], state[:, cur, hd, :], start=True, stop=True)
                    ins.then_inc(sem("ks_full"), 1)
                elif q == 1:
                    pe.wait_ge(sem("xy_done0"), 7 * (n // 2 + 1))
                    pe.wait_ge(sem("xy_done1"), 7 * (n // 2 + 1))
                    pe.wait_ge(sem("r_full"), n + 1)
                    for hd in range(HEADS):
                        ins = pe.matmul(acc[:, S_A, hd * P:hd * P + P], y_all[:, n, hd, :], r_u[:, hd, :], start=True, stop=True)
                    ins.then_inc(sem("xr_full"), 1)
                else:
                    pe.wait_ge(sem("u_full"), n + 1)
                    pe.wait_ge(sem("kd_full"), n + 1)
                    for hd in range(HEADS):
                        ins = pe.matmul(acc[:, S_A, hd * P:hd * P + P], kd[:, hd, :], u_sc[:, hd, :], start=True, stop=True)
                    ins.then_inc(sem("ds_full"), 1)
                    for hd in range(HEADS):
                        o = slice(hd * P, hd * P + P)
                        pe.matmul(acc[:, S_B, o], state[:, cur, hd, :], qT[:, hd, blk(n)], start=True, stop=False)
                        ins = pe.matmul(acc[:, S_B, o], u_sc[:, hd, :], a_all[:, n, hd, :], start=False, stop=True)
                    ins.then_inc(sem("o_full"), 1)

            pe.wait_ge(sem("dscaled"), 8)
            for it in range(NBLK // 2):
                for v in range(2):
                    n = 2 * it + v
                    pe.wait_ge(sem("la_full"), n + 1)
                    if it:
                        pe.wait_ge(sem(f"xy_done{v}"), 7 * it)
                    for hd in range(HEADS):
                        o = slice(hd * P, hd * P + P)
                        pe.matmul(acc[:, 3 * v, o], la_b[v][:, hd, :], const("upper"), start=True, stop=True)
                        pe.matmul(acc[:, 3 * v + 1, o], kT[:, hd, blk(n)], kT[:, hd, blk(n)], start=True, stop=True)
                        ins = pe.matmul(acc[:, 3 * v + 2, o], kT[:, hd, blk(n)], qT[:, hd, blk(n)], start=True, stop=True)
                    ins.then_inc(sem(f"g_full{v}"), 1)
                for lv in range(7):
                    for v in range(2):
                        n = 2 * it + v
                        pe.wait_ge(sem(f"off_full{v}"), 7 * it + lv + 1)
                        if lv:
                            pe.wait_ge(sem(f"xy_done{v}"), 7 * it + lv)
                        for hd in range(HEADS):
                            o = slice(hd * P, hd * P + P)
                            if lv == 0:
                                ins = pe.transpose(acc[:, 3 * v, o], off_t[v][:, hd, :], ident)
                            else:
                                ins = pe.matmul(acc[:, 3 * v, o], off_t[v][:, hd, :], x_inv[v][:, hd, :], start=True, stop=True)
                        ins.then_inc(sem(f"g1_full{v}"), 1)
                    for v in range(2):
                        n = 2 * it + v
                        if lv == 0:
                            continue
                        pe.wait_ge(sem(f"g1_copied{v}"), 6 * it + lv)
                        for hd in range(HEADS):
                            o = slice(hd * P, hd * P + P)
                            if lv < 6:
                                pe.matmul(acc[:, 3 * v + 1, o], y_all[:, n, hd, :], g1[v][:, hd, :], start=True, stop=True)
                            ins = pe.matmul(acc[:, 3 * v + 2, o], g1[v][:, hd, :], y_all[:, n, hd, :], start=True, stop=True)
                        ins.then_inc(sem(f"xy_full{v}"), 1)
                    for n, q in state_steps(it, lv):
                        state_step(n, q)
            for n, q in LAST_STEPS:
                state_step(n, q)
            pe.wait_ge(sem("state_full"), NBLK + 1)
            for hd in range(HEADS + 1):
                if hd < HEADS:
                    pe.wait_ge(sem("osq_full"), hd + 1)
                    aux_take(pe, f"on{hd}")
                    for n in range(NBLK):
                        ins = pe.matmul(aux(f"on{hd}")[:, n:n + 1], osq[:, hd % 2, blk(n)], const("mean128")[:, 0:1],
                                        start=True, stop=True)
                    aux_done(ins, f"on{hd}")
                if hd:
                    pe.wait_ge(sem("odiag_full"), hd)
                    if hd >= 3:
                        pe.wait_ge(sem("o_scaled"), hd - 2)
                    for c in range(2):
                        ins = pe.matmul(acc[:, 2 * ((hd - 1) % 2) + c, :], ones,
                                        odiag[(hd - 1) % 2][:, 4 * c:4 * c + 4, :].rearrange("p n i -> p (n i)"), start=True, stop=True)
                    ins.then_inc(sem("orms_full"), 1)
            pe.wait_ge(sem("mixed1"), 1)
            pe.wait_ge(sem("o_lo"), HEADS + 2)
            with pe.Fori(0, SEG["out1"].pairs) as i:
                for j in range(2):
                    pe_slab(pe, SEG["out1"], i, j, h)

        def act_mix1(act):
            own = Chain(act, sem("act_own"))
            h_ready(act, "mix1", 1)
            act.dma_start(gm_par[:, :], t["gm"]).then_inc(sem("gm_par_full"), 16)
            for c in range(2):
                aux_wait(act, f"logits_{c}")
                aux_release(act.copy(lgt[0:8, cc(c)], aux(f"logits_{c}")[0:8, :]), f"logits_{c}")
            aux_wait(act, "logits")
            aux_release(act.copy(logits, aux("logits")[:, 0:64]), "logits")
            act.wait_ge(aux_free[EVENT["logits"][0]], EVENT["logits"][1] + 1)
            act.sem_inc(sem("logits_full"), 1)
            own.mark(act.activation(beta.rearrange(by_head, h=4), logits.rearrange("p (n e) -> p n e", e=8)[:, :, 0:4], ACT.Sigmoid))
            act.wait_ge(sem("z_full"), 1)
            own.link(act.activation(z_ln, z_abs, ACT.Exp, scale=-1.0))
            own.link(act.activation(z_ln, z_ln, ACT.Ln, bias=ones[:, 0:1]))
            own.link(act.activation(rate[:, 0:4], param("a_log"), ACT.Exp))
            act.sem_inc(sem("z_ln_full"), 1)
            for s in range(4):
                i, j = s // 2, s % 2
                for c in range(2):
                    acc_wait(act, SEG["gm"], i, j, c)
                    dst = (gm_u if i == 0 else gm_v)[:, j, cc(c)]
                    act.activation(dst, acc[:, 3 * j + c, :], ACT.Gelu).then_inc(acc_free[j], 1)
            for j in range(2):
                act.wait_ge(acc_free[j], chunk_no(SEG["gm"], 1, 1) + 1)
            act.sem_inc(sem("gm_full"), 8)
            for s in range(4):
                i, j = s // 2, s % 2
                if s == 1:
                    aux_wait(act, "decays")
                    sums = aux("decays")
                    own.mark(act.copy(g_col, sums[:, 0:32]))
                    own.mark(act.activation(e_col, sums[:, 0:32], ACT.Exp))
                    own.mark(act.activation(k_dec, sums[:, 32:64], ACT.Exp))
                    aux_release(act.activation(c_dec, sums[:, 64:96], ACT.Exp), "decays")
                    for e in range(4):
                        aux_wait(act, f"gm_t{e}")
                        aux_release(act.copy(gm_t[:, 2 * e:2 * e + 2, :], aux(f"gm_t{e}").rearrange("p (n c) -> p n c", n=2)), f"gm_t{e}")
                    act.wait_ge(sem("gm_var"), 1)
                    own.mark(act.activation(gm_sd[:, 0:8], gm_mv.rearrange("p (n e) -> p n e", e=2)[:, :, 1], ACT.Sqrt, bias=const("eps")))
                    own.wait()
                    act.sem_inc(sem("gm_sd_full"), 1)
                for c in range(2):
                    acc_wait(act, SEG["cv"], i, j, c)
                    if i == 0:
                        act.copy(cv_a[:, j, cc(c)], acc[:, 3 * j + c, :]).then_inc(acc_free[j], 1)
                    else:
                        act.activation(cv_g[:, j, cc(c)], acc[:, 3 * j + c, :], ACT.Sigmoid).then_inc(acc_free[j], 1)
            for s in range(16):
                seg, i, j = SLABS1[s]
                for c in range(2):
                    acc_wait(act, SEG[seg], i, j, c)
                    if s < 12:
                        if s >= 2:
                            act.wait_ge(sem("conv_done"), s - 1)
                        a = DTAPS - 1 + c * 512
                        ins = act.copy(pre[:, s % 2, a:a + 512], acc[:, 3 * j + c, :])
                    else:
                        ins = act.activation(gate[:, s - 12, cc(c)], acc[:, 3 * j + c, :], ACT.Silu)
                    ins.then_inc(acc_free[j], 1)
                if 0 <= s - 2 < 12:
                    kind, hd, _ = DN[s - 2]
                    for c in range(2):
                        name = f"dn{s - 2}_{c}"
                        aux_wait(act, name)
                        if kind == "v":
                            ins = act.copy(vtok[:, 4 * c:4 * c + 4, hd, :], aux(name).rearrange("p (n d) -> p n d", n=4))
                        else:
                            done = KQ.index(s - 2)
                            if done:
                                act.wait_ge(sem("dscaled"), done)
                            ins = act.activation(drs[:, cc(c)], aux(name), ACT.Sqrt, bias=const("eps"))
                        aux_release(ins, name)
                if 0 <= s - 1 < 12:
                    act.wait_ge(sem("conv_done"), s)
                    if s - 1 == 0:
                        act.wait_ge(sem("gm_gated"), 1)
                    act.activation(dn_dst(s - 1), cvo[:, (s - 1) % 2, :], ACT.Silu).then_inc(sem("silu_done"), 1)
                    if s - 1 in KQ:
                        act.wait_ge(sem("silu_done"), s)
                        act.activation(dsq[:, :], dn_dst(s - 1), ACT.Square).then_inc(sem("dsq_full"), 1)
            for j in range(2):
                act.wait_ge(acc_full[j], SEG["dn_g"].q0 + 4)

            def mix_high(k):
                src = gm_u[:, k, :] if k < 2 else cv_acc[:, k - 2, :]
                act.copy(h_hi[:, k, META:L], src).then_inc(sem("mix_hi"), 1)

            mix_high(0)
            mix_high(1)
            for c in range(2):
                act.wait_ge(sem("cv_centred"), 2 * c + 2)
                act.activation(cv_sq[:, :, cc(c)], cv_acc[:, :, cc(c)], ACT.Square).then_inc(sem("cv_var_in"), 1)
            for c in range(2):
                aux_wait(act, f"cv_var{c}")
                if c == 0:
                    act.wait_ge(sem("dscaled"), 8)
                aux_release(act.activation(drs[:, cc(c)], aux(f"cv_var{c}"), ACT.Sqrt, bias=const("eps")), f"cv_var{c}")
            act.wait_ge(sem("cv_normed"), 1)
            for ct in range(2):
                own.mark(act.activation(cv_acc[:, ct, :], cv_acc[:, ct, :], ACT.Silu,
                                        bias=param("cvln_b")[:, ct:ct + 1], scale=param("cvln_g")[:, ct:ct + 1]))
            own.wait()
            mix_high(2)
            mix_high(3)

            def state_step(n, q):
                if q == 0:
                    act.wait_ge(sem("ks_full"), n + 1)
                    if n:
                        act.wait_ge(sem("ds_full"), n)
                    for hd in range(HEADS):
                        ins = act.activation(kd[:, hd, :], acc[:, S_B, hd * P:hd * P + P], ACT.Copy,
                                             scale=k_dec[:, n * 4 + hd:n * 4 + hd + 1])
                    ins.then_inc(sem("kd_full"), 1)
                elif q == 2:
                    act.wait_ge(sem("o_full"), n + 1)
                    act.copy(qT[:, :, blk(n)], acc[:, S_B, :].rearrange("p (h i) -> p h i", h=4)).then_inc(sem("o_copied"), 1)

            for it in range(NBLK // 2):
                for v in range(2):
                    act.wait_ge(sem(f"dd_full{v}"), it + 1)
                    own.mark(act.activation(e_row[v][:, :, :], acc[:, 3 * v, :].rearrange("p (h i) -> p h i", h=4), ACT.Exp))
                    act.activation(dec[v][:, :, :], dec[v][:, :, :], ACT.Exp).then_inc(sem(f"dt_full{v}"), 1)
                for lv in range(7):
                    for v in range(2 if lv else 0):
                        act.wait_ge(sem(f"g1_full{v}"), 7 * it + lv + 1)
                        act.copy(g1[v][:, :, :], acc[:, 3 * v, :].rearrange("p (h i) -> p h i", h=4))\
                           .then_inc(sem(f"g1_copied{v}"), 1)
                    for n, q in state_steps(it, lv):
                        state_step(n, q)
            for n, q in LAST_STEPS:
                state_step(n, q)
            act.wait_ge(sem("o_copied"), NBLK)
            for hd in range(HEADS + 2):
                if hd < HEADS:
                    act.activation(osq[:, hd % 2, :], qT[:, hd, :], ACT.Square).then_inc(sem("osq_full"), 1)
                if 1 <= hd <= HEADS:
                    name = f"on{hd - 1}"
                    aux_wait(act, name)
                    aux_release(act.activation(o_sd[:, 8 * hd - 8:8 * hd], aux(name)[:, 0:NBLK], ACT.Sqrt, bias=const("eps")), name)
                if hd >= 2:
                    act.wait_ge(sem("oy_full"), hd - 1)
                    act.copy(h_hi[:, 2 + hd, META:L], oy[:, hd % 2, :]).then_inc(sem("mix_hi"), 1)
            act.wait_ge(sem("oy_full"), HEADS)
            for k in range(0, KD, 4):
                act.dma_start(x[:, k:k + 4, META:L], t["x"][:, k:k + 4, :]).then_inc(sem("residual_full"), 16)

        def dve_mix1(dve, own):
            own.link(dve.tensor_copy(ba_hi[:, :, :], param("w_ba").rearrange("p (k e) -> p k e", k=KD)))
            own.link(dve.tensor_tensor(ba_lo[:, :, :], param("w_ba").rearrange("p (k e) -> p k e", k=KD),
                                       ba_hi[:, :, :].bitcast(F32), ALU.subtract))
            dve.sem_inc(sem("ba_full"), 1)
            dve.wait_ge(sem("logits_full"), 1)
            z3 = z_a.rearrange(by_head, h=4)
            own.link(dve.tensor_tensor(z3, logits.rearrange("p (n e) -> p n e", e=8)[:, :, 4:8],
                                       param("dt_bias").unsqueeze(1).broadcast_to([P, NBLK, 4]), ALU.add))
            dve.scalar_tensor_tensor(z_abs, z_a, -1.0, z_a, ALU.mult, ALU.max).then_inc(sem("z_full"), 1)
            dve.wait_ge(sem("z_full"), 1)
            own.link(dve.tensor_single_scalar(z_a, z_a, 0.0, ALU.max))
            dve.wait_ge(sem("z_ln_full"), 1)
            own.link(dve.tensor_tensor(z_a, z_a, z_ln, ALU.add))
            dve.scalar_tensor_tensor(decay.rearrange(by_head, h=4), z3, -1.0, rate[:, 0:4].unsqueeze(1).broadcast_to([P, NBLK, 4]),
                                     ALU.mult, ALU.mult).then_inc(sem("decay_full"), 1)
            dve.wait_ge(sem("gm_par_full"), 16)
            ws = gm_par[:, 1024:1536].rearrange("p (h i) -> p h i", h=4)
            own.mark(dve.tensor_tensor(ws, ws, const("upper").unsqueeze(1).broadcast_to([P, 4, P]), ALU.mult))
            for n in range(NBLK):
                b, turn = EVENT[f"gm_t{n // 2}"]
                dve.wait_ge(aux_free[b], turn + 1)
                own.link(dve.bn_stats(gm_st[:, 6 * n:6 * n + 6], gm_t[:, n, :]))
                own.mark(dve.bn_aggr(gm_mv[:, 2 * n:2 * n + 2], gm_st[:, 6 * n:6 * n + 6]))
            own.wait()
            dve.sem_inc(sem("gm_var"), 1)
            dve.wait_ge(sem("gm_sd_full"), 1)
            own.link(dve.reciprocal(gm_sd[:, 0:8], gm_sd[:, 0:8]))
            for n in range(NBLK):
                own.mark(dve.tensor_scalar(gm_t[:, n, :], gm_t[:, n, :], gm_mv[:, 2 * n:2 * n + 1], gm_sd[:, n:n + 1],
                                           ALU.subtract, ALU.mult))
            own.wait()
            for k, op in ((0, ALU.mult), (1, ALU.add)):
                own.link(dve.tensor_tensor(gm_t[:, :, :], gm_t[:, :, :],
                                           gm_par[:, 256 * k:256 * k + 256].unsqueeze(1).broadcast_to([P, NBLK, 256]), op))
            dve.sem_inc(sem("gm_normed"), 1)
            own.mark(dve.memset(cv_y[:, :, 0:TAPS - 1], 0.0))
            own.mark(dve.memset(pre[:, :, 0:DTAPS - 1], 0.0))
            for j in range(2):
                dve.wait_ge(acc_free[j], chunk_no(SEG["cv"], 1, 1) + 1)
            own.link(dve.tensor_tensor(cv_y[:, :, TAPS - 1:], cv_a[:, :, :], cv_g[:, :, :], ALU.mult))
            for e in range(4):
                aux_wait(dve, f"gm_s{e}")
                ct, half = e // 2, e % 2
                dst = gm_u[:, ct, cc(half)]
                aux_release(dve.tensor_tensor(dst, dst, aux(f"gm_s{e}"), ALU.mult), f"gm_s{e}")
            for e in (2, 3):
                b, turn = EVENT[f"gm_s{e}"]
                dve.wait_ge(aux_free[b], turn + 1)
            dve.sem_inc(sem("gm_gated"), 1)
            taps = [(ct, i) for i in range(TAPS) for ct in range(2)]
            per = -(-len(taps) // TAP_STEPS)
            for s in range(14):
                if s < 12:
                    seg, i, j = SLABS1[s]
                    for c in range(2):
                        dve.wait_ge(acc_free[j], chunk_no(SEG[seg], i, c) + 1)
                    if s >= 2:
                        dve.wait_ge(sem("silu_done"), s - 1)
                    w = param("dn_w").rearrange("p (t i) -> p t i", i=DTAPS)[:, DN[s][2], :]
                    b, dst = s % 2, cvo[:, s % 2, :]
                    own.link(dve.tensor_scalar(dst, pre[:, b, 0:SEQ], w[:, 0:1], None, ALU.mult))
                    for k in range(1, DTAPS):
                        ins = dve.scalar_tensor_tensor(dst, pre[:, b, k:k + SEQ], w[:, k:k + 1], dst, ALU.mult, ALU.add)
                        if k < DTAPS - 1:
                            own.link(ins)
                    ins.then_inc(sem("conv_done"), 1)
                if s - 2 in KQ:
                    kind = DN[s - 2][0]
                    for c in range(2):
                        b, turn = EVENT[f"dn{s - 2}_{c}"]
                        dve.wait_ge(aux_free[b], turn + 1)
                    own.link(dve.reciprocal(drs[:, :], drs[:, :]))
                    dst = dn_dst(s - 2)
                    dve.scalar_tensor_tensor(dst, dst, P ** -0.5 if kind == "q" else 1.0, drs[:, :],
                                             ALU.mult, ALU.mult).then_inc(sem("dscaled"), 1)
                for ct, k in taps[per * s:per * (s + 1)]:
                    src, w = cv_y[:, ct, k:k + SEQ], param("cv_w")[:, ct * TAPS + k:ct * TAPS + k + 1]
                    if k:
                        own.wait(1)
                        own.mark(dve.scalar_tensor_tensor(cv_acc[:, ct, :], src, w, cv_acc[:, ct, :], ALU.mult, ALU.add))
                    else:
                        own.mark(dve.tensor_scalar(cv_acc[:, ct, :], src, w, param("cv_b")[:, ct:ct + 1], ALU.mult, ALU.add))
                own.wait()
            dve.sem_inc(sem("cv_mean_in"), 1)
            for c in range(2):
                aux_wait(dve, f"cv_mean{c}")
                for ct in range(2):
                    dst = cv_acc[:, ct, cc(c)]
                    ins = dve.tensor_tensor(dst, dst, aux(f"cv_mean{c}"), ALU.subtract)
                    if ct == 0:
                        own.mark(ins)
                aux_release(ins, f"cv_mean{c}")
                own.wait()
                dve.wait_ge(aux_free[EVENT[f"cv_mean{c}"][0]], EVENT[f"cv_mean{c}"][1] + 1)
                dve.sem_inc(sem("cv_centred"), 2)
            for c in range(2):
                dve.wait_ge(aux_free[EVENT[f"cv_var{c}"][0]], EVENT[f"cv_var{c}"][1] + 1)
            own.link(dve.reciprocal(drs[:, :], drs[:, :]))
            dve.wait_ge(sem("cv_var_in"), 2)
            own.link(dve.tensor_tensor(cv_acc[:, :, :], cv_acc[:, :, :], drs[:, :].unsqueeze(1).broadcast_to([P, 2, SEQ]), ALU.mult))
            dve.sem_inc(sem("cv_normed"), 1)
            for k in range(2, 4):
                dve.wait_ge(sem("mix_hi"), k + 1)
                own.mark(dve.tensor_tensor(h_lo[:, k, META:L], cv_acc[:, k - 2, :], h_hi[:, k, META:L].bitcast(F32), ALU.subtract))
            own.wait()
            dve.wait_ge(sem("o_lo"), 2)
            own.link(dve.tensor_single_scalar(e_col, e_col, -1.0, ALU.mult))
            own.mark(dve.memset(state[:, 0, :, :], 0.0))
            own.wait()
            dve.sem_inc(sem("state_full"), 1)
            heads = [P, HEADS, P]

            def bank(b):
                return acc[:, b, :].rearrange("p (h i) -> p h i", h=HEADS)

            def mask(name):
                return const(name).unsqueeze(1).broadcast_to(heads)

            def state_step(n, q):
                cur = n % 2
                if q == 0:
                    dve.wait_ge(sem("ks_full"), n + 1)
                    for hd in range(HEADS):
                        ins = dve.scalar_tensor_tensor(r_u[:, hd, :], acc[:, S_A, hd * P:hd * P + P],
                                                       e_col[:, 4 * n + hd:4 * n + hd + 1], vtok[:, n, hd, :], ALU.mult, ALU.add)
                    ins.then_inc(sem("r_full"), 1)
                elif q == 1:
                    dve.wait_ge(sem("xr_full"), n + 1)
                    if n:
                        dve.wait_ge(sem("o_full"), n)
                    dve.tensor_tensor(u_sc[:, :, :], bank(S_A), beta[:, 4 * n:4 * n + 4].unsqueeze(2).broadcast_to(heads), ALU.mult)\
                       .then_inc(sem("u_full"), 1)
                else:
                    dve.wait_ge(sem("ds_full"), n + 1)
                    for hd in range(HEADS):
                        own.mark(dve.scalar_tensor_tensor(state[:, 1 - cur, hd, :], state[:, cur, hd, :],
                                                          c_dec[:, 4 * n + hd:4 * n + hd + 1],
                                                          acc[:, S_A, hd * P:hd * P + P], ALU.mult, ALU.add))
                    own.wait()
                    dve.sem_inc(sem("state_full"), 1)

            for it in range(NBLK // 2):
                for v in range(2):
                    n = 2 * it + v
                    if it:
                        dve.wait_ge(sem(f"xy_full{v}"), 6 * it)
                    dve.tensor_copy(la_b[v][:, :, :], decay[:, 4 * n:4 * n + 4].unsqueeze(2).broadcast_to(heads))\
                       .then_inc(sem("la_full"), 1)
                for v in range(2):
                    n = 2 * it + v
                    dve.wait_ge(sem(f"g_full{v}"), it + 1)
                    for hd in range(HEADS):
                        ins = dve.scalar_tensor_tensor(dec[v][:, hd, :], const("negmask"), g_col[:, 4 * n + hd:4 * n + hd + 1],
                                                       acc[:, 3 * v, hd * P:hd * P + P], ALU.subtract, ALU.add)
                    ins.then_inc(sem(f"dd_full{v}"), 1)
                for v in range(2):
                    n = 2 * it + v
                    dve.wait_ge(sem(f"dt_full{v}"), it + 1)
                    own.link(dve.tensor_tensor(b_t[v][:, :, :], bank(3 * v + 1), dec[v][:, :, :], ALU.mult))
                    for hd in range(HEADS):
                        own.mark(dve.scalar_tensor_tensor(b_t[v][:, hd, :], b_t[v][:, hd, :], beta[:, 4 * n + hd:4 * n + hd + 1],
                                                          const("strict"), ALU.mult, ALU.mult))
                    own.wait()
                    own.link(dve.tensor_tensor(off_t[v][:, :, :], b_t[v][:, :, :], mask("off1"), ALU.mult))
                    dve.sem_inc(sem(f"off_full{v}"), 1)
                    own.mark(dve.tensor_tensor(y_all[:, n, :, :], mask("ident"), off_t[v][:, :, :], ALU.subtract))
                for v in range(2):
                    n = 2 * it + v
                    own.mark(dve.tensor_tensor(a_all[:, n, :, :], bank(3 * v + 2), dec[v][:, :, :], ALU.mult))
                    own.mark(dve.tensor_tensor(qT[:, :, blk(n)], qT[:, :, blk(n)], e_row[v][:, :, :], ALU.mult))
                for lv in range(7):
                    for v in range(2):
                        n = 2 * it + v
                        dve.wait_ge(sem(f"g1_full{v}"), 7 * it + lv + 1)
                        if lv < 6:
                            own.wait()
                            dve.tensor_tensor(off_t[v][:, :, :], b_t[v][:, :, :], mask(f"off{2 << lv}"), ALU.mult)\
                               .then_inc(sem(f"off_full{v}"), 1)
                        if lv == 0:
                            own.link(dve.tensor_tensor(x_inv[v][:, :, :], mask("ident"), bank(3 * v), ALU.subtract))
                        else:
                            dve.wait_ge(sem(f"xy_full{v}"), 6 * it + lv)
                            if lv < 6:
                                own.mark(dve.tensor_tensor(x_inv[v][:, :, :], x_inv[v][:, :, :], bank(3 * v + 1), ALU.subtract))
                            own.link(dve.tensor_tensor(y_all[:, n, :, :], y_all[:, n, :, :], bank(3 * v + 2), ALU.subtract))
                        dve.sem_inc(sem(f"xy_done{v}"), 1)
                    for n, q in state_steps(it, lv):
                        state_step(n, q)
            for n, q in LAST_STEPS:
                state_step(n, q)
            for hd in range(HEADS + 1):
                if hd < HEADS:
                    b, turn = EVENT[f"on{hd}"]
                    dve.wait_ge(aux_free[b], turn + 1)
                    r = o_sd[:, 8 * hd:8 * hd + 8]
                    own.link(dve.reciprocal(r, r))
                    dve.tensor_tensor(odiag[hd % 2][:, :, :], ident.unsqueeze(1).broadcast_to([P, NBLK, P]),
                                      r.unsqueeze(2).broadcast_to([P, NBLK, P]), ALU.mult).then_inc(sem("odiag_full"), 1)
                if hd:
                    dve.wait_ge(sem("orms_full"), hd)
                    if hd >= 3:
                        dve.wait_ge(sem("o_lo"), hd)
                    dst, b = oy[:, (hd - 1) % 2, :], 2 * ((hd - 1) % 2)
                    dve.scalar_tensor_tensor(dst, qT[:, hd - 1, :], param("dn_norm")[:, 0:1],
                                             acc[:, b:b + 2, :].rearrange("p b n -> p (b n)"), ALU.mult, ALU.mult)\
                       .then_inc(sem("o_scaled"), 1)
            dve.sem_inc(sem("mixed1"), 1)
            own.link(dve.memset(ssq[:, :], 0.0))
            dve.wait_ge(sem("residual_full"), 32)
            dve_residual(dve, own, SEG["out1"], 1.0, True)
            own.wait()
            dve.sem_inc(sem("ssq_ffn0"), 1)

        INV_2PI, ROUND = 1.0 / (2.0 * math.pi), 12582912.0
        PI_A, PI_B = 6.28125, 0.0019350051879882812
        PI_C = 2.0 * math.pi - PI_A - PI_B
        PI_MAX = 3.1415925
        ROWS = dict(step=16, real=17, mag=18, angle=19, turns=20, rest=21, rest_c=22, sin=23, cos=24,
                    l_re=26, l_im=27, c_re=28, c_im=29, den=30, part=31)
        u2s = u2[:, :, :].rearrange("p t (m s) -> p t s m", s=SC)

        def row(name):
            return small[:, ROWS[name], :]

        def power(t, r):
            return small[:, 2 * (t - 1) + r, :]

        step8 = small[:, 16:20, :].rearrange("p (a b) s -> p a b s", a=2)

        UNITS = [(bi, hp) for bi in range(NBLK + 1) for hp in range(8)]

        def unit(u):
            bi, hp = UNITS[u]
            if bi == 0:
                return hp, slice(0, META), META, META, const("band0")[0:META, META:2 * META]
            n = bi - 1
            cols = slice(META + n * P, META + (n + 1) * P)
            return (hp, cols, P, META + P, const("band0")) if n == 0 else (hp, cols, P, META + 2 * P, const("band"))

        def at_bank(u):
            return 2 * ((u + 1) % 2)

        def at_chunk(f):
            return SEG["at_h"], f // 6, f // 3 % 2, f % 3

        GATE_CHUNKS = 6 * (8 - GATES_A)

        def gates_of(u):
            total, n = GATE_CHUNKS * KD, len(UNITS)
            return [divmod(g, KD) for g in range(total * u // n, total * (u + 1) // n)] if u < n else []

        def pe_mix2(pe):
            h = (h_hi, h_lo)
            pe_first_pair(pe, "mix2", SEG["at_u"])
            for j in range(2):
                pe_slab(pe, SEG["at_u"], 1, j, h)
            for j in range(2):
                pe.wait_ge(acc_free[j], SEG["at_u"].q0 + 6)
            pe.wait_ge(sem("ssm_c_full"), 1)
            for d in range(SC):
                pe.wait_ge(sem("bl_full"), d + 1)
                if d >= 2:
                    pe.wait_ge(sem("et_copied"), d - 1)
                b0 = 3 * (d % 2)
                for ct in range(4):
                    for r in range(2):
                        pe.transpose(acc[:, b0 + r, ct * P:ct * P + P],
                                     bl[d % 2][r][:, 4 * ct:4 * ct + 4, :].rearrange("p a b -> p (a b)"), ident)
                for p in range(PAIRS):
                    r0, out = 32 * (p % 4), acc[32 * (p % 4):32 * (p % 4) + 32, b0 + 2, 32 * (p // 4):32 * (p // 4) + 32]
                    pe.matmul(out, bl[d % 2][0][:, p, :], ssm_in[:, 2, p, :], start=True, stop=False, skip_group_check=True)
                    ins = pe.matmul(out, bl[d % 2][1][:, p, :], ssm_in[:, 3, p, :], start=False, stop=True, skip_group_check=True)
                ins.then_inc(sem("et_full"), 1)
            pe.wait_ge(sem("et_copied"), SC)
            for p in range(PAIRS):
                if p >= 2:
                    pe.wait_ge(sem("end_copied"), p - 1)
                r0, ct = 32 * (p % 4), p // 4
                for r in range(2):
                    for s in range(SC):
                        ins = pe.matmul(acc[:, 6 + p % 2, r * NCH:(r + 1) * NCH], et[r0:r0 + 32, ct, SC - 1 - s, r, :],
                                        u2s[r0:r0 + 32, ct, s, :], start=(s == 0), stop=(s == SC - 1))
                ins.then_inc(sem("end_full"), 1)
            pe.wait_ge(sem("end_copied"), PAIRS)
            with pe.Fori(0, 4) as i:
                for j in range(2):
                    pe_slab(pe, SEG["at_q"], i, j, h)
            with pe.Fori(0, GATES_A) as i:
                for j in range(2):
                    pe_slab(pe, SEG["at_g"], i, j, h)
            for j in range(2):
                pe.wait_ge(acc_free[j], SEG["at_g"].q0 + 3 * GATES_A)
            pe.wait_ge(sem("states_full"), 1)
            for n, s in enumerate(reversed(range(SC))):
                pe.wait_ge(sem("gl_full"), n + 1)
                for ct in range(4):
                    bank = 2 * (n % 4) + ct // 2
                    if n >= 4:
                        pe.wait_ge(sem("y_out"), 4 * (n - 4) + 4)
                    cols = slice((ct % 2) * NCH, (ct % 2 + 1) * NCH)
                    for d in range(s + 1):
                        pe.matmul(acc[:, bank, cols], hbd[:, ct, d, :], u2s[:, ct, s - d, :],
                                  start=(d == 0), stop=False, skip_group_check=True)
                    for pp in range(4):
                        p = 4 * ct + pp
                        out = acc[32 * pp:32 * pp + 32, bank, cols]
                        for r in range(2):
                            ins = pe.matmul(out, bl[n % 2][r][:, p, :], xs[:, 0:NCH, r, p],
                                            start=False, stop=(r == 1), skip_group_check=True)
                ins.then_inc(sem("y_full"), 1)
            pe.wait_ge(sem("y_out"), 4 * SC)
            for i in range(2):
                for j in range(2):
                    pe_slab(pe, SEG["at_kv"], i, j, h)
            for j in range(2):
                pe.wait_ge(acc_free[j], SEG["at_kv"].q0 + 6)
            for e in range(4):
                aux_take(pe, f"v2_{e}")
                for nn in range(2):
                    for ct in range(2):
                        c0 = META + (2 * e + nn) * P
                        ins = pe.transpose(aux(f"v2_{e}")[:, nn * 256 + ct * P:nn * 256 + ct * P + P], v2[:, ct, c0:c0 + P], ident)
                aux_done(ins, f"v2_{e}")
            aux_take(pe, "v2_m")
            for ct in range(2):
                ins = pe.transpose(aux("v2_m")[0:META, ct * P:ct * P + P], v2[:, ct, 0:META], ident)
            aux_done(ins, "v2_m")
            for b in range(2):
                name = "v2_m" if EVENT["v2_m"][0] == b else "v2_3"
                pe.wait_ge(aux_free[b], EVENT[name][1] + 1)
            pe.wait_ge(sem("ks_swapped"), 32)

            def gate_piece(piece):
                f, k = piece
                seg, i, j, c = at_chunk(f)
                c0, w = CH2[c]
                if k == 0:
                    pe.wait_ge(split_done, i * 2 + (seg.n0 + j + 1))
                    if f >= 2:
                        _, i_, j_, c_ = at_chunk(f - 2)
                        pe.wait_ge(acc_free[j_], chunk_no(seg, i_, c_) + 1)
                bank = acc[:, 6 + f % 2, 0:w]
                wh, wl = w_hi[:, j, k * P:(k + 1) * P], w_lo[:, j, k * P:(k + 1) * P]
                rh, rl = h_hi[:, k, c0:c0 + w], h_lo[:, k, c0:c0 + w]
                pe.matmul(bank, wh, rh, start=(k == 0), stop=False, skip_group_check=True)
                pe.matmul(bank, wh, rl, start=False, stop=False, skip_group_check=True)
                ins = pe.matmul(bank, wl, rh, start=False, stop=(k == KD - 1), skip_group_check=True)
                if k == KD - 1:
                    ins.then_inc(acc_full[j], 1)

            def scores(u):
                hp, cols, nq, kw, _ = unit(u)
                kv = hp // 2
                if u >= 2:
                    pe.wait_ge(sem("at_masked"), u - 1)
                if u >= 3:
                    pe.wait_ge(sem("at_oc"), u - 2)
                for hd in range(2):
                    r = slice(64 * hd, 64 * hd + 64)
                    keys = (k2 if (kv % 2) == hd else ks2)[r, kv // 2, :]
                    b = 2 * (u % 2) + hd
                    if kw <= META + P:
                        ins = pe.matmul(acc[0:nq, b, 0:kw], q2[r, hp, cols], keys[:, 0:kw], start=True, stop=True)
                    else:
                        pe.matmul(acc[0:nq, b, 0:META], q2[r, hp, cols], keys[:, 0:META], start=True, stop=True)
                        ins = pe.matmul(acc[0:nq, b, META:kw], q2[r, hp, cols], keys[:, cols.start - P:cols.stop], start=True, stop=True)
                ins.then_inc(sem("at_s"), 1)

            def turn(u):
                hp, cols, nq, kw, _ = unit(u)
                pe.wait_ge(sem("at_p"), u + 1)
                if u:
                    pe.wait_ge(sem("at_ptc"), u)
                for hd in range(2):
                    pr = sc[0:nq, u % 2, hd, :]
                    ins = pe.transpose(acc[0:META, 4 + hd, 0:nq], pr[:, 0:META], ident[0:nq, 0:nq])
                    for k in range((kw - META) // P):
                        a = 384 - (kw - META) + k * P
                        ins = pe.transpose(acc[:, 4 + hd, a:a + nq], pr[:, META + k * P:META + (k + 1) * P], ident[0:nq, 0:nq])
                ins.then_inc(sem("at_pt"), 1)

            def values(u):
                hp, cols, nq, kw, _ = unit(u)
                vc = slice(64 * (hp // 2), 64 * (hp // 2) + 64)
                pe.wait_ge(sem("at_ptc"), u + 1)
                if u + 1 < len(UNITS):
                    pe.wait_ge(sem("at_masked"), u + 2)
                else:
                    pe.wait_ge(sem("at_oc"), u - 1)
                nk = (kw - META) // P
                for hd in range(2):
                    out = acc[64 * hd:64 * hd + 64, at_bank(u), 384:384 + nq]
                    ins = pe.matmul(out, vm2[0:META, vc], pt[0:META, u % 2, hd, 0:nq], start=True, stop=(nk == 0), skip_group_check=True)
                    for k in range(nk):
                        n = UNITS[u][0] - nk + k
                        a = 384 - nk * P + k * P
                        ins = pe.matmul(out, vt2[:, n, vc], pt[:, u % 2, hd, a:a + P], start=False, stop=(k == nk - 1), skip_group_check=True)
                ins.then_inc(sem("at_o"), 1)

            for u in range(len(UNITS) + 2):
                for piece in gates_of(u):
                    gate_piece(piece)
                if u >= 2:
                    values(u - 2)
                if u < len(UNITS):
                    scores(u)
                if 1 <= u <= len(UNITS):
                    turn(u - 1)
            pe.wait_ge(sem("at_oc"), len(UNITS))
            pe.wait_ge(sem("at_masked"), len(UNITS))
            pe.wait_ge(sem("y_split"), 4)
            with pe.Fori(0, 8) as i:
                for j in range(2):
                    pe_slab(pe, SEG["glu"], i, j, (y_hi, y_lo))
            pe.wait_ge(sem("glu_done"), 9)
            with pe.Fori(0, SEG["out2"].pairs) as i:
                for j in range(2):
                    pe_slab(pe, SEG["out2"], i, j, h)

        def act_mix2(act):
            own = Chain(act, sem("act_own2"))
            act.dma_start(t["x_kept"], x[:, :, :]).then_inc(sem("x_stored"), 16)
            h_ready(act, "mix2", 2)
            act.dma_start(ssm_in[:, :, :, :], t["ssm"].rearrange("p (a b c) -> p a b c", a=4, b=PAIRS)).then_inc(sem("ssm_full"), 16)
            act.activation(row("step"), param("log_step"), ACT.Exp).then_inc(sem("ssm_step"), 1)
            act.wait_ge(sem("ssm_angle"), 1)
            own.mark(act.activation(row("mag"), row("real"), ACT.Exp))
            act.wait_ge(sem("ssm_rest"), 1)
            own.mark(act.activation(row("sin"), row("rest"), ACT.Sin))
            own.link(act.activation(row("cos"), row("rest_c"), ACT.Sin))
            act.sem_inc(sem("ssm_trig"), 1)
            act.wait_ge(sem("x_stored"), 16)
            def evacuate(seg, i, j, dst, func=ACT.Copy):
                for c, (c0, w) in enumerate(CH2):
                    acc_wait(act, SEG[seg], i, j, c)
                    act.activation(dst[:, c0:c0 + w], acc[:, 3 * j + c, 0:w], func).then_inc(acc_free[j], 1)

            for s in range(4):
                evacuate("at_u", s // 2, s % 2, u2[:, s, :])
            act.wait_ge(sem("hbd_zero"), 1)
            for d in range(SC):
                act.wait_ge(sem("et_full"), d + 1)
                b0 = 3 * (d % 2)
                for r in range(2):
                    own.mark(act.copy(et[:, :, d, r, :], acc[:, b0 + r, :].rearrange("p (t s) -> p t s", t=4)))
                for pp in range(4):
                    rows = slice(32 * pp, 32 * pp + 32)
                    ins = act.copy(hbd[rows, :, d, rows], acc[rows, b0 + 2, 0:P].rearrange("p (t c) -> p t c", t=4))
                ins.then_inc(sem("et_copied"), 1)
            for p in range(PAIRS):
                act.wait_ge(sem("end_full"), p + 1)
                if p == 0:
                    act.wait_ge(sem("xs_zero"), 1)
                act.copy(xs[:, 1:NCH, :, p], acc[:, 6 + p % 2, 0:2 * NCH].rearrange("p (r m) -> p m r", r=2)[:, 0:NCH - 1, :])\
                   .then_inc(sem("end_copied"), 1)
            for s in range(8):
                evacuate("at_q", s // 2, s % 2, q2[:, s, :])
            for s in range(2):
                act.sem_inc(sem(f"gate_stored{s}"), 16)

            def gate_chunk(seg, i, j, c, first, s, bank):
                c0, w = CH2[c]
                act.wait_ge(sem(f"gate_stored{s}"), i * 48 + (first * 16 + 16))
                acc_wait(act, seg, i, j, c)
                act.copy(gstage[:, s, 0:w], acc[:, bank, 0:w]).then_inc(acc_free[j], 1)
                act.wait_ge(acc_free[j], chunk_no(seg, i, c) + 1)
                slab = i * 2 + (j if seg is SEG["at_g"] else j + 2 * GATES_A)
                act.dma_start(t["gates_kept"][bass.ds(slab, 1), :, c0:c0 + w].rearrange("a p n -> p a n"),
                              gstage[:, s:s + 1, 0:w]).then_inc(sem(f"gate_stored{s}"), 16)

            with act.Fori(0, GATES_A) as i:
                for j in range(2):
                    for c in range(3):
                        gate_chunk(SEG["at_g"], i, j, c, (3 * j + c) // 2, (3 * j + c) % 2, 3 * j + c)
            for ct in range(4):
                act.wait_ge(sem("y_out"), 4 * SC)
                act.activation(u2[:, ct, :], u2[:, ct, :], ACT.Gelu_apprx_tanh).then_inc(sem("y_gelu"), 1)
            for s in range(4):
                evacuate("at_kv", s // 2, s % 2, k2[:, s, :] if s < 2 else v2[:, s - 2, :])
                if s == 1:
                    for j in range(2):
                        act.wait_ge(acc_free[j], chunk_no(SEG["at_kv"], 0, 2) + 1)
                    for lo, hi in ((0, 64), (64, 0)):
                        act.dma_start(ks2[lo:lo + 64, :, :], k2[hi:hi + 64, :, :]).then_inc(sem("ks_swapped"), 16)
            for e in range(4):
                aux_wait(act, f"v2_{e}")
                aux_release(act.copy(vt2[:, 2 * e:2 * e + 2, :], aux(f"v2_{e}").rearrange("p (n c) -> p n c", n=2)), f"v2_{e}")
            aux_wait(act, "v2_m")
            aux_release(act.copy(vm2[0:META, :], aux("v2_m")[0:META, 0:256]), "v2_m")

            def exps(u):
                hp, cols, nq, kw, _ = unit(u)
                b = u % 2
                act.wait_ge(sem("at_max"), u + 1)
                for hd in range(2):
                    own.mark(act.activation(sc[0:nq, b, hd, 0:kw], sc[0:nq, b, hd, 0:kw], ACT.Exp,
                                            bias=st[0:nq, b, 0, hd:hd + 1], accum_out=st[0:nq, b, 1, hd:hd + 1]))
                act.activation(st[0:nq, b, 2, :], st[0:nq, b, 4, :], ACT.Exp).then_inc(sem("at_exp"), 1)

            def copies(u):
                hp, cols, nq, kw, _ = unit(u)
                b = u % 2
                act.wait_ge(sem("at_pt"), u + 1)
                if u >= 2:
                    act.wait_ge(sem("at_o"), u - 1)
                ins = act.copy(pt[0:META, b, :, 0:nq], acc[0:META, 4:6, 0:nq])
                if kw > META:
                    own.mark(ins)
                    a = 384 - (kw - META)
                    ins = act.copy(pt[:, b, :, a:384], acc[:, 4:6, a:384])
                ins.then_inc(sem("at_ptc"), 1)

            for u in range(len(UNITS) + 1):
                for f, k in gates_of(u):
                    if k == KD - 1:
                        seg, i, j, c = at_chunk(f)
                        gate_chunk(seg, i, j, c, 3 * GATES_A + (3 * j + c) // 2, f % 2, 6 + f % 2)
                if u:
                    copies(u - 1)
                if u < len(UNITS):
                    exps(u)
            act.wait_ge(sem("at_oc"), len(UNITS))
            for ct in range(4):
                act.copy(y_hi[:, ct, :], u2[:, ct, :]).then_inc(sem("y_hi_full"), 1)
            for s in range(2):
                act.wait_ge(sem(f"gate_stored{s}"), 16 * (24 + 1))

            def load_gates(m, b):
                for r in range(2):
                    act.dma_start(gld[:, b, r:r + 1, :], t["gates_kept"][bass.ds(m + 8 * r, 1)].rearrange("a p n -> p a n"))\
                       .then_inc(sem(f"gates_full{b}"), 16)

            def glu(m, turn_, again, b):
                act.wait_ge(sem(f"gates_full{b}"), (turn_ + 1) * 32)
                act.activation(gld[:, b, :, :], gld[:, b, :, :], ACT.Sigmoid).then_inc(sem("gates_on"), 1)
                for c, (c0, w) in enumerate(CH2):
                    acc_wait(act, SEG["glu"], m, 0, c)
                    act.wait_ge(sem("glu_done"), m + 1)
                    act.activation(gtmp[:, c, 0:w], acc[:, c, 0:w], ACT.Sigmoid).then_inc(acc_free[0], 1)
                if again:
                    load_gates(m + 1, 1 - b)

            load_gates(0, 0)
            with act.Fori(0, 3) as ii:
                for b in range(2):
                    glu(ii * 2 + b, ii, True, b)
            for b in range(2):
                glu(6 + b, 3, b == 0, b)
            act.wait_ge(sem("glu_done"), 9)
            act.dma_start(x[:, :, :], t["x_kept"]).then_inc(sem("x_again"), 16)

        def dve_mix2(dve, own):
            def tt(dst, a, b, op):
                own.link(dve.tensor_tensor(dst, a, b, op))

            def ts(dst, a, s1, s2, op0, op1):
                own.link(dve.tensor_scalar(dst, a, s1, s2, op0, op1))

            def stt(dst, a, s, b, op0, op1):
                own.link(dve.scalar_tensor_tensor(dst, a, s, b, op0, op1))

            R, a_re, a_im = row, param("a_re"), param("a_im")
            dve.wait_ge(sem("ssm_step"), 1)
            tt(R("real"), a_re, R("step"), ALU.mult)
            tt(R("angle"), a_im, R("step"), ALU.mult)
            dve.sem_inc(sem("ssm_angle"), 1)
            ts(R("turns"), R("angle"), INV_2PI, ROUND, ALU.mult, ALU.add)
            ts(R("turns"), R("turns"), ROUND, None, ALU.subtract, ALU.bypass)
            stt(R("rest"), R("turns"), -PI_A, R("angle"), ALU.mult, ALU.add)
            stt(R("rest"), R("turns"), -PI_B, R("rest"), ALU.mult, ALU.add)
            stt(R("rest"), R("turns"), -PI_C, R("rest"), ALU.mult, ALU.add)
            ts(R("rest"), R("rest"), PI_MAX, -PI_MAX, ALU.min, ALU.max)
            stt(R("rest_c"), R("rest"), -1.0, R("rest"), ALU.mult, ALU.max)
            ts(R("rest_c"), R("rest_c"), -1.0, math.pi / 2, ALU.mult, ALU.add)
            dve.sem_inc(sem("ssm_rest"), 1)
            tt(R("den"), a_re, a_re, ALU.mult)
            tt(R("part"), a_im, a_im, ALU.mult)
            tt(R("den"), R("den"), R("part"), ALU.add)
            own.link(dve.reciprocal(R("den"), R("den")))
            dve.wait_ge(sem("ssm_trig"), 1)
            tt(R("l_re"), R("mag"), R("cos"), ALU.mult)
            tt(R("l_im"), R("mag"), R("sin"), ALU.mult)
            ts(R("rest"), R("l_re"), 1.0, None, ALU.subtract, ALU.bypass)
            for dst, first, second_, op in (("c_re", a_re, a_im, ALU.add), ("c_im", None, None, ALU.subtract)):
                if first is not None:
                    tt(R(dst), R("rest"), a_re, ALU.mult)
                    tt(R("part"), R("l_im"), a_im, ALU.mult)
                else:
                    tt(R(dst), R("l_im"), a_re, ALU.mult)
                    tt(R("part"), R("rest"), a_im, ALU.mult)
                tt(R(dst), R(dst), R("part"), op)
                tt(R(dst), R(dst), R("den"), ALU.mult)

            def cmul(dst, a, b, p):
                tt(p[0], a[0], b[0], ALU.mult)
                tt(p[1], a[1], b[1], ALU.mult)
                tt(dst[0], p[0], p[1], ALU.subtract)
                tt(p[0], a[0], b[1], ALU.mult)
                tt(p[1], a[1], b[0], ALU.mult)
                tt(dst[1], p[0], p[1], ALU.add)

            lam, parts2 = (R("l_re"), R("l_im")), (R("den"), R("part"))
            for r in range(2):
                own.link(dve.tensor_copy(power(1, r), lam[r]))
            for k in range(2, SC + 1):
                cmul([power(k, r) for r in range(2)], [power(k - 1, r) for r in range(2)], lam, parts2)
            for a in range(2):
                own.link(dve.tensor_copy(step8[:, 0, a, :], power(SC, 0)))
            own.link(dve.tensor_copy(step8[:, 1, 0, :], power(SC, 1)))
            ts(step8[:, 1, 1, :], power(SC, 1), -1.0, None, ALU.mult, ALU.bypass)

            def wide(r):
                return r.unsqueeze(2).broadcast_to([P, PAIRS, 32])

            dve.wait_ge(sem("x_stored"), 16)
            own.mark(dve.memset(hbd[:, :, :, :], 0.0))
            own.wait()
            dve.sem_inc(sem("hbd_zero"), 1)
            dve.wait_ge(sem("ssm_full"), 16)
            ts(ssm_in[:, 3, :, :], ssm_in[:, 3, :, :], -1.0, None, ALU.mult, ALU.bypass)
            dve.sem_inc(sem("ssm_c_full"), 1)
            pw = [p[:, :, :] for p in prod]
            b_in = [ssm_in[:, r, :, :] for r in range(2)]
            cmul([bl[0][r][:, :, :] for r in range(2)], b_in, [wide(R("c_re")), wide(R("c_im"))], pw)
            dve.sem_inc(sem("bl_full"), 1)
            for d in range(1, SC):
                if d >= 2:
                    dve.wait_ge(sem("et_full"), d - 1)
                cmul([bl[d % 2][r][:, :, :] for r in range(2)], [bl[(d - 1) % 2][r][:, :, :] for r in range(2)],
                     [wide(R("l_re")), wide(R("l_im"))], pw)
                dve.sem_inc(sem("bl_full"), 1)
            own.link(dve.memset(xs[:, 0:1, :, :], 0.0))
            dve.sem_inc(sem("xs_zero"), 1)
            dve.wait_ge(sem("end_copied"), PAIRS)
            per = 4
            with own.loop((NCH - 2) // per, 4 * per) as i:
                for k in range(per):
                    last = xs[:, bass.ds(i * per + (k + 1), 1), :, :]
                    now = xs[:, bass.ds(i * per + (k + 2), 1), :, :]
                    own.link(dve.tensor_tensor(quad[:, :, :, :], last.broadcast_to([P, 2, 2, PAIRS]), step8, ALU.mult))
                    own.link(dve.tensor_tensor(now, now, quad[:, 0:1, :, :], ALU.add))
                    for r in range(2):
                        ins = dve.tensor_tensor(now[:, :, r, :], now[:, :, r, :], quad[:, 1:2, 1 - r, :], ALU.add)
                        own.mark(ins)
                    own.wait()
            dve.sem_inc(sem("states_full"), 1)

            def c_power(n):
                if n >= 2:
                    dve.wait_ge(sem("y_full"), n - 1)
                g, m, k = bl[n % 2], [wide(power(SC - n, r)) for r in range(2)], [ssm_in[:, 2 + r, :, :] for r in range(2)]
                tt(pw[0], k[0], m[0], ALU.mult)
                tt(pw[1], k[1], m[1], ALU.mult)
                tt(g[0][:, :, :], pw[0], pw[1], ALU.add)
                tt(pw[0], k[1], m[0], ALU.mult)
                tt(pw[1], k[0], m[1], ALU.mult)
                tt(g[1][:, :, :], pw[0], pw[1], ALU.subtract)
                dve.sem_inc(sem("gl_full"), 1)

            c_power(0)
            for n in range(SC):
                if n + 1 < SC:
                    c_power(n + 1)
                dve.wait_ge(sem("y_full"), n + 1)
                s = SC - 1 - n
                for ct in range(4):
                    dst = u2s[:, ct, s, :]
                    dve.scalar_tensor_tensor(dst, dst, param("ssm_d")[:, ct:ct + 1],
                                             acc[:, 2 * (n % 4) + ct // 2, (ct % 2) * NCH:(ct % 2 + 1) * NCH],
                                             ALU.mult, ALU.add).then_inc(sem("y_out"), 1)
            neg_sinks = small[:, 20, :]
            ts(neg_sinks, param("sinks"), -1.0, None, ALU.mult, ALU.bypass)

            def mask_max(u):
                hp, cols, nq, kw, mask_ = unit(u)
                b = u % 2
                dve.wait_ge(sem("at_s"), u + 1)
                if u >= 2:
                    dve.wait_ge(sem("at_pt"), u - 1)
                s_ = sc[0:nq, b, :, 0:kw]
                dve.scalar_tensor_tensor(s_, acc[0:nq, 2 * b:2 * b + 2, 0:kw], 0.125, mask_.unsqueeze(1).broadcast_to([nq, 2, kw]),
                                         ALU.mult, ALU.add).then_inc(sem("at_masked"), 1)
                dve.wait_ge(sem("at_masked"), u + 1)
                own.link(dve.tensor_reduce(st[0:nq, b, 0, :], s_, AX_X, ALU.max))
                stt(st[0:nq, b, 0, :], st[0:nq, b, 0, :], -1.0, neg_sinks[0:nq, 2 * hp:2 * hp + 2], ALU.mult, ALU.min)
                dve.tensor_tensor(st[0:nq, b, 4, :], param("sinks")[0:nq, 2 * hp:2 * hp + 2], st[0:nq, b, 0, :],
                                  ALU.add).then_inc(sem("at_max"), 1)

            def probabilities(u):
                hp, cols, nq, kw, _ = unit(u)
                b = u % 2
                dve.wait_ge(sem("at_exp"), u + 1)
                tt(st[0:nq, b, 1, :], st[0:nq, b, 1, :], st[0:nq, b, 2, :], ALU.add)
                own.link(dve.reciprocal(st[0:nq, b, 3, :], st[0:nq, b, 1, :]))
                for hd in range(2):
                    ins = dve.tensor_scalar(sc[0:nq, b, hd, 0:kw], sc[0:nq, b, hd, 0:kw], st[0:nq, b, 3, hd:hd + 1], None, ALU.mult)
                    if hd == 0:
                        own.mark(ins)
                ins.then_inc(sem("at_p"), 1)

            def outputs(u):
                hp, cols, nq, kw, _ = unit(u)
                dve.wait_ge(sem("at_o"), u + 1)
                dve.tensor_copy(q2[:, hp, cols], acc[:, at_bank(u), 384:384 + nq]).then_inc(sem("at_oc"), 1)

            for u in range(len(UNITS) + 2):
                if u < len(UNITS):
                    mask_max(u)
                if u >= 2:
                    outputs(u - 2)
                if u < len(UNITS):
                    probabilities(u)
            for ct in range(4):
                dve.wait_ge(sem("y_hi_full"), ct + 1)
                dve.tensor_tensor(y_lo[:, ct, :], u2[:, ct, :], y_hi[:, ct, :].bitcast(F32), ALU.subtract).then_inc(sem("y_split"), 1)
            dve.wait_ge(sem("at_oc"), len(UNITS))
            dve.sem_inc(sem("glu_done"), 1)
            with own.loop(4, 2 * 3 * 5) as ii:
                for b in range(2):
                    m = ii * 2 + b
                    dve.wait_ge(sem("gates_on"), m + 1)
                    for c, (c0, w) in enumerate(CH2):
                        acc_wait(dve, SEG["glu"], m, 1, c)
                        dve.wait_ge(acc_free[0], chunk_no(SEG["glu"], m, c) + 1)
                        g = gtmp[:, c:c + 1, 0:w]
                        at_, out = q2[:, bass.ds(m, 1), c0:c0 + w], h_hi[:, bass.ds(m, 1), c0:c0 + w]
                        own.mark(dve.tensor_tensor(at_, at_, gld[:, b, 0:1, c0:c0 + w], ALU.mult))
                        dve.tensor_tensor(g, g, acc[:, 3 + c:4 + c, 0:w], ALU.mult).then_inc(acc_free[1], 1)
                        dve.wait_ge(acc_free[1], chunk_no(SEG["glu"], m, c) + 1)
                        own.link(dve.tensor_tensor(g, g, gld[:, b, 1:2, c0:c0 + w], ALU.mult))
                        own.mark(dve.tensor_tensor(out, g, at_, ALU.add))
                        own.link(dve.tensor_tensor(at_, g, at_, ALU.add))
                        own.mark(dve.tensor_tensor(h_lo[:, bass.ds(m, 1), c0:c0 + w], at_, out.bitcast(F32), ALU.subtract))
                    own.wait()
                    dve.sem_inc(sem("glu_done"), 1)
            own.link(dve.memset(ssq[:, :], 0.0))
            dve.wait_ge(sem("x_again"), 16)
            dve_residual(dve, own, SEG["out2"], 1.0, True)
            own.wait()
            dve.sem_inc(sem("ssq_ffn2"), 1)

        REAL, ALL = slice(META, L), slice(0, L)
        second = next(p for p in ("ffn1", "mix2", "ffn2") if p in parts)

        @block.scalar
        def _(act):
            for k in range(0, KD, 2):
                act.dma_start(x[:, k:k + 2, REAL], t["x"][:, k:k + 2, :]).then_inc(sem(f"x_full{k // 2}"), 16)

            def loaded(k):
                act.wait_ge(sem(f"x_full{k // 2}"), 16)

            act.wait_ge(sem("params_full"), 32)
            if "mix1" in parts:
                act_squares(act, "mix1", REAL, loaded)
                act_norm(act, "mix1", CH1)
                act_mix1(act)
            if "ffn0" in parts:
                if "mix1" not in parts:
                    act_squares(act, "ffn0", REAL, loaded)
                act_norm(act, "ffn0", CH1)
                act_ffn(act, "ffn0", CH1)
                act_norm(act, "fin1", CH1, split=False)
            act.wait_ge(sem("x_ready"), 1)
            if "ffn0" in parts:
                act_squares(act, second, ALL, lambda k: act.wait_ge(sem("tile_fin1"), k + 1))
            else:
                act_squares(act, second, ALL, loaded)
            if "ffn1" in parts:
                act_norm(act, "ffn1", CH2)
                act_ffn(act, "ffn1", CH2)
            if "mix2" in parts:
                act_norm(act, "mix2", CH2)
                act_mix2(act)
            if "ffn2" in parts:
                act_norm(act, "ffn2", CH2)
                act_ffn(act, "ffn2", CH2)
                act_norm(act, "fin2", CH2, split=False)
                for k in range(0, KD, 2):
                    act.wait_ge(sem("tile_fin2"), k + 2)
                    act.dma_start(t["out"][:, k:k + 2, :], fin[:, k:k + 2, REAL]).then_inc(sem("out_stored"), 16)
                act.wait_ge(sem("out_stored"), 16 * (KD // 2))

        @block.vector
        def _(dve):
            own = Chain(dve, sem("dve_own"))
            dve.wait_ge(sem("params_full"), 32)
            if "mix1" in parts:
                dve_norm(dve, own, "mix1", CH1, param("mix_g"))
                dve_mix1(dve, own)
            if "ffn0" in parts:
                dve_norm(dve, own, "ffn0", CH1, param("ffn_g"))
                dve_ffn(dve, own, "ffn0", CH1, 1.0, "fin1")
                own.link(dve.tensor_copy(x[:, :, 0:META], param("meta").rearrange("p (k m) -> p k m", k=KD)))
                dve.sem_inc(sem("x_ready"), 1)
                dve_norm_whole(dve, own, "fin1", CH1, param("final_g"), x)
            else:
                own.link(dve.tensor_copy(x[:, :, 0:META], param("meta").rearrange("p (k m) -> p k m", k=KD)))
                dve.sem_inc(sem("x_ready"), 1)
            if "ffn1" in parts:
                dve_norm(dve, own, "ffn1", CH2, param("ffn1_g"))
                dve_ffn(dve, own, "ffn1", CH2, 0.5, "mix2" if "mix2" in parts else "ffn2")
            if "mix2" in parts:
                dve_norm(dve, own, "mix2", CH2, param("mix2_g"))
                dve_mix2(dve, own)
            if "ffn2" in parts:
                dve_norm(dve, own, "ffn2", CH2, param("ffn2_g"))
                dve_ffn(dve, own, "ffn2", CH2, 0.5, "fin2")
                dve_norm_whole(dve, own, "fin2", CH2, param("final2_g"), fin)

        @block.tensor
        def _(pe):
            pe.wait_ge(sem("params_full"), 32)
            if "mix1" in parts:
                pe_norm_of_squares(pe, "mix1", CH1)
                pe_mix1(pe)
            if "ffn0" in parts:
                (pe_norm if "mix1" in parts else pe_norm_of_squares)(pe, "ffn0", CH1)
                pe_ffn(pe, "ffn0", CH1)
                pe_norm(pe, "fin1", CH1)
            if "ffn1" in parts:
                (pe_norm_of_squares if second == "ffn1" else pe_norm)(pe, "ffn1", CH2)
                pe_ffn(pe, "ffn1", CH2)
            if "mix2" in parts:
                (pe_norm_of_squares if second == "mix2" else pe_norm)(pe, "mix2", CH2)
                pe_mix2(pe)
            if "ffn2" in parts:
                (pe_norm_of_squares if second == "ffn2" else pe_norm)(pe, "ffn2", CH2)
                pe_ffn(pe, "ffn2", CH2)
                pe_norm(pe, "fin2", CH2)


def laid_out(a):
    arrays = {"x": a["x"][0].T.reshape(KD, P, SEQ).transpose(1, 0, 2), "consts": CONSTANTS}
    arrays["params"], arrays["ssm"], arrays["gm"] = pack_params(a)
    arrays["w_in"] = slabs_of(a["w_in"][0][:, :3072])
    for name in ("w_out", "w_gate", "w_up", "ffn1_w1_2", "ffn1_w3_2", "w_in_2", "ssm_glu_a_2", "ssm_glu_b_2",
                 "w_out_2", "ffn2_w1_2", "ffn2_w3_2"):
        arrays[name] = slabs_of(a[name][0])
    for name in ("w_down", "ffn1_w2_2", "ffn2_w2_2"):
        f = 0
        for part, nf in enumerate(FQ):
            arrays[f"{name}/{part}"] = slabs_of(a[name][0][f * P:(f + nf) * P])
            f += nf
    return {k: np.ascontiguousarray(v) for k, v in arrays.items()}


def declare(nc, arrays):
    t = {}
    for name, a in arrays.items():
        ap = nc.dram_tensor("in_" + name.replace("/", "_") + "_dram", a.shape, F32, kind="ExternalInput").ap()
        if "/" in name:
            key = name.split("/")[0]
            t.setdefault(key, []).append(ap)
        else:
            t[name] = ap
    t["x_kept"] = nc.dram_tensor("x_kept", (P, KD, L), F32, kind="Internal").ap()
    t["gates_kept"] = nc.dram_tensor("gates_kept", (16, P, L), F32, kind="Internal").ap()
    t["out"] = nc.dram_tensor("out_dram", (P, KD, SEQ), F32, kind="ExternalOutput").ap()
    return t


def kernel(**inputs):
    import concourse.bacc as bacc
    from concourse.bass_utils import run_bass_kernel_spmd

    arrays = laid_out({k: np.asarray(v) for k, v in inputs.items()})
    nc = bacc.Bacc("TRN2", target_bir_lowering=False, num_devices=1)
    t = declare(nc, arrays)
    build_program(nc, t)
    feed = {"in_" + k.replace("/", "_") + "_dram": v for k, v in arrays.items()}
    got = run_bass_kernel_spmd(nc, [feed], core_ids=[0]).results[0]["out_dram"]
    return np.ascontiguousarray(got.transpose(1, 0, 2).reshape(D, SEQ).T)[None]
```
